# Optimizing a Trainium2 kernel written in Bass

```python
import math
import jax, jax.numpy as jnp
from jax import lax
import numpy as np

D_MODEL = 1024
BATCH = 1
SEQ = 256
DEPTH = 2

HEAD_DIM = 64
ROPE_DIM = 16
ROPE_THETA = 500000.0
GRID_W = 64
NA_HEADS = 8
NA_WIN_R = 8
NA_WIN_C = 16
NA_QCOL_BLOCK = 16
NA_KCOL_SPAN = 32
DIFF_HEADS = 4
DIFF_V_DIM = 128
DIFF_Q_BLOCK = 128
DIL_PATTERNS = ((128, 1), (512, 4), (2048, 16))
DIL_HEADS_PER_GROUP = 4
DIL_HEADS = 12
DIL_Q_BLOCK = 64
A_W = 512
B_QK_W = 512
B_V_W = 512
C_W = 768
C_OUT_W = 256
N_BRANCH = 3
IN_W = 3 * A_W + 2 * B_QK_W + B_V_W + 3 * C_W + N_BRANCH * D_MODEL
N_GROUPS = 4
EXPERTS_PER_GROUP = 4
N_EXPERTS = 16
TOP_K = 2
D_FF_EXPERT = D_MODEL // 2
NORM_EPS = 1e-6
SUBLN_EPS = 1e-5
NEG_INF = -1e30

kernel_name = 'hybrid_na_diff_dilated_hmoe_encoder'

def rmsnorm(x, g, eps=NORM_EPS):
    xf = x.astype(jnp.float32)
    y = xf * lax.rsqrt(jnp.mean(xf * xf, axis=-1, keepdims=True) + eps)
    return (y * g.astype(jnp.float32)).astype(x.dtype)

def rope_tables(T):
    inv = 1.0 / (ROPE_THETA ** (jnp.arange(0, ROPE_DIM, 2, dtype=jnp.float32) / ROPE_DIM))
    ang = jnp.arange(T, dtype=jnp.float32)[:, None] * inv[None, :]
    return jnp.cos(ang), jnp.sin(ang)

def partial_rope(x, cos, sin):
    half = ROPE_DIM // 2
    xr = x[..., :ROPE_DIM].astype(jnp.float32)
    x1, x2 = xr[..., :half], xr[..., half:]
    c = cos[None, :, None, :]
    s = sin[None, :, None, :]
    rot = jnp.concatenate([x1 * c - x2 * s, x2 * c + x1 * s], axis=-1).astype(x.dtype)
    return jnp.concatenate([rot, x[..., ROPE_DIM:]], axis=-1)

def neighbourhood_attention(q, k, v, rpb):
    B, T, H, dh = q.shape
    rows = T // GRID_W
    wr = min(NA_WIN_R, rows)
    ncb = GRID_W // NA_QCOL_BLOCK

    def grid(t):
        return t.reshape(B, rows, GRID_W, H, dh).transpose(0, 3, 1, 2, 4)

    qg, kg, vg = grid(q), grid(k), grid(v)
    qc = np.arange(GRID_W).reshape(ncb, NA_QCOL_BLOCK)
    cs = np.clip(np.arange(ncb) * NA_QCOL_BLOCK - NA_WIN_C // 2, 0, GRID_W - NA_KCOL_SPAN)
    kc = cs[:, None] + np.arange(NA_KCOL_SPAN)[None, :]
    c0 = np.clip(qc - NA_WIN_C // 2, 0, GRID_W - NA_WIN_C)
    col_ok = (kc[:, None, :] >= c0[:, :, None]) & (kc[:, None, :] < c0[:, :, None] + NA_WIN_C)
    dc_idx = np.clip(kc[:, None, :] - qc[:, :, None] + NA_WIN_C - 1, 0, 2 * NA_WIN_C - 2)
    rpb_c = rpb[:, :, dc_idx]
    col_mask = jnp.asarray(col_ok)[None, None, :, :, None, :]
    kc_j = jnp.asarray(kc)
    scale = dh ** -0.5

    def one_row(r):
        r0 = jnp.clip(r - wr // 2, 0, rows - wr)
        q_r = lax.dynamic_index_in_dim(qg, r, axis=2, keepdims=False)
        k_b = lax.dynamic_slice_in_dim(kg, r0, wr, axis=2)[:, :, :, kc_j]
        v_b = lax.dynamic_slice_in_dim(vg, r0, wr, axis=2)[:, :, :, kc_j]
        q_r = q_r.reshape(B, H, ncb, NA_QCOL_BLOCK, dh)
        s = jnp.einsum('bhcqd,bhrckd->bhcqrk', q_r, k_b,
                       preferred_element_type=jnp.float32) * scale
        dr = r0 + jnp.arange(wr) - r + NA_WIN_R - 1
        bias = jnp.take(rpb_c, dr, axis=1).transpose(0, 2, 3, 1, 4)
        s = jnp.where(col_mask, s + bias.astype(jnp.float32)[None], NEG_INF)
        p = jax.nn.softmax(s.reshape(B, H, ncb, NA_QCOL_BLOCK, wr * NA_KCOL_SPAN), axis=-1)
        p = p.reshape(s.shape).astype(v.dtype)
        o = jnp.einsum('bhcqrk,bhrckd->bhcqd', p, v_b)
        return o.reshape(B, H, GRID_W, dh)

    out = lax.map(one_row, jnp.arange(rows))
    return out.transpose(1, 0, 3, 2, 4).reshape(B, T, H * dh)

def differential_attention(q, k, v, lam, lam_init, subln_g):
    B, T, H, _, dh = q.shape
    nb = T // DIFF_Q_BLOCK
    scale = dh ** -0.5
    qb = q.reshape(B, nb, DIFF_Q_BLOCK, H, 2, dh).transpose(1, 0, 3, 4, 2, 5)
    kt = k.transpose(0, 2, 3, 1, 4)
    vt = v.transpose(0, 2, 1, 3)

    def one_block(q_blk):
        s = jnp.einsum('bhcqd,bhckd->bhcqk', q_blk, kt,
                       preferred_element_type=jnp.float32) * scale
        p = jax.nn.softmax(s, axis=-1)
        a = p[:, :, 0] - lam * p[:, :, 1]
        return jnp.einsum('bhqk,bhkd->bhqd', a.astype(v.dtype), vt)

    o = lax.map(one_block, qb)
    o = o.transpose(1, 0, 3, 2, 4).reshape(B, T, H, 2 * dh)
    o = rmsnorm(o, subln_g, SUBLN_EPS) * (1.0 - lam_init)
    return o.reshape(B, T, H * 2 * dh)

def dilated_group(q, k, v, dil, radius):
    B, T, H, dh = q.shape
    L = T // dil
    nb = -(-L // DIL_Q_BLOCK)
    Lp = nb * DIL_Q_BLOCK
    kb = DIL_Q_BLOCK + 2 * radius

    def phase(t):
        return t.reshape(B, L, dil, H, dh).transpose(0, 2, 3, 1, 4)

    qp = jnp.pad(phase(q), ((0, 0), (0, 0), (0, 0), (0, Lp - L), (0, 0)))
    pad_k = ((0, 0), (0, 0), (0, 0), (radius, Lp - L + radius), (0, 0))
    kp = jnp.pad(phase(k), pad_k)
    vp = jnp.pad(phase(v), pad_k)
    idx = np.arange(nb)[:, None] * DIL_Q_BLOCK + np.arange(kb)[None, :]
    k_blk = kp[:, :, :, idx]
    v_blk = vp[:, :, :, idx]
    q_blk = qp.reshape(B, dil, H, nb, DIL_Q_BLOCK, dh)
    s = jnp.einsum('bphnqd,bphnkd->bphnqk', q_blk, k_blk,
                   preferred_element_type=jnp.float32) * (dh ** -0.5)
    key_pos = idx - radius
    q_pos = np.arange(Lp).reshape(nb, DIL_Q_BLOCK)
    rel = key_pos[:, None, :] - q_pos[:, :, None]
    ok = (np.abs(rel) <= radius) & (key_pos[:, None, :] >= 0) & (key_pos[:, None, :] < L)
    s = jnp.where(jnp.asarray(ok), s, NEG_INF)
    lse = jax.nn.logsumexp(s, axis=-1)
    p = jnp.exp(s - lse[..., None]).astype(v.dtype)
    o = jnp.einsum('bphnqk,bphnkd->bphnqd', p, v_blk)
    o = o.reshape(B, dil, H, Lp, dh)[:, :, :, :L].transpose(0, 3, 1, 2, 4).reshape(B, T, H, dh)
    lse = lse.reshape(B, dil, H, Lp)[:, :, :, :L].transpose(0, 3, 1, 2).reshape(B, T, H)
    return o, lse

def dilated_mixture(q, k, v):
    B, T = q.shape[0], q.shape[1]
    outs, lses = [], []
    for g, (window, dil) in enumerate(DIL_PATTERNS):
        sl = slice(g * DIL_HEADS_PER_GROUP, (g + 1) * DIL_HEADS_PER_GROUP)
        o, l = dilated_group(q[:, :, sl], k[:, :, sl], v[:, :, sl], dil, window // (2 * dil))
        outs.append(o)
        lses.append(l)
    o = jnp.stack(outs, axis=0)
    wts = jax.nn.softmax(jnp.stack(lses, axis=0), axis=0)
    y = jnp.sum(o * wts[..., None].astype(o.dtype), axis=0)
    return y.reshape(B, T, C_OUT_W)

def hybrid_mixer(xn, w_in, rpb, lq1, lk1, lq2, lk2, subln_g, w_pa, w_pb, w_pc, w_o, lam_init, cos, sin):
    B, T, _ = xn.shape
    proj = xn @ w_in
    widths = [A_W] * 3 + [B_QK_W] * 2 + [B_V_W] + [C_W] * 3 + [D_MODEL] * 2
    cuts = [int(c) for c in np.cumsum(widths)]
    qa, ka, va, qb, kb, vb, qc, kc, vc, ga, gb, gc = jnp.split(proj, cuts, axis=-1)

    def heads(t, h):
        return t.reshape(B, T, h, HEAD_DIM)

    ya = neighbourhood_attention(heads(qa, NA_HEADS), heads(ka, NA_HEADS), heads(va, NA_HEADS), rpb)
    qb = partial_rope(heads(qb, 2 * DIFF_HEADS), cos, sin).reshape(B, T, DIFF_HEADS, 2, HEAD_DIM)
    kb = partial_rope(heads(kb, 2 * DIFF_HEADS), cos, sin).reshape(B, T, DIFF_HEADS, 2, HEAD_DIM)
    vb = vb.reshape(B, T, DIFF_HEADS, DIFF_V_DIM)
    f32 = jnp.float32
    lam = (jnp.exp(jnp.sum(lq1.astype(f32) * lk1.astype(f32)))
           - jnp.exp(jnp.sum(lq2.astype(f32) * lk2.astype(f32))) + lam_init)
    yb = differential_attention(qb, kb, vb, lam, lam_init, subln_g)
    yc = dilated_mixture(partial_rope(heads(qc, DIL_HEADS), cos, sin),
                         partial_rope(heads(kc, DIL_HEADS), cos, sin),
                         heads(vc, DIL_HEADS))
    merged = (jax.nn.sigmoid(ga) * (ya @ w_pa) + jax.nn.sigmoid(gb) * (yb @ w_pb)
              + jax.nn.sigmoid(gc) * (yc @ w_pc))
    return merged @ w_o

def hierarchical_moe(xn, wg, bg, we, be, w1, w3, w2):
    B, T, D = xn.shape
    xf = xn.reshape(-1, D)
    N = xf.shape[0]
    g_logits = (xf @ wg).astype(jnp.float32) + bg.astype(jnp.float32)
    g_prob = jax.nn.softmax(g_logits, axis=-1)
    g_sel = jnp.argmax(g_logits, axis=-1)
    g_gate = jnp.take_along_axis(g_prob, g_sel[:, None], axis=-1)
    e_logits = ((xf @ we).astype(jnp.float32) + be.astype(jnp.float32)).reshape(N, N_GROUPS, EXPERTS_PER_GROUP)
    e_logits = jnp.take_along_axis(e_logits, g_sel[:, None, None], axis=1)[:, 0]
    top_v, top_i = lax.top_k(e_logits, TOP_K)
    top_w = jax.nn.softmax(top_v, axis=-1) * g_gate
    eid = g_sel[:, None] * EXPERTS_PER_GROUP + top_i
    combine = jnp.sum(jax.nn.one_hot(eid, N_EXPERTS, dtype=jnp.float32) * top_w[..., None], axis=1)
    combine = combine.astype(xf.dtype)
    out = jnp.zeros_like(xf)
    for e in range(N_EXPERTS):
        h = jax.nn.silu(xf @ w1[e]) * (xf @ w3[e])
        out = out + combine[:, e:e + 1] * (h @ w2[e])
    return out.reshape(B, T, D)

def setup_inputs(seed: int = 0) -> dict:
    key = jax.random.key(seed)
    ks = jax.random.split(key, 22)
    L = DEPTH

    def nrm(k, shape, scale):
        return jax.random.normal(k, shape, jnp.float32) * scale

    return {
        'x': nrm(ks[0], (BATCH, SEQ, D_MODEL), 1.0),
        'w_in': nrm(ks[1], (L, D_MODEL, IN_W), D_MODEL ** -0.5),
        'na_rpb': nrm(ks[2], (L, NA_HEADS, 2 * NA_WIN_R - 1, 2 * NA_WIN_C - 1), 0.02),
        'lam_q1': nrm(ks[3], (L, HEAD_DIM), 0.1),
        'lam_k1': nrm(ks[4], (L, HEAD_DIM), 0.1),
        'lam_q2': nrm(ks[5], (L, HEAD_DIM), 0.1),
        'lam_k2': nrm(ks[6], (L, HEAD_DIM), 0.1),
        'diff_subln': 1.0 + nrm(ks[7], (L, DIFF_V_DIM), 0.01),
        'w_pa': nrm(ks[8], (L, A_W, D_MODEL), A_W ** -0.5),
        'w_pb': nrm(ks[9], (L, B_V_W, D_MODEL), B_V_W ** -0.5),
        'w_pc': nrm(ks[10], (L, C_OUT_W, D_MODEL), C_OUT_W ** -0.5),
        'w_o': nrm(ks[11], (L, D_MODEL, D_MODEL), D_MODEL ** -0.5),
        'norm_mix': 1.0 + nrm(ks[12], (L, D_MODEL), 0.01),
        'norm_ffn': 1.0 + nrm(ks[13], (L, D_MODEL), 0.01),
        'router_group_w': nrm(ks[14], (L, D_MODEL, N_GROUPS), D_MODEL ** -0.5),
        'router_group_b': nrm(ks[15], (L, N_GROUPS), 0.01),
        'router_expert_w': nrm(ks[16], (L, D_MODEL, N_EXPERTS), D_MODEL ** -0.5),
        'router_expert_b': nrm(ks[17], (L, N_EXPERTS), 0.01),
        'w1': nrm(ks[18], (L, N_EXPERTS, D_MODEL, D_FF_EXPERT), D_MODEL ** -0.5),
        'w3': nrm(ks[19], (L, N_EXPERTS, D_MODEL, D_FF_EXPERT), D_MODEL ** -0.5),
        'w2': nrm(ks[20], (L, N_EXPERTS, D_FF_EXPERT, D_MODEL), D_FF_EXPERT ** -0.5),
        'norm_final': 1.0 + nrm(ks[21], (D_MODEL,), 0.01),
    }

def reference(x, w_in, na_rpb, lam_q1, lam_k1, lam_q2, lam_k2, diff_subln, w_pa, w_pb, w_pc, w_o,
              norm_mix, norm_ffn, router_group_w, router_group_b, router_expert_w, router_expert_b,
              w1, w3, w2, norm_final):
    T = x.shape[1]
    cos, sin = rope_tables(T)
    h = x
    for l in range(DEPTH):
        lam_init = 0.8 - 0.6 * math.exp(-0.3 * l)
        h = h + hybrid_mixer(rmsnorm(h, norm_mix[l]), w_in[l], na_rpb[l], lam_q1[l], lam_k1[l],
                             lam_q2[l], lam_k2[l], diff_subln[l], w_pa[l], w_pb[l], w_pc[l], w_o[l],
                             lam_init, cos, sin)
        h = h + hierarchical_moe(rmsnorm(h, norm_ffn[l]), router_group_w[l], router_group_b[l],
                                 router_expert_w[l], router_expert_b[l], w1[l], w3[l], w2[l])
    return rmsnorm(h, norm_final)


_drawn_inputs = setup_inputs


def setup_inputs(seed=0):
    import zlib

    import numpy as np

    out = dict(_drawn_inputs(seed))
    spreads = {}
    factors = {'na_rpb': 31.501,
     'diff_subln': 15.612,
     'router_group_b': 17.129,
     'router_expert_b': 23.678,
     'norm_final': 29.992,
     'norm_ffn': 4.941}
    for name, (base, spread) in spreads.items():
        noise = np.random.default_rng([zlib.crc32(name.encode()), seed]).standard_normal(out[name].shape)
        drawn = base * np.exp(spread * noise) if base else spread * noise
        out[name] = __import__('jax').numpy.asarray(drawn.astype(out[name].dtype))
    for name, factor in factors.items():
        out[name] = (out[name] * factor).astype(out[name].dtype)
    return out
```

```python
import math
from contextlib import ExitStack

import numpy as np

import concourse.bass as bass
from concourse import mybir

F32 = mybir.dt.float32
BF16 = mybir.dt.bfloat16
I32 = mybir.dt.int32
U32 = mybir.dt.uint32
ALU = mybir.AluOpType
ACT = mybir.ActivationFunctionType
AX_X = mybir.AxisListType.X

P = 128
T = 256
TT = T // P
D = 1024
KD = D // P
DEPTH = 2
DH = 64
GRID_W = 64
A_HEADS = 8
B_HEADS = 4
C_GROUPS = 3
C_HEADS = 4
SCALE = DH ** -0.5
NEG = -1e30
NORM_EPS = 1e-6
SUBLN_EPS = 1e-5
N_EXP = 16
N_GRP = 4
PER_GRP = N_EXP // N_GRP
F_EXP = D // 2
KF = F_EXP // P
CAP = 64
FAR = 1000.0
PAIRS = N_EXP // 2
N_OVER = 8
SLOT = 4096
RING = 6
RPB = 15 * 31
RPB_C = 31
N_GAIN, N_SUBG, N_LAM, N_RB, N_WR, N_TAB = 0, 16, 17, 18, 38, 198

C_IDENT, C_SWAP, C_COS, C_SIN = 0, 128, 256, 512
C_IOTA, C_IOTA64, C_W16, C_THR, C_EIDX, C_JROW, C_LINIT = 768, 896, 1024, 1040, 1072, 1104, 1112
C_KEEP = 1116
C_TRI, C_IDB, C_ONE, C_MASKA = C_KEEP, C_KEEP + 128, C_KEEP + 256, C_KEEP + 384
C_MASKC = C_MASKA + 512
C_ALL = C_MASKC + C_GROUPS * TT * T
NB16 = C_ALL - C_KEEP


def constants():
    c = np.zeros((P, C_ALL), np.float32)
    p = np.arange(P)
    c[:, C_IDENT:C_IDENT + P] = np.eye(P)
    half = 8
    inv = (1.0 / (np.float32(500000.0) ** (np.arange(0, 16, 2, dtype=np.float32) / np.float32(16)))).astype(np.float32)
    ang = np.arange(T, dtype=np.float32)[:, None] * inv[None, :]
    cos, sin = np.cos(ang).T, np.sin(ang).T
    c[:, C_COS:C_COS + T] = 1.0
    for q in p:
        d = q % DH
        if d < 2 * half:
            partner = q + half if d < half else q - half
            c[partner, C_SWAP + q] = 1.0
            c[q, C_COS:C_COS + T] = cos[d % half]
            c[q, C_SIN:C_SIN + T] = -sin[d] if d < half else sin[d - half]
    tok = np.arange(T)
    col = tok % GRID_W
    first = np.clip(col - 8, 0, GRID_W - 16)
    ok = (col[None, :] >= first[:, None]) & (col[None, :] < first[:, None] + 16)
    mask = lambda ok: np.where(ok, 0.0, NEG).reshape(TT, P, T).transpose(1, 0, 2).reshape(P, TT * T)
    c[:, C_MASKA:C_MASKA + TT * T] = mask(ok)
    c[:, C_IOTA:C_IOTA + P] = np.arange(P)
    c[:, C_IOTA64:C_IOTA64 + P] = np.arange(P) % CAP
    c[:, C_W16:C_W16 + 16] = 16 - np.arange(16)
    c[:, C_THR:C_THR + 32] = np.tile([CAP, CAP + P], 16)
    c[:, C_EIDX:C_EIDX + 32] = np.repeat(np.arange(16), 2)
    c[:, C_JROW:C_JROW + N_OVER] = 1 + np.arange(N_OVER)
    for layer in range(DEPTH):
        lam = 0.8 - 0.6 * math.exp(-0.3 * layer)
        c[:, C_LINIT + 2 * layer] = lam
        c[:, C_LINIT + 2 * layer + 1] = 1.0 - lam
    c[:, C_TRI:C_TRI + P] = p[:, None] < p[None, :]
    c[:, C_IDB:C_IDB + P] = np.eye(P)
    c[:, C_ONE:C_ONE + P] = 1.0
    for g, dil in enumerate((1, 4, 16)):
        diff = tok[None, :] - tok[:, None]
        ok = (diff % dil == 0) & (np.abs(diff) <= 64 * dil)
        c[:, C_MASKC + g * TT * T:C_MASKC + (g + 1) * TT * T] = mask(ok)
    return c


ORDER = [("in", b) for b in range(10)] + [("pa", 0), ("in", 10), ("in", 11), ("in", 12), ("pb", 0), ("in", 13),
         ("in", 14), ("pc", 0), ("in", 15), ("in", 16)] + [("wo", s) for s in range(4)]
AT = {w: n for n, w in enumerate(ORDER)}
assert len(ORDER) % RING == 0
ROUNDS_1 = len(ORDER) // RING

UNITS = []
for _br, _b0 in (("A", 0), ("B", 3)):
    for _role, _b in (("q", 0), ("k", 1)):
        UNITS += [(_br, _role, i, _b0 + _b, 2 * i) for i in range(2)]
    UNITS += [(_br, "v", tt, _b0 + 2, 0) for tt in range(TT)]
UNITS += [("C", "q", 0, 6, 0), ("C", "q", 1, 6, 2), ("C", "q", 2, 7, 0),
          ("C", "k", 0, 7, 2), ("C", "k", 1, 8, 0), ("C", "k", 2, 8, 2),
          ("C", "v", 0, 9, 0), ("C", "v", 1, 9, 0), ("C", "v2", 0, 10, 0)]
UNITS += [("ABC"[(g := (4 * b + t - 42) // 2) // 4], "gate", g, b, t)
          for b in range(10, 17) for t in (0, 2) if 4 * b + t >= 42 and 4 * b + t < 66]
GATE0 = UNITS.index(("A", "gate", 0, 10, 2))
N_UNITS = len(UNITS)
ROPE = [u for u, x in enumerate(UNITS) if x[0] in "BC" and x[1] in "qk"]
LAST_UNIT = {b: max(u for u, x in enumerate(UNITS) if x[3] == b) for b in range(17)}


def timeline():
    after = {
        6: [("score", "A", 0), ("score", "A", 1), ("soft", "A", 0), ("soft", "A", 1)],
        7: [("turn", "A", 0), ("score", "A", 2), ("turn", "A", 1), ("score", "A", 3), ("soft", "A", 2), ("soft", "A", 3)],
        8: [("pv", "A", 0), ("turn", "A", 2), ("score", "A", 4), ("turn", "A", 3), ("score", "A", 5), ("soft", "A", 4),
            ("soft", "A", 5)],
        9: [("pv", "A", 1), ("turn", "A", 4), ("score", "A", 6), ("turn", "A", 5), ("score", "A", 7), ("soft", "A", 6),
            ("soft", "A", 7)],
        10: [("pv", "A", 2), ("turn", "A", 6), ("turn", "A", 7)],
        11: [("pv", "A", 3)],
        12: [("score", "B", 0), ("soft", "B", 0)],
        13: [("turn", "B", 0), ("score", "B", 1), ("soft", "B", 1)],
        14: [("pv", "B", 0), ("turn", "B", 1), ("score", "B", 2), ("soft", "B", 2)],
        15: [("ms", "B", 0), ("pv", "B", 1), ("turn", "B", 2), ("score", "B", 3), ("soft", "B", 3)],
        16: [("ms", "B", 1), ("pv", "B", 2), ("turn", "B", 3)],
        17: [("ms", "B", 2), ("pv", "B", 3)],
        18: [("ms", "B", 3)],
        20: [("score", "C", 0), ("soft", "C", 0)],
        GATE0: [("turn", "C", 0)], GATE0 + 1: [("pv", "C", 0), ("score", "C", 1), ("soft", "C", 1)],
        GATE0 + 2: [("turn", "C", 1)], GATE0 + 3: [("pv", "C", 1), ("score", "C", 2), ("soft", "C", 2)],
        GATE0 + 4: [("turn", "C", 2)], GATE0 + 5: [("pv", "C", 2), ("score", "C", 3), ("soft", "C", 3)],
        GATE0 + 6: [("turn", "C", 3)], GATE0 + 7: [("pv", "C", 3)],
    }
    steps = []
    for u, x in enumerate(UNITS):
        steps.append(("unit", x[0], u))
        if u - 1 in ROPE:
            steps.append(("swap", UNITS[u - 1][0], u - 1))
        if x[1] == "gate":
            steps.append(("branch", x[0], x[2]))
        steps += after.get(u, [])
    return steps + [("out", "", s) for s in range(4)]


TIMELINE = timeline()

N_SCORE = A_HEADS + 2 * B_HEADS + C_GROUPS * C_HEADS
N_TURN = A_HEADS + B_HEADS + C_GROUPS * C_HEADS


def score_no(br, n, part=0):
    return {"A": n, "B": A_HEADS + 2 * n + part, "C": A_HEADS + 2 * B_HEADS + C_GROUPS * n + part}[br]


def turn_no(br, n, part=0):
    return {"A": n, "B": A_HEADS + n, "C": A_HEADS + B_HEADS + C_GROUPS * n + part}[br]


def max_no(br, n, part=0):
    return {"A": n, "B": A_HEADS + 2 * n + part, "C": A_HEADS + 2 * B_HEADS + n}[br]


N_MAX = A_HEADS + 2 * B_HEADS + C_HEADS


def pv_no(br, n):
    return {"A": n, "B": 4 + n, "C": 8 + n}[br]


def build(nc, x, w_in, na_rpb, lam_q1, lam_k1, lam_q2, lam_k2, diff_subln, w_pa, w_pb, w_pc, w_o,
          norm_mix, norm_ffn, router_group_w, router_group_b, router_expert_w, router_expert_b,
          w1, w3, w2, norm_final, consts, out):
    with ExitStack() as ctx:
        def sb(name, cols, dt=F32):
            return ctx.enter_context(nc.sbuf_tensor(name, [P, cols], dt))

        def sem(name):
            return ctx.enter_context(nc.semaphore(name))

        ring = sb("ring", RING * SLOT)
        h = sb("h", TT * D)
        xh = sb("xh", TT * D)
        xnT = sb("xnT", KD * T)
        zone_q1 = sb("zone_q1", 6 * 2 * T)
        zone_k1 = sb("zone_k1", 6 * T)
        zone_v1 = sb("zone_v1", TT * 512)
        zone_b = sb("zone_b", 2048)
        zone_q2 = sb("zone_q2", 4 * 2 * T)
        zone_k2 = xh[:, 0:4 * T]
        zone_v2 = xh[:, 4 * T:4 * T + TT * 512]
        zone_y = sb("zone_y", 10 * T)
        zone_p = sb("zone_p", 4 * TT * T)
        zone_t = sb("zone_t", 4 * TT * T)
        zone_s = sb("zone_s", 2 * 512)
        zone_c = sb("zone_c", 512)
        cf = sb("cf", C_KEEP)
        cb = sb("cb", NB16, BF16)
        msq = sb("msq", P)
        tab = sb("tab", DEPTH * N_TAB)
        cur = sb("cur", N_TAB)
        sm = sb("sm", 640)
        nexp = sb("nexp", 16, I32)

        h3 = h[:, :].rearrange("p (t d) -> p t d", t=TT)
        xh3 = xh[:, :].rearrange("p (t d) -> p t d", t=TT)
        mT = xh[:, :].rearrange("p (c t) -> p c t", c=KD)
        xnT3 = xnT[:, :].rearrange("p (c t) -> p c t", c=KD)
        q_of = {"A": zone_q1, "B": zone_q2, "C": zone_q1}
        k_of = {"A": zone_k1[:, :], "B": zone_k2, "C": zone_k1[:, :]}
        q_of = {b: z[:, :].rearrange("p (i m t) -> p i m t", m=2, t=T) for b, z in q_of.items()}
        k_of = {b: z.rearrange("p (i t) -> p i t", t=T) for b, z in k_of.items()}
        v_of = {"A": zone_v1[:, :].rearrange("p (t n) -> p t n", t=TT),
                "B": zone_v2.rearrange("p (t n) -> p t n", t=TT),
                "C": zone_b[:, 0:TT * 768].rearrange("p (t n) -> p t n", t=TT)}
        biasA = zone_b[:, :].rearrange("p (s h t k) -> p s h t k", s=2, h=2, t=TT)
        yT = zone_y[:, :].rearrange("p (i t) -> p i t", t=T)
        y_at = {"A": 0, "B": 4, "C": 8}
        prob = zone_p[:, :].rearrange("p (s t k) -> p s t k", s=4, t=TT)
        probT = zone_t[:, :].rearrange("p (s k t) -> p s k t", s=4, k=TT)
        tab3 = tab[:, :].rearrange("p (l n) -> p l n", l=DEPTH)
        gain = cur[:, N_GAIN:N_GAIN + 2 * KD].rearrange("p (n c) -> p n c", n=2)
        subg, lam = cur[:, N_SUBG:N_SUBG + 1], cur[:, N_LAM:N_LAM + 1]
        rb, wr = cur[:, N_RB:N_RB + 20], cur[:, N_WR:N_WR + KD * 20]
        lam_in = zone_k1[:, 0:DEPTH * 4 * DH].rearrange("p (l n d) -> p l n d", l=DEPTH, n=4)
        lam_pr = zone_k1[:, 512:512 + DEPTH * 2 * DH].rearrange("p (l n d) -> p l n d", l=DEPTH, n=2)
        root = zone_v1[:, 0:512].rearrange("p (s t) -> p s t", s=2)
        fin = zone_k1[:, 0:D]
        pre = zone_s[:, :].rearrange("p (s n) -> p s n", s=2)
        ident = cf[:, C_IDENT:C_IDENT + P]
        swap = cf[:, C_SWAP:C_SWAP + P]
        cos2 = cf[:, C_COS:C_COS + T].unsqueeze(1).broadcast_to([P, 2, T])
        sin2 = cf[:, C_SIN:C_SIN + T].unsqueeze(1).broadcast_to([P, 2, T])
        bcol = lambda at, n: cb[:, at - C_KEEP:at - C_KEEP + n]
        tri, identb, oneb = bcol(C_TRI, P), bcol(C_IDB, P), bcol(C_ONE, P)
        maskA = bcol(C_MASKA, TT * T)
        maskC = bcol(C_MASKC, C_GROUPS * TT * T).rearrange("p (g t k) -> p g t k", g=C_GROUPS, t=TT)
        xg = zone_p[:, 0:D]
        xgT = zone_p[:, D:2 * D].rearrange("p (c s) -> p c s", c=KD)
        y_e = zone_t[:, 0:D]
        hT = zone_t[:, D:D + 512].rearrange("p (f s) -> p f s", f=KF)
        sig = zone_t[:, D + 512:D + 1024]
        hid = zone_y[:, 0:512]
        selT = zone_y[:, 512:768]
        sel = zone_y[:, 768:1024].rearrange("p (t s) -> p t s", t=TT)
        selg = zone_y[:, 1024:1280].rearrange("p (t s) -> p t s", t=TT)
        over_a = zone_y[:, 1280:1536].rearrange("p (j e) -> p j e", j=N_OVER)
        over_b = zone_y[:, 1536:1792].rearrange("p (j e) -> p j e", j=N_OVER)

        at = [0]

        def small(n):
            at[0] += n
            return sm[:, at[0] - n:at[0]]

        ss, std, rstd = small(2), small(2), small(2)
        eps1, eps2 = small(1), small(1)
        lam2, lam_e = (small(2 * DEPTH).rearrange("p (l n) -> p l n", l=DEPTH) for _ in range(2))
        nmx = small(4 * 2).rearrange("p (s t) -> p s t", s=4)
        raw = small(4 * 2).rearrange("p (s t) -> p s t", s=4)
        mxc = small(2 * 3).rearrange("p (t g) -> p t g", g=3)
        psum_ = small(4 * 2).rearrange("p (s t) -> p s t", s=4)
        psc = small(2 * 3).rearrange("p (t g) -> p t g", g=3)
        rin = small(4 * 2).rearrange("p (s t) -> p s t", s=4)
        lg = small(2 * 20).rearrange("p (t e) -> p t e", t=TT)
        g4a, g4b, goh = (small(8).rearrange("p (t e) -> p t e", t=TT) for _ in range(3))
        s2 = [small(2) for _ in range(12)]
        e16 = [small(32).rearrange("p (t e) -> p t e", t=TT) for _ in range(5)]
        pos, gat = (small(32).rearrange("p (t e) -> p t e", t=TT) for _ in range(2))
        cnt = small(16)
        exist, cum, zero32 = small(32), small(32), small(32)
        pos_o, gat_o = (small(2 * N_OVER).rearrange("p (t j) -> p t j", t=TT) for _ in range(2))
        eid_o = small(N_OVER)
        asg = sb("asg", 32, BF16)[:, :].rearrange("p (t e) -> p t e", t=TT)
        assert at[0] <= 640, at[0]

        copies = nc.dram_tensor("copies", (GRID_W, DEPTH * A_HEADS * RPB), F32).ap()

        bank = [ctx.enter_context(nc.psum_tensor(f"bank{i}", [P, 512], F32)) for i in range(8)]

        names = """consts_in copies_in setup_v setup_b x_in small_in bias_in fin_in out_done lam_v lam_s cur_v final_v
            sq std_s xh_v turned xnT_v xnT_s
            unit_pe unit_s swap_pe cos_p rope_v vstep pstep bias_p
            score_pe scoreA_v max_v exp_s prob_v turn_pe turn_v pv_pe y_s yb_v msq_s ms_pe std_b
            branch_pe mix_v mix_p out_pe h_v
            logit_pe rexp_s rd_v asg_v rank_pe pos_v over_v list_seen
            m_sel_v m_selg_v m_gather m_xg_s m_xg_v m_xt m_xgT_v m_h m_sig_s m_hid_v m_ht m_hT_s m_st m_selT_s
            m_y m_y_s m_y_v m_sc m_add_v""".split()
        S = {n: sem(n) for n in names}
        landed = [sem(f"landed{i}") for i in range(RING)]

        def slot(n, cols=SLOT):
            return ring[:, n * SLOT:n * SLOT + cols]

        def ring_view(n, k, cols):
            return slot(n, k * cols).rearrange("p (k n) -> p k n", k=k)

        block = ctx.enter_context(nc.Block())

        @block.sync
        def _(sp):
            units = sp.alloc_register("sp_units")
            sp.reg_mov(units, 0)
            layers = sp.alloc_register("sp_layers")
            sp.reg_mov(layers, 0)

            def load(n, l):
                kind, b = ORDER[n]
                if kind == "in":
                    cols = min(512, 8448 - 512 * b)
                    src = w_in[l, :, 512 * b:512 * b + cols].rearrange("(k p) n -> p k n", p=P)
                    dst = ring_view(n % RING, KD, cols)
                elif kind == "wo":
                    src = w_o[l, :, 256 * b:256 * b + 256].rearrange("(k p) n -> p k n", p=P)
                    dst = ring_view(n % RING, KD, 256)
                else:
                    w = {"pa": w_pa, "pb": w_pb, "pc": w_pc}[kind]
                    src = w[l].rearrange("(k p) n -> p k n", p=P)
                    dst = ring_view(n % RING, w.shape[1] // P, D)
                sp.dma_start(dst, src).then_inc(landed[n % RING], 16)

            def wait_free(n, l):
                kind, b = ORDER[n]
                if kind == "in":
                    sp.wait_ge(S["unit_pe"], l * N_UNITS + LAST_UNIT[b] + 1)
                elif kind == "wo":
                    sp.wait_ge(S["out_pe"], l * 4 + b + 1)
                else:
                    sp.wait_ge(S["branch_pe"], l * 12 + {"pa": 4, "pb": 8, "pc": 12}[kind])

            w1_r = w1.rearrange("l e (k p) f -> (l e) p k f", p=P)
            w3_r = w3.rearrange("l e (k p) f -> (l e) p k f", p=P)
            w2_r = w2.rearrange("l e (k p) f -> (l e) p k f", p=P)

            def load_expert(which, item, e):
                src = (w1_r, w3_r, w2_r)[which][bass.ds(e, 1)].rearrange("o p k f -> p (o k) f")
                k, cols = (KF, D) if which == 2 else (KD, F_EXP)
                sp.dma_start(ring_view(2 * which + item, k, cols), src).then_inc(landed[2 * which + item], 16)

            def wait_unit(which, last):
                if which < 2:
                    sp.wait_ge(S["m_h"], last * 2 + 1 + which)
                else:
                    sp.wait_ge(S["m_y"], last * 2 + 2)

            sp.dma_start(h3, x[0].rearrange("(t p) d -> p t d", p=P)).then_inc(S["x_in"], 16)
            for n in range(RING):
                load(n, 0)
            with sp.Fori(0, DEPTH) as l:
                for n in range(RING, len(ORDER)):
                    wait_free(n - RING, l)
                    load(n, l)
                for which in range(3):
                    for item in range(2):
                        wait_free(len(ORDER) - RING + 2 * which + item, l)
                        load_expert(which, item, l * N_EXP + item)
                with sp.Fori(1, PAIRS) as p:
                    last = sp.snap(units)
                    for which in range(3):
                        wait_unit(which, last)
                        for item in range(2):
                            load_expert(which, item, l * N_EXP + p * 2 + item)
                    sp.reg_add(units, units, 1)
                sp.wait_ge(S["over_v"], l + 1)
                sp.sem_inc(S["list_seen"], 1)
                n_over = sp.value_load(nexp[0:1, 0:1], min_val=0, max_val=N_OVER)
                with sp.If(n_over > 0):
                    with sp.Fori(0, n_over) as j:
                        last = sp.snap(units)
                        e = sp.value_load(nexp[0:1, bass.ds(j + 1, 1)], min_val=0, max_val=N_EXP - 1)
                        for which in range(3):
                            wait_unit(which, last)
                            src = (w1_r, w3_r, w2_r)[which][bass.ds(l * N_EXP + e, 1)].rearrange("o p k f -> p (o k) f")
                            k, cols = (KF, D) if which == 2 else (KD, F_EXP)
                            for part in range(2):
                                sp.dma_start(ring_view(2 * which + part, k // 2, cols),
                                             src[:, part * k // 2:(part + 1) * k // 2, :]).then_inc(
                                                 landed[2 * which + part], 16)
                        sp.reg_add(units, units, 1)
                sp.reg_add(layers, layers, 1)
                with sp.If(l < DEPTH - 1):
                    last = sp.snap(units)
                    following = sp.snap(layers, min_val=1, max_val=DEPTH - 1)
                    for n in range(RING):
                        wait_unit(n // 2, last)
                        load(n, following)
                sp.reg_add(units, units, 1)

        @block.gpsimd
        def _(pool):
            pool.dma_start(zone_q1[:, 0:C_ALL - C_KEEP], consts[:, C_KEEP:C_ALL]).then_inc(S["consts_in"], 16)
            pool.dma_start(cf[:, :], consts[:, 0:C_KEEP]).then_inc(S["consts_in"], 16)
            pool.wait_ge(S["consts_in"], 32)
            nc.gpsimd.tensor_copy(cb[:, :], zone_q1[:, 0:NB16]).then_inc(S["setup_b"], 1)
            pool.wait_ge(S["setup_b"], 1)
            nc.gpsimd.memset(zone_q1[:, :], 0.0).then_inc(S["setup_b"], 1)
            nc.gpsimd.memset(zone_q2[:, :], 0.0).then_inc(S["setup_b"], 1)

            pool.dma_start(copies, na_rpb.rearrange("l h a b -> (l h a b)").partition_broadcast(GRID_W)
                           ).then_inc(S["copies_in"], 16)

            def get(dst, src):
                pool.dma_start(dst, src, allow_slow_non_contiguous=True).then_inc(S["small_in"], 16)

            for l in range(DEPTH):
                get(tab3[:, l, N_GAIN:N_GAIN + KD], norm_mix[l, :].rearrange("(c p) -> p c", p=P))
                get(tab3[:, l, N_GAIN + KD:N_GAIN + 2 * KD], norm_ffn[l, :].rearrange("(c p) -> p c", p=P))
                get(tab3[:, l, N_SUBG:N_SUBG + 1], diff_subln[l, :].unsqueeze(1))
                get(tab3[:, l, N_RB:N_RB + 4], router_group_b[l, :].partition_broadcast(P))
                get(tab3[:, l, N_RB + 4:N_RB + 20], router_expert_b[l, :].partition_broadcast(P))
                w = tab3[:, l, N_WR:N_WR + KD * 20].rearrange("p (k e) -> p k e", e=20)
                get(w[:, :, 0:4], router_group_w[l].rearrange("(k p) e -> p k e", p=P))
                get(w[:, :, 4:20], router_expert_w[l].rearrange("(k p) e -> p k e", p=P))
                for i, a in enumerate((lam_q1, lam_q2, lam_k1, lam_k2)):
                    get(lam_in[:, l, i, :], a[l, :].partition_broadcast(P))

            def bias_loads(l, pair):
                for hh in range(2):
                    for r in range(4):
                        tt, p0 = r // 2, 64 * (r % 2)
                        at = (2 * pair + hh) * RPB + (7 - r) * RPB_C + 15
                        src = copies[:, bass.ds(l * A_HEADS * RPB + at, 3 * RPB_C + GRID_W)]
                        src = bass.AP(tensor=src.tensor, offset=src.offset,
                                      ap=[[DEPTH * A_HEADS * RPB - 1, GRID_W], [RPB_C, 4], [1, GRID_W]])
                        dst = biasA[p0:p0 + 64, pair % 2, hh, tt, :].rearrange("p (a b) -> p a b", b=GRID_W)
                        pool.dma_start(dst, src).then_inc(S["bias_in"], 16)

            pool.wait_ge(S["copies_in"], 16)
            with pool.Fori(0, DEPTH) as l:
                for kind, br, n in TIMELINE:
                    if kind == "unit" and n in (0, 1, 7, 8):
                        pair = {0: 0, 1: 1, 7: 2, 8: 3}[n]
                        if pair >= 2:
                            pool.wait_ge(S["scoreA_v"], l * A_HEADS + 2 * (pair - 2) + 2)
                        else:
                            pool.wait_ge(S["turned"], l * 8 + 1)
                        bias_loads(l, pair)
                        pool.wait_ge(S["bias_in"], (l * 4 + pair + 1) * 128)
                        b = biasA[:, pair % 2, :, :, :].rearrange("p h t k -> p h (t k)")
                        nc.gpsimd.tensor_tensor(b, b, maskA.unsqueeze(1).broadcast_to([P, 2, TT * T]),
                                                ALU.add).then_inc(S["bias_p"], 1)
                    if kind == "swap":
                        i = ROPE.index(n)
                        pool.wait_ge(S["unit_s"], l * N_UNITS + n + 1)
                        if i > 0:
                            pool.wait_ge(S["rope_v"], l * len(ROPE) + i)
                        nc.gpsimd.tensor_tensor(zone_c[:, :].rearrange("p (i t) -> p i t", i=2),
                                                pre[:, n % 2, :].rearrange("p (i t) -> p i t", i=2),
                                                cos2, ALU.mult).then_inc(S["cos_p"], 1)
                    if kind == "branch" and br != "A":
                        pool.wait_ge(S["mix_v"], l * 12 + n + 1)
                        if n >= 8:
                            pool.wait_ge(S["mix_p"], l * 8 + n - 7)
                        i = n % 4
                        m = xh[:, 512 * i:512 * i + 512]
                        nc.gpsimd.tensor_tensor(m, m, pre[:, n % 2, :], ALU.add).then_inc(S["mix_p"], 1)

            pool.wait_ge(S["over_v"], DEPTH)
            pool.dma_start(fin, norm_final[:].partition_broadcast(P)).then_inc(S["fin_in"], 16)

        @block.tensor
        def _(pe):
            units = pe.alloc_register("pe_units")
            pe.reg_mov(units, 0)

            def arrived(n, l, first=None):
                pe.wait_ge(landed[n % RING], (l * ROUNDS_1 + pe.snap(units) + n // RING + 1) * 16)

            def turn_x(l, which):
                pe.wait_ge(S["xh_v"], l * 4 + which * 2 + 2)
                for b in range(4):
                    for c in (2 * b, 2 * b + 1):
                        for tt in range(TT):
                            at = (c % 2) * T + tt * P
                            last = pe.transpose(bank[b][:, at:at + P], xh3[:, tt, c * P:c * P + P], ident)
                    last.then_inc(S["turned"], 1)

            pe.wait_ge(S["consts_in"], 32)
            pe.wait_ge(S["setup_b"], 3)
            pe.wait_ge(S["setup_v"], 4)
            with pe.Fori(0, DEPTH) as l:
                turn_x(l, 0)
                pe.wait_ge(S["xnT_v"], l * 4 + 2)
                pe.wait_ge(S["xnT_s"], l * 8 + 4)
                seen = set()
                for kind, br, n in TIMELINE:
                    if kind == "unit":
                        _, role, i, b, t0 = UNITS[n]
                        if b not in seen:
                            seen.add(b)
                            arrived(AT["in", b], l)
                        w = ring_view(AT["in", b] % RING, KD, min(512, 8448 - 512 * b))
                        o = bank[1] if role == "gate" else bank[n % 2]
                        if role == "gate" and n > GATE0:
                            pe.wait_ge(S["unit_s"], l * N_UNITS + n)
                        elif n >= 2:
                            pe.wait_ge(S["unit_s"], l * N_UNITS + n - 1)
                        if role in ("q", "k", "gate"):
                            for c2 in range(2):
                                for k in range(KD):
                                    last = pe.matmul(o[:, c2 * T:c2 * T + T], w[:, k, (t0 + c2) * P:(t0 + c2 + 1) * P],
                                                     xnT3[:, k, :], start=(k == 0), stop=(k == KD - 1))
                        elif role == "v":
                            for k in range(KD):
                                last = pe.matmul(o[:, :], xnT3[:, k, i * P:i * P + P], w[:, k, :],
                                                 start=(k == 0), stop=(k == KD - 1))
                        else:
                            for tt in range(TT):
                                for k in range(KD):
                                    last = pe.matmul(o[:, tt * 256:tt * 256 + 256], xnT3[:, k, tt * P:tt * P + P],
                                                     w[:, k, 0:256], start=(k == 0), stop=(k == KD - 1))
                        last.then_inc(S["unit_pe"], 1)
                    elif kind == "swap":
                        i = ROPE.index(n)
                        pe.wait_ge(S["unit_s"], l * N_UNITS + n + 1)
                        if i > 0:
                            pe.wait_ge(S["rope_v"], l * len(ROPE) + i)
                        pe.matmul(bank[6][:, :], swap, pre[:, n % 2, :], start=True, stop=True).then_inc(S["swap_pe"], 1)
                    elif kind == "score":
                        for part in range({"A": 1, "B": 2, "C": 3}[br]):
                            no = score_no(br, n, part)
                            if br == "A":
                                tile, m, o = n // 2, n % 2, bank[2 + n % 2]
                                if n == 0:
                                    pe.wait_ge(S["unit_s"], l * N_UNITS + 6)
                                if n >= 2:
                                    pe.wait_ge(S["scoreA_v"], l * A_HEADS + n - 1)
                            elif br == "B":
                                tile, m, o = n, part, bank[2 + part]
                                if n == 0 and part == 0:
                                    pe.wait_ge(S["rope_v"], l * len(ROPE) + 4)
                                    pe.wait_ge(S["scoreA_v"], l * A_HEADS + A_HEADS)
                                if n > 0:
                                    pe.wait_ge(S["exp_s"], l * N_SCORE + score_no(br, n - 1, part) + 1)
                            else:
                                tile, m, o = (part * C_HEADS + n) // 2, n % 2, bank[2 + part]
                                if n == 0 and part == 0:
                                    pe.wait_ge(S["rope_v"], l * len(ROPE) + 10)
                                    pe.wait_ge(S["exp_s"], l * N_SCORE + score_no("B", 3, 1) + 1)
                                    pe.wait_ge(S["yb_v"], l * B_HEADS + 4)
                                if n > 0:
                                    pe.wait_ge(S["exp_s"], l * N_SCORE + score_no(br, n - 1, part) + 1)
                                for tt in range(TT):
                                    pe.matmul(o[:, tt * T:tt * T + T], identb, maskC[:, part, tt, :],
                                              start=True, stop=False, skip_group_check=True)
                                    last = pe.matmul(o[:, tt * T:tt * T + T], q_of[br][:, tile, m, tt * P:tt * P + P],
                                                     k_of[br][:, tile, :], start=False, stop=True, skip_group_check=True)
                            if br != "C":
                                for tt in range(TT):
                                    last = pe.matmul(o[:, tt * T:tt * T + T], q_of[br][:, tile, m, tt * P:tt * P + P],
                                                     k_of[br][:, tile, :], start=True, stop=True)
                            last.then_inc(S["score_pe"], 1)
                    elif kind == "turn":
                        for part in range(C_GROUPS if br == "C" else 1):
                            no = turn_no(br, n, part)
                            slot_p = {"A": n % 4, "B": 2 * (n % 2), "C": part}[br]
                            o = {"A": bank[4 + n % 2], "B": bank[5], "C": bank[5 + part % 2]}[br]
                            pe.wait_ge(S["prob_v"], l * N_TURN + no + 1)
                            if br == "A" and n >= 2:
                                pe.wait_ge(S["turn_v"], l * N_TURN + no - 1)
                            elif br == "B":
                                pe.wait_ge(S["turn_v"], l * N_TURN + no)
                            elif br == "C":
                                pe.wait_ge(S["turn_v"], l * N_TURN + no - (1 if part == 2 or part == 1 else 0))
                            for kt in range(TT):
                                for tt in range(TT):
                                    at = kt * T + tt * P
                                    last = pe.transpose(o[:, at:at + P], prob[:, slot_p, tt, kt * P:kt * P + P], ident)
                            last.then_inc(S["turn_pe"], 1)
                    elif kind == "pv":
                        if br == "A":
                            o = bank[7]
                            pe.wait_ge(S["turn_v"], l * N_TURN + turn_no("A", 2 * n + 1) + 1)
                            if n > 0:
                                pe.wait_ge(S["y_s"], l * 8 + n)
                            for kt in range(TT):
                                for m in range(2):
                                    hd = 2 * n + m
                                    last = pe.matmul(o[m * DH:m * DH + DH, 0:T], v_of["A"][:, kt, hd * DH:hd * DH + DH],
                                                     probT[:, hd % 4, kt, :], start=(kt == 0), stop=(kt == TT - 1))
                        elif br == "B":
                            o = bank[7 if n % 2 == 0 else 4]
                            pe.wait_ge(S["turn_v"], l * N_TURN + turn_no("B", n) + 1)
                            if n == 0:
                                pe.wait_ge(S["y_s"], l * 8 + 4)
                                pe.wait_ge(S["unit_s"], l * N_UNITS + 12)
                            if n >= 2:
                                pe.wait_ge(S["yb_v"], l * B_HEADS + n - 1)
                            for kt in range(TT):
                                last = pe.matmul(o[:, 0:T], v_of["B"][:, kt, n * P:n * P + P], probT[:, n % 4, kt, :],
                                                 start=(kt == 0), stop=(kt == TT - 1))
                        else:
                            o = bank[7]
                            pe.wait_ge(S["turn_v"], l * N_TURN + turn_no("C", n, 2) + 1)
                            if n == 0:
                                pe.wait_ge(S["yb_v"], l * B_HEADS + 4)
                                pe.wait_ge(S["unit_s"], l * N_UNITS + GATE0)
                            else:
                                pe.wait_ge(S["y_s"], l * 8 + 4 + n)
                            m = n % 2
                            for g in range(C_GROUPS):
                                hd = g * C_HEADS + n
                                for kt in range(TT):
                                    last = pe.matmul(o[m * DH:m * DH + DH, 0:T], v_of["C"][:, kt, hd * DH:hd * DH + DH],
                                                     probT[:, g, kt, :], start=(g == 0 and kt == 0),
                                                     stop=(g == C_GROUPS - 1 and kt == TT - 1))
                        last.then_inc(S["pv_pe"], 1)
                    elif kind == "ms":
                        o = bank[7 if n % 2 == 0 else 4]
                        pe.wait_ge(S["msq_s"], l * B_HEADS + n + 1)
                        pe.matmul(o[:, T:2 * T], msq[:, :], root[:, n % 2, :], start=True, stop=True,
                                  skip_group_check=True).then_inc(S["ms_pe"], 1)
                    elif kind == "branch":
                        w_at = AT[{"A": "pa", "B": "pb", "C": "pc"}[br], 0]
                        kk = 2 if br == "C" else 4
                        w = ring_view(w_at % RING, kk, D)
                        if n % 4 == 0:
                            arrived(w_at, l)
                        if n == 0:
                            pe.wait_ge(S["unit_s"], l * N_UNITS + GATE0)
                            pe.wait_ge(S["y_s"], l * 8 + 4)
                        if n == 4:
                            pe.wait_ge(S["yb_v"], l * B_HEADS + 4)
                        if n == 8:
                            pe.wait_ge(S["y_s"], l * 8 + 8)
                        if n > 0:
                            pe.wait_ge(S["mix_v"], l * 12 + n)
                        for c2 in range(2):
                            c = 2 * (n % 4) + c2
                            for k in range(kk):
                                last = pe.matmul(bank[0][:, c2 * T:c2 * T + T], w[:, k, c * P:c * P + P],
                                                 yT[:, y_at[br] + k, :], start=(k == 0), stop=(k == kk - 1))
                        last.then_inc(S["branch_pe"], 1)
                    elif kind == "out":
                        arrived(AT["wo", n], l)
                        w = ring_view(AT["wo", n] % RING, KD, 256)
                        if n == 0:
                            pe.wait_ge(S["mix_p"], l * 8 + 8)
                            pe.wait_ge(S["mix_v"], l * 12 + 12)
                        if n == 1:
                            pe.wait_ge(S["unit_s"], l * N_UNITS + N_UNITS)
                        if n >= 2:
                            pe.wait_ge(S["h_v"], l * 4 + n - 1)
                        for tt in range(TT):
                            for k in range(KD):
                                last = pe.matmul(bank[n % 2][:, tt * 256:tt * 256 + 256], mT[:, k, tt * P:tt * P + P],
                                                 w[:, k, :], start=(k == 0), stop=(k == KD - 1))
                        last.then_inc(S["out_pe"], 1)

                turn_x(l, 1)
                pe.wait_ge(S["xnT_v"], l * 4 + 4)
                pe.wait_ge(S["xnT_s"], l * 8 + 8)
                pe.wait_ge(S["cur_v"], l + 1)
                for tt in range(TT):
                    for k in range(KD):
                        last = pe.matmul(bank[4][:, tt * 20:tt * 20 + 20], xnT3[:, k, tt * P:tt * P + P],
                                         wr[:, k * 20:k * 20 + 20], start=(k == 0), stop=(k == KD - 1))
                last.then_inc(S["logit_pe"], 1)
                pe.wait_ge(S["asg_v"], l + 1)
                pe.matmul(bank[5][:, 0:16], tri, asg[:, 0, :], start=True, stop=True)
                pe.matmul(bank[5][:, 16:32], oneb, asg[:, 0, :], start=True, stop=False, skip_group_check=True)
                pe.matmul(bank[5][:, 16:32], tri, asg[:, 1, :], start=False, stop=True, skip_group_check=True)
                pe.matmul(bank[5][:, 32:48], oneb, asg[:, 0, :], start=True, stop=False, skip_group_check=True)
                pe.matmul(bank[5][:, 32:48], oneb, asg[:, 1, :], start=False, stop=True,
                          skip_group_check=True).then_inc(S["rank_pe"], 1)

                def gather(r, first=False):
                    pe.wait_ge(S["m_sel_v"], r + 1)
                    if not first:
                        pe.wait_ge(S["m_xgT_v"], r * 2)
                    for dh in range(2):
                        for tt in range(TT):
                            last = pe.matmul(bank[dh][:, :], sel[:, tt, :], xh3[:, tt, dh * 512:dh * 512 + 512],
                                             start=(tt == 0), stop=(tt == TT - 1))
                        last.then_inc(S["m_gather"], 1)

                def turn_rows(r):
                    for b in range(2):
                        if b == 0:
                            pe.wait_ge(S["m_xg_s"], r + 1)
                        else:
                            pe.wait_ge(S["m_xg_v"], r + 1)
                        for c in range(4 * b, 4 * b + 4):
                            last = pe.transpose(bank[b][:, (c % 4) * P:(c % 4) * P + P], xg[:, c * P:c * P + P], ident)
                        last.then_inc(S["m_xt"], 1)

                def landed_unit(which, r, l):
                    for i in range(2):
                        pe.wait_ge(landed[2 * which + i], ((l + 1) * ROUNDS_1 + r + 1) * 16)

                def hidden(r, l, pair, first=False):
                    pe.wait_ge(S["m_xgT_v"], r * 2 + 2)
                    if first:
                        pe.wait_ge(S["pos_v"], l + 1)
                    else:
                        pe.wait_ge(S["m_hid_v"], r)
                    for which in range(2):
                        landed_unit(which, r, l)
                        o = bank[4 + which]
                        if pair:
                            w = [ring_view(2 * which + i, KD, F_EXP) for i in range(2)]
                            for k in range(KD):
                                for i in range(2):
                                    last = pe.matmul(o[i * CAP:i * CAP + CAP, :], xgT[:, k, i * CAP:i * CAP + CAP],
                                                     w[i][:, k, :], start=(k == 0), stop=(k == KD - 1))
                        else:
                            w = [ring_view(2 * which + i, KD // 2, F_EXP) for i in range(2)]
                            for k in range(KD):
                                last = pe.matmul(o[:, :], xgT[:, k, :], w[k // 4][:, k % 4, :],
                                                 start=(k == 0), stop=(k == KD - 1))
                        last.then_inc(S["m_h"], 1)

                def turn_hidden(r, first=False):
                    pe.wait_ge(S["m_hid_v"], r + 1)
                    if not first:
                        pe.wait_ge(S["m_add_v"], r * 4)
                    for f in range(KF):
                        last = pe.transpose(bank[2][:, f * P:f * P + P], hid[:, f * P:f * P + P], ident)
                    last.then_inc(S["m_ht"], 1)
                    pe.wait_ge(S["m_selg_v"], r + 1)
                    for tt in range(TT):
                        last = pe.transpose(bank[3][:, tt * P:tt * P + P], selg[:, tt, :], ident)
                    last.then_inc(S["m_st"], 1)

                def expert_out(r, l, pair, first=False):
                    landed_unit(2, r, l)
                    pe.wait_ge(S["m_hT_s"], r + 1)
                    if not first:
                        pe.wait_ge(S["m_y_s"], r)
                        pe.wait_ge(S["m_y_v"], r)
                    for dh in range(2):
                        for f in range(KF):
                            if pair:
                                for i in range(2):
                                    last = pe.matmul(bank[6 + dh][i * CAP:i * CAP + CAP, :], hT[:, f, i * CAP:i * CAP + CAP],
                                                     ring_view(4 + i, KF, D)[:, f, dh * 512:dh * 512 + 512],
                                                     start=(f == 0), stop=(f == KF - 1))
                            else:
                                last = pe.matmul(bank[6 + dh][:, :], hT[:, f, :],
                                                 ring_view(4 + f // 2, KF // 2, D)[:, f % 2, dh * 512:dh * 512 + 512],
                                                 start=(f == 0), stop=(f == KF - 1))
                        last.then_inc(S["m_y"], 1)

                def scatter(r):
                    pe.wait_ge(S["m_selT_s"], r + 1)
                    for dh in range(2):
                        pe.wait_ge(S["m_y_v" if dh else "m_y_s"], r + 1)
                        for tt in range(TT):
                            if dh:
                                pe.wait_ge(S["m_add_v"], r * 4 + tt + 1)
                            pe.matmul(bank[2 + tt][:, :], selT[:, tt * P:tt * P + P], y_e[:, dh * 512:dh * 512 + 512],
                                      start=True, stop=True).then_inc(S["m_sc"], 1)

                def unit(r, l, more, first=False):
                    hidden(r, l, True, first)
                    if more:
                        gather(r + 1)
                    turn_hidden(r, first)
                    expert_out(r, l, True, first)
                    if more:
                        turn_rows(r + 1)
                    scatter(r)

                r = pe.snap(units)
                gather(r, first=True)
                turn_rows(r)
                unit(r, l, True, first=True)
                pe.reg_add(units, units, 1)
                with pe.Fori(1, PAIRS - 1):
                    r = pe.snap(units)
                    unit(r, l, True)
                    pe.reg_add(units, units, 1)
                r = pe.snap(units)
                unit(r, l, False)
                pe.reg_add(units, units, 1)
                pe.wait_ge(S["over_v"], l + 1)
                pe.sem_inc(S["list_seen"], 1)
                n_over = pe.value_load(nexp[0:1, 0:1], min_val=0, max_val=N_OVER)
                with pe.If(n_over > 0):
                    with pe.Fori(0, n_over):
                        r = pe.snap(units)
                        gather(r)
                        turn_rows(r)
                        hidden(r, l, False)
                        turn_hidden(r)
                        expert_out(r, l, False)
                        scatter(r)
                        pe.reg_add(units, units, 1)

        @block.scalar
        def _(act):
            units = act.alloc_register("act_units")
            act.reg_mov(units, 0)

            def squares(l, which, n_done):
                for tt in range(TT):
                    last = nc.scalar.activation(zone_p[:, tt * D:tt * D + D], h3[:, tt, :], ACT.Square,
                                                accum_out=ss[:, tt:tt + 1])
                last.then_inc(S["sq"], 1)
                act.wait_ge(S["sq"], n_done + 1)
                nc.scalar.activation(std, ss, ACT.Sqrt, bias=eps1, scale=1.0 / D).then_inc(S["std_s"], 1)

            def xnT_half(l, which):
                if which == 0:
                    act.wait_ge(S["cur_v"], l + 1)
                for b in (1, 3):
                    act.wait_ge(S["turned"], l * 8 + which * 4 + b + 1)
                    for c in (2 * b, 2 * b + 1):
                        nc.scalar.activation(xnT3[:, c, :], bank[b][:, (c % 2) * T:(c % 2) * T + T], ACT.Copy,
                                             scale=gain[:, which, c:c + 1]).then_inc(S["xnT_s"], 1)

            act.wait_ge(S["x_in"], 16)
            act.wait_ge(S["setup_v"], 4)
            act.wait_ge(S["lam_v"], 1)
            nc.scalar.activation(lam_e, lam2, ACT.Exp).then_inc(S["lam_s"], 1)
            with act.Fori(0, DEPTH) as l:
                squares(l, 0, l * 2)
                xnT_half(l, 0)
                for kind, br, n in TIMELINE:
                    if kind == "unit":
                        _, role, i, b, t0 = UNITS[n]
                        o = bank[1] if role == "gate" else bank[n % 2]
                        act.wait_ge(S["unit_pe"], l * N_UNITS + n + 1)
                        if role == "gate":
                            g = i
                            if g == 0:
                                act.wait_ge(S["rope_v"], l * len(ROPE) + 10)
                            if g >= 2:
                                act.wait_ge(S["mix_v"], l * 12 + g - 1)
                            if g - 2 >= 4:
                                act.wait_ge(S["mix_p"], l * 8 + g - 2 - 4 + 1)
                            nc.scalar.activation(pre[:, g % 2, :], o[:, :], ACT.Sigmoid).then_inc(S["unit_s"], 1)
                        elif br == "A" and role == "q":
                            o2 = o[:, :].rearrange("p (i t) -> p i t", i=2)
                            nc.scalar.activation(q_of["A"][0:64, 2 * i:2 * i + 2, 0, :], o2[0:64], ACT.Copy)
                            nc.scalar.activation(q_of["A"][64:128, 2 * i:2 * i + 2, 1, :], o2[64:128],
                                                 ACT.Copy).then_inc(S["unit_s"], 1)
                        elif br == "A" and role == "k":
                            nc.scalar.activation(zone_k1[:, 512 * i:512 * i + 512], o[:, :], ACT.Copy).then_inc(S["unit_s"], 1)
                        elif role in "qk":
                            j = ROPE.index(n)
                            if j >= 2:
                                act.wait_ge(S["rope_v"], l * len(ROPE) + j - 1)
                            nc.scalar.activation(pre[:, n % 2, :], o[:, :], ACT.Copy).then_inc(S["unit_s"], 1)
                        elif role == "v":
                            if br == "C" and i == 0:
                                act.wait_ge(S["scoreA_v"], l * A_HEADS + A_HEADS)
                            nc.scalar.activation(v_of[br][:, i, 0:512], o[:, :], ACT.Copy).then_inc(S["unit_s"], 1)
                        else:
                            nc.scalar.activation(v_of["C"][:, :, 512:768], o[:, :].rearrange("p (t n) -> p t n", t=TT),
                                                 ACT.Copy).then_inc(S["unit_s"], 1)
                    elif kind == "score":
                        for part in range({"A": 1, "B": 2, "C": 3}[br]):
                            no = score_no(br, n, part)
                            act.wait_ge(S["max_v"], l * N_MAX + max_no(br, n, part) + 1)
                            if br == "A":
                                for tt in range(TT):
                                    last = nc.scalar.activation(prob[:, n % 4, tt, :], prob[:, n % 4, tt, :], ACT.Exp,
                                                                bias=nmx[:, n % 4, tt:tt + 1],
                                                                accum_out=psum_[:, n % 4, tt:tt + 1])
                            else:
                                s = 2 * (n % 2) + part if br == "B" else part
                                if br == "B":
                                    m = turn_no("A", 4 + s) if n < 2 else turn_no("B", n - 2)
                                    act.wait_ge(S["turn_pe"], l * N_TURN + m + 1)
                                elif n == 0:
                                    act.wait_ge(S["turn_pe"], l * N_TURN + turn_no("B", 3) + 1)
                                else:
                                    act.wait_ge(S["turn_pe"], l * N_TURN + turn_no("C", n - 1, part) + 1)
                                o = bank[2 + part]
                                for tt in range(TT):
                                    bias = nmx[:, s, tt:tt + 1] if br == "B" else nmx[:, n % 4, tt:tt + 1]
                                    acc = psum_[:, s, tt:tt + 1] if br == "B" else psc[:, tt, part:part + 1]
                                    last = nc.scalar.activation(prob[:, s, tt, :], o[:, tt * T:tt * T + T], ACT.Exp,
                                                                bias=bias, scale=SCALE, accum_out=acc)
                            last.then_inc(S["exp_s"], 1)
                    elif kind == "pv":
                        act.wait_ge(S["pv_pe"], l * 12 + pv_no(br, n) + 1)
                        if br == "A":
                            nc.scalar.activation(yT[:, n, :], bank[7][:, 0:T], ACT.Copy).then_inc(S["y_s"], 1)
                        elif br == "C":
                            m = n % 2
                            nc.scalar.activation(yT[m * DH:m * DH + DH, 8 + n // 2, :], bank[7][m * DH:m * DH + DH, 0:T],
                                                 ACT.Copy).then_inc(S["y_s"], 1)
                        else:
                            if n >= 2:
                                act.wait_ge(S["yb_v"], l * B_HEADS + n - 1)
                            nc.scalar.activation(root[:, n % 2, :], bank[7 if n % 2 == 0 else 4][:, 0:T],
                                                 ACT.Square).then_inc(S["msq_s"], 1)
                    elif kind == "ms":
                        act.wait_ge(S["ms_pe"], l * B_HEADS + n + 1)
                        nc.scalar.activation(root[:, n % 2, :], bank[7 if n % 2 == 0 else 4][:, T:2 * T], ACT.Sqrt,
                                             bias=eps2).then_inc(S["std_b"], 1)

                act.wait_ge(S["h_v"], l * 4 + 4)
                squares(l, 1, l * 2 + 1)
                xnT_half(l, 1)
                act.wait_ge(S["rd_v"], l * 2 + 1)
                nc.scalar.activation(g4b, g4a, ACT.Exp).then_inc(S["rexp_s"], 1)
                act.wait_ge(S["rd_v"], l * 2 + 2)
                nc.scalar.activation(s2[3], s2[2], ACT.Exp).then_inc(S["rexp_s"], 1)

                def rows_out(r):
                    act.wait_ge(S["m_gather"], r * 2 + 1)
                    nc.scalar.activation(xg[:, 0:512], bank[0][:, :], ACT.Copy).then_inc(S["m_xg_s"], 1)

                def gate(r):
                    act.wait_ge(S["m_h"], r * 2 + 1)
                    nc.scalar.activation(sig, bank[4][:, :], ACT.Sigmoid).then_inc(S["m_sig_s"], 1)

                def turned_out(r):
                    act.wait_ge(S["m_ht"], r + 1)
                    nc.scalar.activation(zone_t[:, D:D + 512], bank[2][:, :], ACT.Copy).then_inc(S["m_hT_s"], 1)
                    act.wait_ge(S["m_st"], r + 1)
                    nc.scalar.activation(selT, bank[3][:, 0:T], ACT.Copy).then_inc(S["m_selT_s"], 1)

                def y_out(r):
                    act.wait_ge(S["m_y"], r * 2 + 1)
                    nc.scalar.activation(y_e[:, 0:512], bank[6][:, :], ACT.Copy).then_inc(S["m_y_s"], 1)

                def unit(r, more):
                    gate(r)
                    if more:
                        rows_out(r + 1)
                    turned_out(r)
                    y_out(r)

                rows_out(act.snap(units))
                with act.Fori(0, PAIRS - 1):
                    unit(act.snap(units), True)
                    act.reg_add(units, units, 1)
                unit(act.snap(units), False)
                act.reg_add(units, units, 1)
                act.wait_ge(S["over_v"], l + 1)
                act.sem_inc(S["list_seen"], 1)
                n_over = act.value_load(nexp[0:1, 0:1], min_val=0, max_val=N_OVER)
                with act.If(n_over > 0):
                    with act.Fori(0, n_over):
                        r = act.snap(units)
                        rows_out(r)
                        unit(r, False)
                        act.reg_add(units, units, 1)
                act.wait_ge(S["m_add_v"], act.snap(units) * 4)

            squares(0, 0, DEPTH * 2)
            act.wait_ge(S["final_v"], 1)
            act.dma_start(out[0].rearrange("(t p) d -> p t d", p=P), xh3).then_inc(S["out_done"], 16)
            act.wait_ge(S["out_done"], 16)

        @block.vector
        def _(dve):
            units = dve.alloc_register("dve_units")
            steps = dve.alloc_register("dve_steps")
            dve.reg_mov(units, 0)
            dve.reg_mov(steps, 0)
            link, base = [0], [0]

            def chain(ins):
                link[0] += 1
                ins.then_inc(S["vstep"], 1)
                dve.wait_ge(S["vstep"], base[0] + link[0])

            def begin():
                base[0] = dve.snap(steps)

            def chained():
                if link[0]:
                    dve.reg_add(steps, steps, link[0])
                link[0] = 0

            V = nc.vector
            V.memset(msq[:, :], 1.0 / P).then_inc(S["setup_v"], 1)
            V.memset(zero32, 0.0).then_inc(S["setup_v"], 1)
            V.memset(eps1, NORM_EPS).then_inc(S["setup_v"], 1)
            V.memset(eps2, SUBLN_EPS).then_inc(S["setup_v"], 1)
            begin()
            dve.wait_ge(S["small_in"], DEPTH * 11 * 16)
            dve.wait_ge(S["consts_in"], 32)
            linit = cf[:, C_LINIT:C_LINIT + 2 * DEPTH].rearrange("p (l n) -> p l n", n=2)
            chain(V.tensor_tensor(lam_pr, lam_in[:, :, 0:2, :], lam_in[:, :, 2:4, :], ALU.mult))
            V.tensor_reduce(lam2, lam_pr, AX_X, ALU.add).then_inc(S["lam_v"], 1)
            dve.wait_ge(S["lam_s"], 1)
            lam_t = tab3[:, :, N_LAM:N_LAM + 1]
            chain(V.tensor_tensor(lam_t, lam_e[:, :, 0:1], lam_e[:, :, 1:2], ALU.subtract))
            chain(V.tensor_tensor(lam_t, lam_t, linit[:, :, 0:1], ALU.add))
            chain(V.tensor_tensor(tab3[:, :, N_SUBG:N_SUBG + 1], tab3[:, :, N_SUBG:N_SUBG + 1], linit[:, :, 1:2], ALU.mult))
            chained()

            def bc(ap, shape):
                return ap.broadcast_to(shape)

            def normalise(which, n_std):
                dve.wait_ge(S["std_s"], n_std)
                chain(V.reciprocal(rstd, std))
                for tt in range(TT):
                    V.tensor_scalar(xh3[:, tt, :], h3[:, tt, :], rstd[:, tt:tt + 1], None, ALU.mult).then_inc(S["xh_v"], 1)

            def xnT_half(l, which):
                for b in (0, 2):
                    dve.wait_ge(S["turned"], l * 8 + which * 4 + b + 1)
                    V.tensor_tensor(xnT3[:, 2 * b:2 * b + 2, :], bank[b][:, :].rearrange("p (c t) -> p c t", c=2),
                                    bc(gain[:, which, 2 * b:2 * b + 2].unsqueeze(2), [P, 2, T]),
                                    ALU.mult).then_inc(S["xnT_v"], 1)

            with dve.Fori(0, DEPTH) as l:
                begin()
                V.tensor_copy(cur[:, :], tab[:, bass.ds(l * N_TAB, N_TAB)]).then_inc(S["cur_v"], 1)
                normalise(0, l * 2 + 1)
                dve.wait_ge(S["cur_v"], l + 1)
                xnT_half(l, 0)

                for kind, br, n in TIMELINE:
                    if kind == "swap":
                        i = ROPE.index(n)
                        b_, role, pr, _, _ = UNITS[n]
                        dve.wait_ge(S["swap_pe"], l * len(ROPE) + i + 1)
                        dve.wait_ge(S["cos_p"], l * len(ROPE) + i + 1)
                        o2 = bank[6][:, :].rearrange("p (i t) -> p i t", i=2)
                        x2 = pre[:, n % 2, :].rearrange("p (i t) -> p i t", i=2)
                        c2 = zone_c[:, :].rearrange("p (i t) -> p i t", i=2)
                        chain(V.tensor_tensor(x2, o2, sin2, ALU.mult))
                        if role == "q":
                            V.tensor_tensor(q_of[b_][0:64, 2 * pr:2 * pr + 2, 0, :], x2[0:64], c2[0:64], ALU.add)
                            V.tensor_tensor(q_of[b_][64:128, 2 * pr:2 * pr + 2, 1, :], x2[64:128], c2[64:128],
                                            ALU.add).then_inc(S["rope_v"], 1)
                        else:
                            V.tensor_tensor(k_of[b_][:, 2 * pr:2 * pr + 2, :], x2, c2, ALU.add).then_inc(S["rope_v"], 1)
                    elif kind == "score" and br == "A":
                        s = n % 4
                        if n % 2 == 0:
                            dve.wait_ge(S["bias_p"], l * 4 + n // 2 + 1)
                        dve.wait_ge(S["score_pe"], l * N_SCORE + n + 1)
                        if n >= 4:
                            dve.wait_ge(S["turn_pe"], l * N_TURN + n - 3)
                        V.scalar_tensor_tensor(prob[:, s, :, :].rearrange("p t k -> p (t k)"), bank[2 + n % 2][:, :], SCALE,
                                               biasA[:, (n // 2) % 2, n % 2, :, :].rearrange("p t k -> p (t k)"),
                                               ALU.mult, ALU.add).then_inc(S["scoreA_v"], 1)
                        dve.wait_ge(S["scoreA_v"], l * A_HEADS + n + 1)
                        V.tensor_reduce(nmx[:, s, :], prob[:, s, :, :], AX_X, ALU.max, negate=True).then_inc(S["max_v"], 1)
                    elif kind == "score":
                        for part in range({"B": 2, "C": 3}[br]):
                            dve.wait_ge(S["score_pe"], l * N_SCORE + score_no(br, n, part) + 1)
                            s = 2 * (n % 2) + part if br == "B" else n % 4
                            o = bank[2 + part][:, :].rearrange("p (t k) -> p t k", t=TT)
                            if br == "B":
                                chain(V.tensor_reduce(raw[:, s, :], o, AX_X, ALU.max, negate=True))
                                V.tensor_scalar(nmx[:, s, :], raw[:, s, :], SCALE, None, ALU.mult).then_inc(S["max_v"], 1)
                            else:
                                chain(V.tensor_reduce(mxc[:, :, part:part + 1], o, AX_X, ALU.max))
                        if br == "C":
                            chain(V.tensor_reduce(raw[:, s, :], mxc, AX_X, ALU.max, negate=True))
                            V.tensor_scalar(nmx[:, s, :], raw[:, s, :], SCALE, None, ALU.mult).then_inc(S["max_v"], 1)
                    elif kind == "soft":
                        for b_, m in [(br, n)]:
                            if b_ == "A":
                                s = m % 4
                                dve.wait_ge(S["exp_s"], l * N_SCORE + m + 1)
                                chain(V.reciprocal(rin[:, s, :], psum_[:, s, :]))
                                for tt in range(TT):
                                    last = V.tensor_scalar(prob[:, s, tt, :], prob[:, s, tt, :], rin[:, s, tt:tt + 1],
                                                           None, ALU.mult)
                                last.then_inc(S["prob_v"], 1)
                            elif b_ == "B":
                                s = 2 * (m % 2)
                                dve.wait_ge(S["exp_s"], l * N_SCORE + score_no("B", m, 1) + 1)
                                chain(V.reciprocal(rin[:, s:s + 2, :], psum_[:, s:s + 2, :]))
                                chain(V.tensor_scalar(rin[:, s + 1, :], rin[:, s + 1, :], lam, None, ALU.mult))
                                for tt in range(TT):
                                    chain(V.tensor_scalar(prob[:, s + 1, tt, :], prob[:, s + 1, tt, :],
                                                          rin[:, s + 1, tt:tt + 1], None, ALU.mult))
                                for tt in range(TT):
                                    last = V.scalar_tensor_tensor(prob[:, s, tt, :], prob[:, s, tt, :],
                                                                  rin[:, s, tt:tt + 1], prob[:, s + 1, tt, :],
                                                                  ALU.mult, ALU.subtract)
                                last.then_inc(S["prob_v"], 1)
                            else:
                                dve.wait_ge(S["exp_s"], l * N_SCORE + score_no("C", m, 2) + 1)
                                chain(V.tensor_reduce(s2[1], psc, AX_X, ALU.add))
                                chain(V.reciprocal(rin[:, m % 4, :], s2[1]))
                                for g in range(C_GROUPS):
                                    for tt in range(TT):
                                        last = V.tensor_scalar(prob[:, g, tt, :], prob[:, g, tt, :],
                                                               rin[:, m % 4, tt:tt + 1], None, ALU.mult)
                                    last.then_inc(S["prob_v"], 1)
                    elif kind == "turn":
                        for part in range(C_GROUPS if br == "C" else 1):
                            no = turn_no(br, n, part)
                            o = {"A": bank[4 + n % 2], "B": bank[5], "C": bank[5 + part % 2]}[br]
                            s = part if br == "C" else n % 4
                            dve.wait_ge(S["turn_pe"], l * N_TURN + no + 1)
                            if br == "A" and n >= 4:
                                dve.wait_ge(S["pv_pe"], l * 12 + (n - 4) // 2 + 1)
                            elif br == "B":
                                dve.wait_ge(S["pv_pe"], l * 12 + 4)
                            elif br == "C":
                                dve.wait_ge(S["pv_pe"], l * 12 + 8 + n)
                            V.tensor_copy(probT[:, s, :, :].rearrange("p k t -> p (k t)"), o[:, :]).then_inc(S["turn_v"], 1)
                    elif kind == "ms":
                        o = bank[7 if n % 2 == 0 else 4]
                        dve.wait_ge(S["std_b"], l * B_HEADS + n + 1)
                        chain(V.reciprocal(root[:, n % 2, :], root[:, n % 2, :]))
                        V.scalar_tensor_tensor(yT[:, 4 + n, :], o[:, 0:T], subg, root[:, n % 2, :], ALU.mult,
                                               ALU.mult).then_inc(S["yb_v"], 1)
                    elif kind == "branch":
                        dve.wait_ge(S["branch_pe"], l * 12 + n + 1)
                        dve.wait_ge(S["unit_s"], l * N_UNITS + GATE0 + n + 1)
                        dst = xh[:, 512 * n:512 * n + 512] if br == "A" else pre[:, n % 2, :]
                        V.tensor_tensor(dst, bank[0][:, :], pre[:, n % 2, :], ALU.mult).then_inc(S["mix_v"], 1)
                    elif kind == "out":
                        dve.wait_ge(S["out_pe"], l * 4 + n + 1)
                        hs = h3[:, :, 256 * n:256 * n + 256]
                        V.tensor_tensor(hs, bank[n % 2][:, :].rearrange("p (t d) -> p t d", t=TT), hs,
                                        ALU.add).then_inc(S["h_v"], 1)

                normalise(1, l * 2 + 2)
                xnT_half(l, 1)
                dve.wait_ge(S["logit_pe"], l + 1)
                chain(V.tensor_tensor(lg, bank[4][:, 0:40].rearrange("p (t e) -> p t e", t=TT),
                                      bc(rb.unsqueeze(1), [P, TT, 20]), ALU.add))
                w16 = bc(cf[:, C_W16:C_W16 + 16].unsqueeze(1), [P, TT, 16])
                w4 = bc(cf[:, C_W16:C_W16 + 4].unsqueeze(1), [P, TT, 4])
                col = lambda a, n: bc(a.unsqueeze(2), [P, TT, n])
                lg4, lg16 = lg[:, :, 0:4], lg[:, :, 4:20]
                chain(V.tensor_reduce(s2[4], lg4, AX_X, ALU.max))
                V.tensor_tensor(g4a, lg4, col(s2[4], 4), ALU.subtract).then_inc(S["rd_v"], 1)
                chain(V.tensor_tensor(goh, lg4, col(s2[4], 4), ALU.is_equal))
                chain(V.tensor_tensor(goh, goh, w4, ALU.mult))
                chain(V.tensor_reduce(s2[5], goh, AX_X, ALU.max))
                chain(V.tensor_tensor(goh, goh, col(s2[5], 4), ALU.is_equal))
                chain(V.tensor_scalar(goh, goh, -NEG, NEG, ALU.mult, ALU.add))
                chain(V.tensor_tensor(e16[0].rearrange("p t (g e) -> p t g e", g=N_GRP),
                                      lg16.rearrange("p t (g e) -> p t g e", g=N_GRP),
                                      goh.unsqueeze(3).broadcast_to([P, TT, N_GRP, PER_GRP]), ALU.add))

                def first_max(dst, value, src):
                    chain(V.tensor_reduce(value, src, AX_X, ALU.max))
                    chain(V.tensor_tensor(dst, src, col(value, 16), ALU.is_equal))
                    chain(V.tensor_tensor(dst, dst, w16, ALU.mult))
                    chain(V.tensor_reduce(s2[5], dst, AX_X, ALU.max))
                    chain(V.tensor_tensor(dst, dst, col(s2[5], 16), ALU.is_equal))

                first_max(e16[1], s2[6], e16[0])
                chain(V.scalar_tensor_tensor(e16[0], e16[1], NEG, e16[0], ALU.mult, ALU.add))
                first_max(e16[2], s2[7], e16[0])
                V.tensor_tensor(asg, e16[1], e16[2], ALU.add).then_inc(S["asg_v"], 1)
                V.tensor_tensor(s2[2], s2[7], s2[6], ALU.subtract).then_inc(S["rd_v"], 1)
                dve.wait_ge(S["rexp_s"], l * 2 + 1)
                chain(V.tensor_reduce(s2[8], g4b, AX_X, ALU.add))
                chain(V.reciprocal(s2[8], s2[8]))
                dve.wait_ge(S["rexp_s"], l * 2 + 2)
                chain(V.tensor_scalar(s2[9], s2[3], 1.0, None, ALU.add))
                chain(V.reciprocal(s2[9], s2[9]))
                chain(V.tensor_tensor(s2[9], s2[9], s2[8], ALU.mult))
                chain(V.tensor_tensor(s2[3], s2[3], s2[9], ALU.mult))
                chain(V.tensor_tensor(gat, e16[1], col(s2[9], 16), ALU.mult))
                chain(V.tensor_tensor(e16[3], e16[2], col(s2[3], 16), ALU.mult))
                chain(V.tensor_tensor(gat, gat, e16[3], ALU.add))
                chain(V.tensor_tensor(e16[4], e16[1], e16[2], ALU.add))
                chain(V.tensor_scalar(e16[4], e16[4], -FAR, FAR, ALU.mult, ALU.add))
                dve.wait_ge(S["rank_pe"], l + 1)
                chain(V.tensor_tensor(pos, bank[5][:, 0:32].rearrange("p (t e) -> p t e", t=TT), e16[4], ALU.add))
                V.tensor_copy(cnt, bank[5][:, 32:48]).then_inc(S["pos_v"], 1)
                dve.wait_ge(S["pos_v"], l + 1)
                chained()
                begin()

                iota = cf[:, C_IOTA:C_IOTA + P]
                iota64 = cf[:, C_IOTA64:C_IOTA64 + CAP]

                def one(a, tt, e):
                    return a[:, tt, e:e + 1] if isinstance(e, int) else a[:, tt, bass.ds(e, 1)]

                def select(r, e0):
                    for i in range(2):
                        for tt in range(TT):
                            last = V.tensor_scalar(sel[:, tt, i * CAP:i * CAP + CAP], iota64,
                                                   one(pos, tt, e0 + i), None, ALU.is_equal)
                    last.then_inc(S["m_sel_v"], 1)

                def select_gated(r, e0):
                    for i in range(2):
                        for tt in range(TT):
                            last = V.tensor_scalar(selg[:, tt, i * CAP:i * CAP + CAP], iota64,
                                                   one(pos, tt, e0 + i), one(gat, tt, e0 + i),
                                                   ALU.is_equal, ALU.mult)
                    last.then_inc(S["m_selg_v"], 1)

                def rows_out(r):
                    dve.wait_ge(S["m_gather"], r * 2 + 2)
                    V.tensor_copy(xg[:, 512:1024], bank[1][:, :]).then_inc(S["m_xg_v"], 1)

                def rows_turned(r):
                    for b in range(2):
                        dve.wait_ge(S["m_xt"], r * 2 + b + 1)
                        V.tensor_tensor(xgT[:, 4 * b:4 * b + 4, :], bank[b][:, :].rearrange("p (c s) -> p c s", c=4),
                                        bc(gain[:, 1, 4 * b:4 * b + 4].unsqueeze(2), [P, 4, P]),
                                        ALU.mult).then_inc(S["m_xgT_v"], 1)

                def hidden(r):
                    dve.wait_ge(S["m_sig_s"], r + 1)
                    chain(V.tensor_tensor(sig, bank[4][:, :], sig, ALU.mult))
                    dve.wait_ge(S["m_h"], r * 2 + 2)
                    V.tensor_tensor(hid, bank[5][:, :], sig, ALU.mult).then_inc(S["m_hid_v"], 1)

                def y_out(r):
                    dve.wait_ge(S["m_y"], r * 2 + 2)
                    V.tensor_copy(y_e[:, 512:1024], bank[7][:, :]).then_inc(S["m_y_v"], 1)

                def add(r):
                    for dh in range(2):
                        for tt in range(TT):
                            dve.wait_ge(S["m_sc"], r * 4 + dh * 2 + tt + 1)
                            hs = h3[:, tt, dh * 512:dh * 512 + 512]
                            V.tensor_tensor(hs, bank[2 + tt][:, :], hs, ALU.add).then_inc(S["m_add_v"], 1)

                def unit(r, p, more):
                    if more:
                        dve.wait_ge(S["m_gather"], r * 2 + 2)
                        select(r + 1, p * 2 + 2)
                    hidden(r)
                    if more:
                        rows_out(r + 1)
                    y_out(r)
                    if more:
                        rows_turned(r + 1)
                        dve.wait_ge(S["m_st"], r + 1)
                        select_gated(r + 1, p * 2 + 2)
                    add(r)
                    chained()

                r = dve.snap(units)
                select(r, 0)
                select_gated(r, 0)
                rows_out(r)
                rows_turned(r)
                thr = cf[:, C_THR:C_THR + 32]
                by2 = lambda a: a.rearrange("p (e c) -> p e c", c=2)
                chain(V.tensor_tensor(by2(exist), bc(cnt.unsqueeze(2), [P, 16, 2]), by2(thr), ALU.is_gt))
                chain(V.tensor_tensor_scan(cum, exist, zero32, 0.0, ALU.add, ALU.add))
                row = lambda a: bc(a.unsqueeze(1), [P, N_OVER, 32])
                jrow = cf[:, C_JROW:C_JROW + N_OVER]
                chain(V.tensor_tensor(over_a, row(cum), bc(jrow.unsqueeze(2), [P, N_OVER, 32]), ALU.is_equal))
                chain(V.tensor_tensor(over_a, over_a, row(exist), ALU.mult))
                for src, dst in ((pos, pos_o), (gat, gat_o)):
                    for tt in range(TT):
                        wide = src[:, tt, :].unsqueeze(1).unsqueeze(3).broadcast_to([P, N_OVER, 16, 2])
                        by4 = lambda a: a.rearrange("p j (e c) -> p j e c", c=2)
                        chain(V.tensor_tensor(by4(over_b), by4(over_a), wide, ALU.mult))
                        chain(V.tensor_reduce(dst[:, tt, :], over_b, AX_X, ALU.add))
                chain(V.tensor_tensor(over_b, over_a, row(thr), ALU.mult))
                chain(V.tensor_reduce(eid_o, over_b, AX_X, ALU.add))
                for tt in range(TT):
                    chain(V.tensor_tensor(pos_o[:, tt, :], pos_o[:, tt, :], eid_o, ALU.subtract))
                chain(V.tensor_tensor(over_b, over_a, row(cf[:, C_EIDX:C_EIDX + 32]), ALU.mult))
                chain(V.tensor_reduce(eid_o, over_b, AX_X, ALU.add))
                chain(V.tensor_copy(nexp[:, 1:1 + N_OVER], eid_o))
                V.tensor_copy(nexp[:, 0:1], cum[:, 31:32]).then_inc(S["over_v"], 1)
                chained()

                with dve.Fori(0, PAIRS - 1) as p:
                    begin()
                    unit(dve.snap(units), p, True)
                    dve.reg_add(units, units, 1)
                begin()
                unit(dve.snap(units), 0, False)
                dve.reg_add(units, units, 1)
                dve.wait_ge(S["over_v"], l + 1)
                dve.sem_inc(S["list_seen"], 1)
                n_over = dve.value_load(nexp[0:1, 0:1], min_val=0, max_val=N_OVER)
                with dve.If(n_over > 0):
                    with dve.Fori(0, n_over) as j:
                        begin()
                        r = dve.snap(units)
                        dve.wait_ge(S["m_st"], r)
                        for tt in range(TT):
                            last = V.tensor_scalar(sel[:, tt, :], iota, pos_o[:, tt, bass.ds(j, 1)], None, ALU.is_equal)
                        last.then_inc(S["m_sel_v"], 1)
                        for tt in range(TT):
                            last = V.tensor_scalar(selg[:, tt, :], iota, pos_o[:, tt, bass.ds(j, 1)],
                                                   gat_o[:, tt, bass.ds(j, 1)], ALU.is_equal, ALU.mult)
                        last.then_inc(S["m_selg_v"], 1)
                        rows_out(r)
                        rows_turned(r)
                        unit(r, 0, False)
                        dve.reg_add(units, units, 1)

            begin()
            dve.wait_ge(S["fin_in"], 16)
            dve.wait_ge(S["std_s"], DEPTH * 2 + 1)
            chain(V.reciprocal(rstd, std))
            for tt in range(TT):
                last = V.scalar_tensor_tensor(xh3[:, tt, :], h3[:, tt, :], rstd[:, tt:tt + 1], fin[:, :], ALU.mult, ALU.mult)
            last.then_inc(S["final_v"], 1)


_INS = ["x", "w_in", "na_rpb", "lam_q1", "lam_k1", "lam_q2", "lam_k2", "diff_subln", "w_pa", "w_pb", "w_pc", "w_o",
        "norm_mix", "norm_ffn", "router_group_w", "router_group_b", "router_expert_w", "router_expert_b",
        "w1", "w3", "w2", "norm_final"]


def kernel(**inputs):
    import concourse.bacc as bacc
    from concourse.bass_utils import run_bass_kernel_spmd

    nc = bacc.Bacc("TRN2", target_bir_lowering=False, num_devices=1)
    arrays = {f"in_{n}": np.ascontiguousarray(inputs[n]) for n in _INS}
    arrays["in_consts"] = constants()
    args = [nc.dram_tensor(n, a.shape, mybir.dt.from_np(a.dtype), kind="ExternalInput").ap() for n, a in arrays.items()]
    out = nc.dram_tensor("out", (1, T, D), F32, kind="ExternalOutput").ap()
    build(nc, *args, out)
    return run_bass_kernel_spmd(nc, [arrays], core_ids=[0]).results[0]["out"]
```

```python
import math
from contextlib import ExitStack

import numpy as np

import concourse.bass as bass
from concourse import mybir

F32 = mybir.dt.float32
F32R = mybir.dt.float32r
BF16 = mybir.dt.bfloat16
I32 = mybir.dt.int32
U32 = mybir.dt.uint32
ALU = mybir.AluOpType
ACT = mybir.ActivationFunctionType
AX_X = mybir.AxisListType.X

P = 128
T = 256
TT = T // P
D = 1024
KD = D // P
DEPTH = 2
DH = 64
GRID_W = 64
A_HEADS = 8
B_HEADS = 4
C_GROUPS = 3
C_HEADS = 4
SCALE = DH ** -0.5
NEG = -1e30
NORM_EPS = 1e-6
SUBLN_EPS = 1e-5
N_EXP = 16
N_GRP = 4
PER_GRP = N_EXP // N_GRP
F_EXP = D // 2
KF = F_EXP // P
CAP = 64
FAR = 1000.0
PAIRS = N_EXP // 2
N_OVER = 8
SLOT = 4096
RING = 6
RPB = 15 * 31
RPB_C = 31
N_GAIN, N_SUBG, N_LAM, N_RB, N_WR, N_VEC, N_CUR = 0, 8, 9, 10, 30, 190, 194
N_LOADS = 10

C_IDENT, C_SWAP, C_COS, C_SIN = 0, 128, 256, 512
C_IOTA, C_W16, C_THR, C_EIDX, C_JROW, C_LINIT = 768, 896, 912, 944, 976, 984
C_KEEP = 988
C_TRI, C_IDB, C_ONE, C_MASKA = C_KEEP, C_KEEP + 128, C_KEEP + 256, C_KEEP + 384
C_MASKC = C_MASKA + 512
C_ALL = C_MASKC + C_GROUPS * TT * T
NB16 = C_ALL - C_KEEP


def constants():
    c = np.zeros((P, C_ALL), np.float32)
    p = np.arange(P)
    c[:, C_IDENT:C_IDENT + P] = np.eye(P)
    half = 8
    inv = (1.0 / (np.float32(500000.0) ** (np.arange(0, 16, 2, dtype=np.float32) / np.float32(16)))).astype(np.float32)
    ang = np.arange(T, dtype=np.float32)[:, None] * inv[None, :]
    cos, sin = np.cos(ang).T, np.sin(ang).T
    c[:, C_COS:C_COS + T] = 1.0
    for q in p:
        d = q % DH
        if d < 2 * half:
            partner = q + half if d < half else q - half
            c[partner, C_SWAP + q] = 1.0
            c[q, C_COS:C_COS + T] = cos[d % half]
            c[q, C_SIN:C_SIN + T] = -sin[d] if d < half else sin[d - half]
    tok = np.arange(T)
    col = tok % GRID_W
    first = np.clip(col - 8, 0, GRID_W - 16)
    ok = (col[None, :] >= first[:, None]) & (col[None, :] < first[:, None] + 16)
    mask = lambda ok: np.where(ok, 0.0, NEG).reshape(TT, P, T).transpose(1, 0, 2).reshape(P, TT * T)
    c[:, C_MASKA:C_MASKA + TT * T] = mask(ok)
    c[:, C_IOTA:C_IOTA + P] = np.arange(P)
    c[:, C_W16:C_W16 + 16] = 16 - np.arange(16)
    c[:, C_THR:C_THR + 32] = np.tile([CAP, CAP + P], 16)
    c[:, C_EIDX:C_EIDX + 32] = np.repeat(np.arange(16), 2)
    c[:, C_JROW:C_JROW + N_OVER] = 1 + np.arange(N_OVER)
    for layer in range(DEPTH):
        lam = 0.8 - 0.6 * math.exp(-0.3 * layer)
        c[:, C_LINIT + 2 * layer] = lam
        c[:, C_LINIT + 2 * layer + 1] = 1.0 - lam
    c[:, C_TRI:C_TRI + P] = p[:, None] < p[None, :]
    c[:, C_IDB:C_IDB + P] = np.eye(P)
    c[:, C_ONE:C_ONE + P] = 1.0
    for g, dil in enumerate((1, 4, 16)):
        diff = tok[None, :] - tok[:, None]
        ok = (diff % dil == 0) & (np.abs(diff) <= 64 * dil)
        c[:, C_MASKC + g * TT * T:C_MASKC + (g + 1) * TT * T] = mask(ok)
    return c


ORDER = [("in", b) for b in range(10)] + [("pa", 0), ("in", 10), ("in", 11), ("in", 12), ("pb", 0), ("in", 13),
         ("in", 14), ("pc", 0), ("in", 15), ("in", 16)] + [("wo", s) for s in range(4)]
AT = {w: n for n, w in enumerate(ORDER)}
SLOT_OF = [0, 1, 2, 3, 0, 1, 2, 3, 0, 1, 2, 3, 0, 1, 3, 0, 1, 2, 0, 1, 3, 0, 1, 2]
USES = [SLOT_OF.count(i) for i in range(RING)]
NTH = [SLOT_OF[:n].count(i) for n, i in enumerate(SLOT_OF)]
BEFORE = [max((m for m in range(n) if SLOT_OF[m] == i), default=None) for n, i in enumerate(SLOT_OF)]
LAST_USE = [max((n for n, j in enumerate(SLOT_OF) if j == i), default=None) for i in range(RING)]
assert len(ORDER) == len(SLOT_OF) and USES[4] == USES[5] == 0

UNITS = []
for _br, _b0 in (("A", 0), ("B", 3)):
    for _role, _b in (("q", 0), ("k", 1)):
        UNITS += [(_br, _role, i, _b0 + _b, 2 * i) for i in range(2)]
    UNITS += [(_br, "v", half, _b0 + 2, 0) for half in range(2)]
UNITS += [("C", "q", 0, 6, 0), ("C", "q", 1, 6, 2), ("C", "q", 2, 7, 0),
          ("C", "k", 0, 7, 2), ("C", "k", 1, 8, 0), ("C", "k", 2, 8, 2),
          ("C", "v", 0, 9, 0), ("C", "v", 1, 9, 0), ("C", "v2", 0, 10, 0)]
UNITS += [("ABC"[(g := (4 * b + t - 42) // 2) // 4], "gate", g, b, t)
          for b in range(10, 17) for t in (0, 2) if 4 * b + t >= 42 and 4 * b + t < 66]
GATE0 = UNITS.index(("A", "gate", 0, 10, 2))
N_UNITS = len(UNITS)
ROPE = [u for u, x in enumerate(UNITS) if x[0] in "BC" and x[1] in "qk"]
LAST_UNIT = {b: max(u for u, x in enumerate(UNITS) if x[3] == b) for b in range(17)}


def timeline():
    after = {
        6: [("score", "A", 0), ("score", "A", 1), ("soft", "A", 0), ("soft", "A", 1)],
        7: [("turn", "A", 0), ("score", "A", 2), ("turn", "A", 1), ("score", "A", 3), ("soft", "A", 2), ("soft", "A", 3)],
        8: [("pv", "A", 0), ("turn", "A", 2), ("score", "A", 4), ("turn", "A", 3), ("score", "A", 5), ("soft", "A", 4),
            ("soft", "A", 5)],
        9: [("pv", "A", 1), ("turn", "A", 4), ("score", "A", 6), ("turn", "A", 5), ("score", "A", 7), ("soft", "A", 6),
            ("soft", "A", 7)],
        10: [("pv", "A", 2), ("turn", "A", 6), ("turn", "A", 7)],
        11: [("pv", "A", 3), ("lambda", "B", 0)],
        12: [("score", "B", 0), ("soft", "B", 0)],
        13: [("turn", "B", 0), ("score", "B", 1), ("soft", "B", 1)],
        14: [("pv", "B", 0), ("turn", "B", 1), ("score", "B", 2), ("soft", "B", 2)],
        15: [("ms", "B", 0), ("pv", "B", 1), ("turn", "B", 2), ("score", "B", 3), ("soft", "B", 3)],
        16: [("ms", "B", 1), ("pv", "B", 2), ("turn", "B", 3)],
        17: [("ms", "B", 2), ("pv", "B", 3)],
        18: [("ms", "B", 3)],
        20: [("score", "C", 0), ("soft", "C", 0)],
        GATE0: [("turn", "C", 0)], GATE0 + 1: [("pv", "C", 0), ("score", "C", 1), ("soft", "C", 1)],
        GATE0 + 2: [("turn", "C", 1)], GATE0 + 3: [("pv", "C", 1), ("score", "C", 2), ("soft", "C", 2)],
        GATE0 + 4: [("turn", "C", 2)], GATE0 + 5: [("pv", "C", 2), ("score", "C", 3), ("soft", "C", 3)],
        GATE0 + 6: [("turn", "C", 3)], GATE0 + 7: [("pv", "C", 3)],
    }
    steps = []
    for u, x in enumerate(UNITS):
        steps.append(("unit", x[0], u))
        if u - 1 in ROPE:
            steps.append(("swap", UNITS[u - 1][0], u - 1))
        if x[1] == "gate":
            steps.append(("branch", x[0], x[2]))
        steps += after.get(u, [])
    return steps + [("out", "", s) for s in range(4)]


TIMELINE = timeline()

N_SCORE = A_HEADS + 2 * B_HEADS + C_GROUPS * C_HEADS
N_TURN = A_HEADS + B_HEADS + C_GROUPS * C_HEADS


def score_no(br, n, part=0):
    return {"A": n, "B": A_HEADS + 2 * n + part, "C": A_HEADS + 2 * B_HEADS + C_GROUPS * n + part}[br]


def turn_no(br, n, part=0):
    return {"A": n, "B": A_HEADS + n, "C": A_HEADS + B_HEADS + C_GROUPS * n + part}[br]


def max_no(br, n, part=0):
    return {"A": n, "B": A_HEADS + 2 * n + part, "C": A_HEADS + 2 * B_HEADS + n}[br]


BIAS_IN = 4 * 8 * 16
N_MAX = A_HEADS + 2 * B_HEADS + C_HEADS


def pv_no(br, n):
    return {"A": n, "B": 4 + n, "C": 8 + n}[br]


def build(nc, x, w_in, na_rpb, lam_q1, lam_k1, lam_q2, lam_k2, diff_subln, w_pa, w_pb, w_pc, w_o,
          norm_mix, norm_ffn, router_group_w, router_group_b, router_expert_w, router_expert_b,
          w1, w3, w2, norm_final, consts, out):
    with ExitStack() as ctx:
        def sb(name, cols, dt=F32):
            return ctx.enter_context(nc.sbuf_tensor(name, [P, cols], dt))

        def sem(name):
            return ctx.enter_context(nc.semaphore(name))

        ring = sb("ring", RING * SLOT)
        ring_at = nc.sbuf_base - 4 * RING * SLOT
        w_hi, w_lo = (nc.alloc_sbuf_tensor_at(name, [P, SLOT], F32R, offset=ring_at + 4 * i * SLOT)
                      for i, name in ((4, "w_hi"), (5, "w_lo")))
        h = sb("h", TT * D)
        xh = sb("xh", TT * D)
        xn_hi = sb("xn_hi", KD * T, F32R)
        xn_lo = sb("xn_lo", KD * T, F32R)
        zone_q1 = sb("zone_q1", 6 * 2 * T)
        zone_k1 = sb("zone_k1", 6 * T)
        zone_v1 = sb("zone_v1", TT * 512)
        zone_b = sb("zone_b", 2048)
        zone_q2 = sb("zone_q2", 4 * 2 * T)
        zone_k2 = xh[:, 0:4 * T]
        zone_v2 = xh[:, 4 * T:4 * T + TT * 512]
        zone_y = sb("zone_y", 6 * T)
        zone_p = sb("zone_p", 4 * TT * T)
        zone_t = sb("zone_t", 4 * TT * T)
        zone_s = sb("zone_s", 2 * 512)
        zone_c = sb("zone_c", 512)
        cf = sb("cf", C_KEEP)
        cb = sb("cb", NB16, BF16)
        msq = sb("msq", P)
        gains1 = sb("gains1", DEPTH * KD)
        gain1 = sb("gain1", KD)
        cur = sb("cur", N_CUR)
        sm = sb("sm", 640)
        nexp = sb("nexp", 16, I32)

        h3 = h[:, :].rearrange("p (t d) -> p t d", t=TT)
        xh3 = xh[:, :].rearrange("p (t d) -> p t d", t=TT)
        mT = xh[:, :].rearrange("p (c t) -> p c t", c=KD)
        xn_hi3 = xn_hi[:, :].rearrange("p (c t) -> p c t", c=KD)
        xn_lo3 = xn_lo[:, :].rearrange("p (c t) -> p c t", c=KD)
        xnT3 = zone_q2[:, :].rearrange("p (c t) -> p c t", c=KD)
        q_of = {"A": zone_q1, "B": zone_q2, "C": zone_q1}
        k_of = {"A": zone_k1[:, :], "B": zone_k2, "C": zone_k1[:, :]}
        q_of = {b: z[:, :].rearrange("p (i m t) -> p i m t", m=2, t=T) for b, z in q_of.items()}
        k_of = {b: z.rearrange("p (i t) -> p i t", t=T) for b, z in k_of.items()}
        v_of = {"A": zone_v1[:, :].rearrange("p (t n) -> p t n", t=TT),
                "B": zone_v2.rearrange("p (t n) -> p t n", t=TT),
                "C": zone_b[:, 0:TT * 768].rearrange("p (t n) -> p t n", t=TT)}
        biasA = [z.rearrange("p (h t k) -> p h t k", h=2, t=TT)
                 for z in (zone_b[:, 0:1024], zone_b[:, 1024:2048], zone_v2, zone_b[:, 0:1024])]
        y_of = {"A": zone_y[:, 0:4 * T], "B": zone_v1[:, :], "C": zone_y[:, 4 * T:6 * T]}
        y_of = {b: z.rearrange("p (i t) -> p i t", t=T) for b, z in y_of.items()}
        prob = zone_p[:, :].rearrange("p (s t k) -> p s t k", s=4, t=TT)
        probT = zone_t[:, :].rearrange("p (s k t) -> p s k t", s=4, k=TT)
        gain2 = cur[:, N_GAIN:N_GAIN + KD]
        vec = cur[0:DH, N_VEC:N_VEC + 4]
        subg, lam = cur[:, N_SUBG:N_SUBG + 1], cur[:, N_LAM:N_LAM + 1]
        rb, wr = cur[:, N_RB:N_RB + 20], cur[:, N_WR:N_WR + KD * 20]
        root = zone_y[:, 4 * T:6 * T].rearrange("p (s t) -> p s t", s=2)
        fin = zone_k1[:, 0:D]
        pre = zone_s[:, :].rearrange("p (s n) -> p s n", s=2)
        ident = cf[:, C_IDENT:C_IDENT + P]
        swap = cf[:, C_SWAP:C_SWAP + P]
        cos2 = cf[:, C_COS:C_COS + T].unsqueeze(1).broadcast_to([P, 2, T])
        sin2 = cf[:, C_SIN:C_SIN + T].unsqueeze(1).broadcast_to([P, 2, T])
        bcol = lambda at, n: cb[:, at - C_KEEP:at - C_KEEP + n]
        tri, identb, oneb = bcol(C_TRI, P), bcol(C_IDB, P), bcol(C_ONE, P)
        maskA = bcol(C_MASKA, TT * T)
        maskC = bcol(C_MASKC, C_GROUPS * TT * T).rearrange("p (g t k) -> p g t k", g=C_GROUPS, t=TT)
        xg = zone_p[:, 0:D]
        xgT = zone_p[:, D:2 * D].rearrange("p (c s) -> p c s", c=KD)
        y_e = zone_t[:, 0:D]
        hT = zone_t[:, D:D + 512].rearrange("p (f s) -> p f s", f=KF)
        sig = zone_t[:, D + 512:D + 1024]
        hid = zone_y[:, 0:512]
        selT = zone_y[:, 512:768]
        sel = zone_y[:, 768:1024].rearrange("p (t s) -> p t s", t=TT)
        selg = zone_y[:, 1024:1280].rearrange("p (t s) -> p t s", t=TT)
        over_a = zone_v1[:, 0:256].rearrange("p (j e) -> p j e", j=N_OVER)
        over_b = zone_v1[:, 256:512].rearrange("p (j e) -> p j e", j=N_OVER)

        at = [0]

        def small(n):
            at[0] += n
            return sm[:, at[0] - n:at[0]]

        ss, std, rstd = small(2), small(2), small(2)
        eps1, eps2 = small(1), small(1)
        lam_pr, lam_e = small(2), small(2)
        nmx = small(4 * 2).rearrange("p (s t) -> p s t", s=4)
        raw = small(4 * 2).rearrange("p (s t) -> p s t", s=4)
        mxc = small(2 * 3).rearrange("p (t g) -> p t g", g=3)
        psum_ = small(4 * 2).rearrange("p (s t) -> p s t", s=4)
        psc = small(2 * 3).rearrange("p (t g) -> p t g", g=3)
        rin = small(4 * 2).rearrange("p (s t) -> p s t", s=4)
        lg = small(2 * 20).rearrange("p (t e) -> p t e", t=TT)
        g4a, g4b, goh = (small(8).rearrange("p (t e) -> p t e", t=TT) for _ in range(3))
        s2 = [small(2) for _ in range(12)]
        e16 = [small(32).rearrange("p (t e) -> p t e", t=TT) for _ in range(5)]
        pos, gat = (small(32).rearrange("p (t e) -> p t e", t=TT) for _ in range(2))
        cnt = small(16)
        exist, cum, zero32 = small(32), small(32), small(32)
        pos_o, gat_o = (small(2 * N_OVER).rearrange("p (t j) -> p t j", t=TT) for _ in range(2))
        eid_o = small(N_OVER)
        asg = sb("asg", 32, BF16)[:, :].rearrange("p (t e) -> p t e", t=TT)
        assert at[0] <= 640, at[0]

        copies = nc.dram_tensor("copies", (GRID_W, DEPTH * A_HEADS * RPB), F32).ap()

        bank = [ctx.enter_context(nc.psum_tensor(f"bank{i}", [P, 512], F32)) for i in range(8)]

        names = """cf_in cb_in copies_in setup_v zero_q1 zero_q2 x_in gains_in small_in bias_in fin_in out_done
            lam_v lam_pe lam_s gain1_v final_v
            sq std_s xh_v turned x_hi_s x_lo_v xnT_v xnT_s
            hi_s lo_v v_pe unit_pe unit_s swap_pe cos_p rope_v vstep pstep bias_p
            score_pe scoreA_v max_v exp_s prob_v turn_pe turn_v pv_pe y_s yb_v msq_s ms_pe std_b
            branch_pe mix_v mix_p out_pe h_v
            logit_pe logit_seen rexp_s rd_v asg_v rank_pe pos_v over_v list_seen
            m_sel_v m_selg_v m_gather m_xg_s m_xg_v m_xt m_xgT_v m_h m_sig_s m_hid_v m_ht m_hT_s m_st m_selT_s
            m_y m_y_s m_y_v m_sc m_add_v""".split()
        S = {n: sem(n) for n in names}
        landed = [sem(f"landed{i}") for i in range(RING)]

        def slot(n, cols=SLOT):
            return ring[:, n * SLOT:n * SLOT + cols]

        def ring_view(n, k, cols):
            return slot(n, k * cols).rearrange("p (k n) -> p k n", k=k)

        def weights_of(n):
            _, role, i, b, t0 = UNITS[n]
            w = ring_view(SLOT_OF[AT["in", b]], KD, min(512, 8448 - 512 * b))
            return w[:, 4 * i:4 * i + 4, :] if role == "v" else w[:, :, t0 * P:t0 * P + 256]

        def part_of(parts, n):
            k = 4 if UNITS[n][1] == "v" else KD
            return parts[:, (n % 2) * 2048:(n % 2) * 2048 + 2048].rearrange("p (k n) -> p k n", k=k)

        block = ctx.enter_context(nc.Block())

        @block.sync
        def _(sp):
            units = sp.alloc_register("sp_units")
            sp.reg_mov(units, 0)
            layers = sp.alloc_register("sp_layers")
            sp.reg_mov(layers, 0)

            def load(n, l):
                kind, b = ORDER[n]
                if kind == "in":
                    cols = min(512, 8448 - 512 * b)
                    src = w_in[l, :, 512 * b:512 * b + cols].rearrange("(k p) n -> p k n", p=P)
                    dst = ring_view(SLOT_OF[n], KD, cols)
                elif kind == "wo":
                    src = w_o[l, :, 256 * b:256 * b + 256].rearrange("(k p) n -> p k n", p=P)
                    dst = ring_view(SLOT_OF[n], KD, 256)
                else:
                    w = {"pa": w_pa, "pb": w_pb, "pc": w_pc}[kind]
                    src = w[l].rearrange("(k p) n -> p k n", p=P)
                    dst = ring_view(SLOT_OF[n], w.shape[1] // P, D)
                sp.dma_start(dst, src).then_inc(landed[SLOT_OF[n]], 16)

            def wait_free(n, l):
                kind, b = ORDER[n]
                if kind == "in":
                    sp.wait_ge(S["lo_v"], l * N_UNITS + LAST_UNIT[b] + 1)
                elif kind == "wo":
                    sp.wait_ge(S["out_pe"], l * 4 + b + 1)
                else:
                    sp.wait_ge(S["branch_pe"], l * 12 + {"pa": 4, "pb": 8, "pc": 12}[kind])

            w1_r = w1.rearrange("l e (k p) f -> (l e) p k f", p=P)
            w3_r = w3.rearrange("l e (k p) f -> (l e) p k f", p=P)
            w2_r = w2.rearrange("l e (k p) f -> (l e) p k f", p=P)

            def load_expert(which, item, e):
                src = (w1_r, w3_r, w2_r)[which][bass.ds(e, 1)].rearrange("o p k f -> p (o k) f")
                k, cols = (KF, D) if which == 2 else (KD, F_EXP)
                sp.dma_start(ring_view(2 * which + item, k, cols), src).then_inc(landed[2 * which + item], 16)

            def wait_unit(which, last):
                if which < 2:
                    sp.wait_ge(S["m_h"], last * 2 + 1 + which)
                else:
                    sp.wait_ge(S["m_y"], last * 2 + 2)

            sp.dma_start(h3, x[0].rearrange("(t p) d -> p t d", p=P)).then_inc(S["x_in"], 16)
            sp.dma_start(cf[:, :], consts[:, 0:C_KEEP]).then_inc(S["cf_in"], 16)
            sp.dma_start(gains1[:, :].rearrange("p (l c) -> p l c", l=DEPTH), norm_mix.rearrange("l (c p) -> p l c", p=P),
                         allow_slow_non_contiguous=True).then_inc(S["gains_in"], 16)
            for n in range(4):
                load(n, 0)
            with sp.Fori(0, DEPTH) as l:
                for n in range(4, len(ORDER)):
                    wait_free(BEFORE[n], l)
                    load(n, l)
                sp.wait_ge(S["unit_pe"], l * N_UNITS + N_UNITS)
                for item in range(2):
                    load_expert(2, item, l * N_EXP + item)
                for i in sorted(range(4), key=lambda i: LAST_USE[i]):
                    wait_free(LAST_USE[i], l)
                    load_expert(i // 2, i % 2, l * N_EXP + i % 2)
                with sp.Fori(1, PAIRS) as p:
                    last = sp.snap(units)
                    for which in range(3):
                        wait_unit(which, last)
                        for item in range(2):
                            load_expert(which, item, l * N_EXP + p * 2 + item)
                    sp.reg_add(units, units, 1)
                sp.wait_ge(S["over_v"], l + 1)
                sp.sem_inc(S["list_seen"], 1)
                n_over = sp.value_load(nexp[0:1, 0:1], min_val=0, max_val=N_OVER)
                with sp.If(n_over > 0):
                    with sp.Fori(0, n_over) as j:
                        last = sp.snap(units)
                        e = sp.value_load(nexp[0:1, bass.ds(j + 1, 1)], min_val=0, max_val=N_EXP - 1)
                        for which in range(3):
                            wait_unit(which, last)
                            src = (w1_r, w3_r, w2_r)[which][bass.ds(l * N_EXP + e, 1)].rearrange("o p k f -> p (o k) f")
                            k, cols = (KF, D) if which == 2 else (KD, F_EXP)
                            for part in range(2):
                                sp.dma_start(ring_view(2 * which + part, k // 2, cols),
                                             src[:, part * k // 2:(part + 1) * k // 2, :]).then_inc(
                                                 landed[2 * which + part], 16)
                        sp.reg_add(units, units, 1)
                sp.reg_add(layers, layers, 1)
                with sp.If(l < DEPTH - 1):
                    last = sp.snap(units)
                    following = sp.snap(layers, min_val=1, max_val=DEPTH - 1)
                    for n in range(4):
                        wait_unit(SLOT_OF[n] // 2, last)
                        load(n, following)
                sp.reg_add(units, units, 1)

        @block.gpsimd
        def _(pool):
            pool.dma_start(cb[:, :], consts[:, C_KEEP:C_ALL]).then_inc(S["cb_in"], 16)
            pool.dma_start(copies, na_rpb.rearrange("l h a b -> (l h a b)").partition_broadcast(GRID_W)
                           ).then_inc(S["copies_in"], 16)
            nc.gpsimd.memset(zone_q1[:, :], 0.0).then_inc(S["zero_q1"], 1)
            nc.gpsimd.memset(zone_q2[:, :], 0.0).then_inc(S["zero_q2"], 1)

            def small_loads(l):
                def get(dst, src):
                    pool.dma_start(dst, src, allow_slow_non_contiguous=True).then_inc(S["small_in"], 16)

                def row(a):
                    return a[bass.ds(l, 1), :].rearrange("l n -> (l n)")

                for i, a in enumerate((lam_q1, lam_q2, lam_k1, lam_k2)):
                    get(cur[0:DH, N_VEC + i:N_VEC + i + 1], row(a).unsqueeze(1))
                get(cur[:, N_SUBG:N_SUBG + 1], row(diff_subln).unsqueeze(1))
                get(gain2, row(norm_ffn).rearrange("(c p) -> p c", p=P))
                get(cur[:, N_RB:N_RB + 4], row(router_group_b).partition_broadcast(P))
                get(cur[:, N_RB + 4:N_RB + 20], row(router_expert_b).partition_broadcast(P))
                w = wr.rearrange("p (k e) -> p k e", e=20)
                get(w[:, :, 0:4], router_group_w[bass.ds(l, 1)].rearrange("l (k p) e -> p (l k) e", p=P))
                get(w[:, :, 4:20], router_expert_w[bass.ds(l, 1)].rearrange("l (k p) e -> p (l k) e", p=P))

            def bias_loads(l, pair):
                for hh in range(2):
                    for r in range(4):
                        tt, p0 = r // 2, 64 * (r % 2)
                        at = (2 * pair + hh) * RPB + (7 - r) * RPB_C + 15
                        src = copies[:, bass.ds(l * A_HEADS * RPB + at, 3 * RPB_C + GRID_W)]
                        src = bass.AP(tensor=src.tensor, offset=src.offset,
                                      ap=[[DEPTH * A_HEADS * RPB - 1, GRID_W], [RPB_C, 4], [1, GRID_W]])
                        dst = biasA[pair][p0:p0 + 64, hh, tt, :].rearrange("p (a b) -> p a b", b=GRID_W)
                        pool.dma_start(dst, src).then_inc(S["bias_in"], 16)

            def add_mask(pair):
                b = biasA[pair].rearrange("p h t k -> p h (t k)")
                nc.gpsimd.tensor_tensor(b, b, maskA.unsqueeze(1).broadcast_to([P, 2, TT * T]),
                                        ALU.add).then_inc(S["bias_p"], 1)

            pool.wait_ge(S["copies_in"], 16)
            pool.wait_ge(S["cb_in"], 16)
            pool.wait_ge(S["cf_in"], 16)
            with pool.Fori(0, DEPTH) as l:
                for kind, br, n in TIMELINE:
                    if kind == "unit" and n == 0:
                        pool.wait_ge(S["turned"], l * 8 + 4)
                        for pair in range(3):
                            bias_loads(l, pair)
                        pool.wait_ge(S["bias_in"], l * BIAS_IN + 3 * 8 * 16)
                        for pair in range(3):
                            add_mask(pair)
                        small_loads(l)
                    if kind == "unit" and n == 8:
                        pool.wait_ge(S["scoreA_v"], l * A_HEADS + 2)
                        bias_loads(l, 3)
                    if kind == "unit" and n == 9:
                        pool.wait_ge(S["bias_in"], l * BIAS_IN + BIAS_IN)
                        add_mask(3)
                    if kind == "swap":
                        i = ROPE.index(n)
                        pool.wait_ge(S["unit_s"], l * N_UNITS + n + 1)
                        if i > 0:
                            pool.wait_ge(S["rope_v"], l * len(ROPE) + i)
                        nc.gpsimd.tensor_tensor(zone_c[:, :].rearrange("p (i t) -> p i t", i=2),
                                                pre[:, n % 2, :].rearrange("p (i t) -> p i t", i=2),
                                                cos2, ALU.mult).then_inc(S["cos_p"], 1)
                    if kind == "branch" and br != "A":
                        pool.wait_ge(S["mix_v"], l * 12 + n + 1)
                        if n >= 8:
                            pool.wait_ge(S["mix_p"], l * 8 + n - 7)
                        i = n % 4
                        m = xh[:, 512 * i:512 * i + 512]
                        nc.gpsimd.tensor_tensor(m, m, pre[:, n % 2, :], ALU.add).then_inc(S["mix_p"], 1)
                pool.wait_ge(S["logit_pe"], l + 1)
                pool.sem_inc(S["logit_seen"], 1)
                nc.gpsimd.memset(zone_q2[:, :], 0.0).then_inc(S["zero_q2"], 1)

            pool.wait_ge(S["over_v"], DEPTH)
            pool.dma_start(fin, norm_final[:].partition_broadcast(P)).then_inc(S["fin_in"], 16)

        @block.tensor
        def _(pe):
            units = pe.alloc_register("pe_units")
            pe.reg_mov(units, 0)

            def arrived(n, l, first=None):
                i = SLOT_OF[n]
                pe.wait_ge(landed[i], (l * USES[i] + pe.snap(units) + NTH[n] + 1) * 16)

            def turn_x(l, which):
                pe.wait_ge(S["xh_v"], l * 4 + which * 2 + 2)
                for b in range(4):
                    for c in (2 * b, 2 * b + 1):
                        for tt in range(TT):
                            at = (c % 2) * T + tt * P
                            last = pe.transpose(bank[b + 2 - 2 * which][:, at:at + P], xh3[:, tt, c * P:c * P + P], ident)
                    last.then_inc(S["turned"], 1)

            pe.wait_ge(S["cf_in"], 16)
            with pe.Fori(0, DEPTH) as l:
                turn_x(l, 0)
                for kind, br, n in TIMELINE:
                    if kind == "unit":
                        _, role, i, b, t0 = UNITS[n]
                        w_h, w_l = part_of(w_hi, n), part_of(w_lo, n)

                        def product(o, m_of, low):
                            ks = range(w_h.shape[1])
                            for k in ks:
                                if n == 0 and low == 0:
                                    pe.wait_ge(S["x_lo_v"], l * KD + k + 1)
                                for w, x_ in ((w_l, xn_hi3),) if low else ((w_h, xn_hi3), (w_h, xn_lo3)):
                                    lhs, rhs = m_of(w, x_, k)
                                    last = pe.matmul(o, lhs, rhs, start=(m_start and k == 0 and w is w_h and x_ is xn_hi3),
                                                     stop=(m_stop and low == 1 and k == ks[-1]))
                            return last

                        m_start, m_stop = role != "v" or i == 0, role != "v" or i == 1
                        pe.wait_ge(S["hi_s"], l * N_UNITS + n + 1)
                        for c in range(2):
                            if role == "v":
                                o = bank[(n - i + c) % 2][:, :]
                                m_of = lambda w, x_, k: (x_[:, 4 * i + k, c * P:c * P + P], w[:, k, :])
                                if i == 0:
                                    pe.wait_ge(S["unit_s"], l * N_UNITS + n - 1 + c)
                            else:
                                o = bank[1 if role == "gate" else n % 2][:, c * T:c * T + T]
                                if role == "v2":
                                    m_of = lambda w, x_, k: (x_[:, k, c * P:c * P + P], w[:, k, :])
                                else:
                                    m_of = lambda w, x_, k: (w[:, k, c * P:c * P + P], x_[:, k, :])
                                if c == 0 and role == "gate" and n > GATE0:
                                    pe.wait_ge(S["unit_s"], l * N_UNITS + n)
                                elif c == 0 and n >= 2:
                                    pe.wait_ge(S["unit_s"], l * N_UNITS + n - 1)
                            product(o, m_of, 0)
                            if c == 0:
                                pe.wait_ge(S["lo_v"], l * N_UNITS + n + 1)
                            last = product(o, m_of, 1)
                            if role == "v" and i == 1 and c == 0:
                                last.then_inc(S["v_pe"], 1)
                        last.then_inc(S["unit_pe"], 1)
                    elif kind == "swap":
                        i = ROPE.index(n)
                        pe.wait_ge(S["unit_s"], l * N_UNITS + n + 1)
                        if i > 0:
                            pe.wait_ge(S["rope_v"], l * len(ROPE) + i)
                        pe.matmul(bank[6][:, :], swap, pre[:, n % 2, :], start=True, stop=True).then_inc(S["swap_pe"], 1)
                    elif kind == "lambda":
                        pe.wait_ge(S["lam_v"], l + 1)
                        pe.wait_ge(S["turn_v"], l * N_TURN + A_HEADS)
                        pe.matmul(bank[5][:, 0:2], msq[0:DH, :], lam_pr[0:DH, :], start=True,
                                  stop=True).then_inc(S["lam_pe"], 1)
                    elif kind == "score":
                        if br == "C" and n == 0:
                            pe.wait_ge(S["cb_in"], 16)
                        for part in range({"A": 1, "B": 2, "C": 3}[br]):
                            no = score_no(br, n, part)
                            if br == "A":
                                tile, m, o = n // 2, n % 2, bank[2 + n % 2]
                                if n == 0:
                                    pe.wait_ge(S["unit_s"], l * N_UNITS + 6)
                                if n >= 2:
                                    pe.wait_ge(S["scoreA_v"], l * A_HEADS + n - 1)
                            elif br == "B":
                                tile, m, o = n, part, bank[2 + part]
                                if n == 0 and part == 0:
                                    pe.wait_ge(S["rope_v"], l * len(ROPE) + 4)
                                    pe.wait_ge(S["scoreA_v"], l * A_HEADS + A_HEADS)
                                if n > 0:
                                    pe.wait_ge(S["exp_s"], l * N_SCORE + score_no(br, n - 1, part) + 1)
                            else:
                                tile, m, o = (part * C_HEADS + n) // 2, n % 2, bank[2 + part]
                                if n == 0 and part == 0:
                                    pe.wait_ge(S["rope_v"], l * len(ROPE) + 10)
                                    pe.wait_ge(S["exp_s"], l * N_SCORE + score_no("B", 3, 1) + 1)
                                    pe.wait_ge(S["yb_v"], l * B_HEADS + 4)
                                if n > 0:
                                    pe.wait_ge(S["exp_s"], l * N_SCORE + score_no(br, n - 1, part) + 1)
                                for tt in range(TT):
                                    pe.matmul(o[:, tt * T:tt * T + T], identb, maskC[:, part, tt, :],
                                              start=True, stop=False, skip_group_check=True)
                                    last = pe.matmul(o[:, tt * T:tt * T + T], q_of[br][:, tile, m, tt * P:tt * P + P],
                                                     k_of[br][:, tile, :], start=False, stop=True, skip_group_check=True)
                            if br != "C":
                                for tt in range(TT):
                                    last = pe.matmul(o[:, tt * T:tt * T + T], q_of[br][:, tile, m, tt * P:tt * P + P],
                                                     k_of[br][:, tile, :], start=True, stop=True)
                            last.then_inc(S["score_pe"], 1)
                    elif kind == "turn":
                        for part in range(C_GROUPS if br == "C" else 1):
                            no = turn_no(br, n, part)
                            slot_p = {"A": n % 4, "B": 2 * (n % 2), "C": part}[br]
                            o = {"A": bank[4 + n % 2], "B": bank[5], "C": bank[5 + part % 2]}[br]
                            pe.wait_ge(S["prob_v"], l * N_TURN + no + 1)
                            if br == "A" and n >= 2:
                                pe.wait_ge(S["turn_v"], l * N_TURN + no - 1)
                            elif br == "B":
                                pe.wait_ge(S["turn_v"], l * N_TURN + no)
                                if n == 0:
                                    pe.wait_ge(S["lam_s"], l + 1)
                            elif br == "C":
                                pe.wait_ge(S["turn_v"], l * N_TURN + no - (1 if part == 2 or part == 1 else 0))
                            for kt in range(TT):
                                for tt in range(TT):
                                    at = kt * T + tt * P
                                    last = pe.transpose(o[:, at:at + P], prob[:, slot_p, tt, kt * P:kt * P + P], ident)
                            last.then_inc(S["turn_pe"], 1)
                    elif kind == "pv":
                        if br == "A":
                            o = bank[7]
                            pe.wait_ge(S["turn_v"], l * N_TURN + turn_no("A", 2 * n + 1) + 1)
                            if n > 0:
                                pe.wait_ge(S["y_s"], l * 8 + n)
                            for kt in range(TT):
                                for m in range(2):
                                    hd = 2 * n + m
                                    last = pe.matmul(o[m * DH:m * DH + DH, 0:T], v_of["A"][:, kt, hd * DH:hd * DH + DH],
                                                     probT[:, hd % 4, kt, :], start=(kt == 0), stop=(kt == TT - 1))
                        elif br == "B":
                            o = bank[7 if n % 2 == 0 else 4]
                            pe.wait_ge(S["turn_v"], l * N_TURN + turn_no("B", n) + 1)
                            if n == 0:
                                pe.wait_ge(S["y_s"], l * 8 + 4)
                                pe.wait_ge(S["unit_s"], l * N_UNITS + 12)
                            if n >= 2:
                                pe.wait_ge(S["yb_v"], l * B_HEADS + n - 1)
                            for kt in range(TT):
                                last = pe.matmul(o[:, 0:T], v_of["B"][:, kt, n * P:n * P + P], probT[:, n % 4, kt, :],
                                                 start=(kt == 0), stop=(kt == TT - 1))
                        else:
                            o = bank[7]
                            pe.wait_ge(S["turn_v"], l * N_TURN + turn_no("C", n, 2) + 1)
                            if n == 0:
                                pe.wait_ge(S["yb_v"], l * B_HEADS + 4)
                                pe.wait_ge(S["unit_s"], l * N_UNITS + GATE0)
                            else:
                                pe.wait_ge(S["y_s"], l * 8 + 4 + n)
                            m = n % 2
                            for g in range(C_GROUPS):
                                hd = g * C_HEADS + n
                                for kt in range(TT):
                                    last = pe.matmul(o[m * DH:m * DH + DH, 0:T], v_of["C"][:, kt, hd * DH:hd * DH + DH],
                                                     probT[:, g, kt, :], start=(g == 0 and kt == 0),
                                                     stop=(g == C_GROUPS - 1 and kt == TT - 1))
                        last.then_inc(S["pv_pe"], 1)
                    elif kind == "ms":
                        o = bank[7 if n % 2 == 0 else 4]
                        pe.wait_ge(S["msq_s"], l * B_HEADS + n + 1)
                        pe.matmul(o[:, T:2 * T], msq[:, :], root[:, n % 2, :], start=True, stop=True,
                                  skip_group_check=True).then_inc(S["ms_pe"], 1)
                    elif kind == "branch":
                        w_at = AT[{"A": "pa", "B": "pb", "C": "pc"}[br], 0]
                        kk = 2 if br == "C" else 4
                        w = ring_view(SLOT_OF[w_at], kk, D)
                        if n % 4 == 0:
                            arrived(w_at, l)
                        if n == 0:
                            pe.wait_ge(S["unit_s"], l * N_UNITS + GATE0)
                            pe.wait_ge(S["y_s"], l * 8 + 4)
                        if n == 4:
                            pe.wait_ge(S["yb_v"], l * B_HEADS + 4)
                        if n == 8:
                            pe.wait_ge(S["y_s"], l * 8 + 8)
                        if n > 0:
                            pe.wait_ge(S["mix_v"], l * 12 + n)
                        for c2 in range(2):
                            c = 2 * (n % 4) + c2
                            for k in range(kk):
                                last = pe.matmul(bank[0][:, c2 * T:c2 * T + T], w[:, k, c * P:c * P + P],
                                                 y_of[br][:, k, :], start=(k == 0), stop=(k == kk - 1))
                        last.then_inc(S["branch_pe"], 1)
                    elif kind == "out":
                        arrived(AT["wo", n], l)
                        w = ring_view(SLOT_OF[AT["wo", n]], KD, 256)
                        if n == 0:
                            pe.wait_ge(S["mix_p"], l * 8 + 8)
                            pe.wait_ge(S["mix_v"], l * 12 + 12)
                        if n == 1:
                            pe.wait_ge(S["unit_s"], l * N_UNITS + N_UNITS)
                        if n >= 2:
                            pe.wait_ge(S["h_v"], l * 4 + n - 1)
                        for tt in range(TT):
                            for k in range(KD):
                                last = pe.matmul(bank[n % 2][:, tt * 256:tt * 256 + 256], mT[:, k, tt * P:tt * P + P],
                                                 w[:, k, :], start=(k == 0), stop=(k == KD - 1))
                        last.then_inc(S["out_pe"], 1)

                turn_x(l, 1)
                pe.wait_ge(S["xnT_v"], l * 2 + 2)
                pe.wait_ge(S["xnT_s"], l * 4 + 4)
                for tt in range(TT):
                    for k in range(KD):
                        last = pe.matmul(bank[4][:, tt * 20:tt * 20 + 20], xnT3[:, k, tt * P:tt * P + P],
                                         wr[:, k * 20:k * 20 + 20], start=(k == 0), stop=(k == KD - 1))
                last.then_inc(S["logit_pe"], 1)
                pe.wait_ge(S["asg_v"], l + 1)
                pe.matmul(bank[5][:, 0:16], tri, asg[:, 0, :], start=True, stop=True)
                pe.matmul(bank[5][:, 16:32], oneb, asg[:, 0, :], start=True, stop=False, skip_group_check=True)
                pe.matmul(bank[5][:, 16:32], tri, asg[:, 1, :], start=False, stop=True, skip_group_check=True)
                pe.matmul(bank[5][:, 32:48], oneb, asg[:, 0, :], start=True, stop=False, skip_group_check=True)
                pe.matmul(bank[5][:, 32:48], oneb, asg[:, 1, :], start=False, stop=True,
                          skip_group_check=True).then_inc(S["rank_pe"], 1)

                def gather(r, first=False):
                    pe.wait_ge(S["m_sel_v"], r + 1)
                    if not first:
                        pe.wait_ge(S["m_xgT_v"], r * 2)
                    for dh in range(2):
                        for tt in range(TT):
                            last = pe.matmul(bank[dh][:, :], sel[:, tt, :], xh3[:, tt, dh * 512:dh * 512 + 512],
                                             start=(tt == 0), stop=(tt == TT - 1))
                        last.then_inc(S["m_gather"], 1)

                def turn_rows(r):
                    for b in range(2):
                        if b == 0:
                            pe.wait_ge(S["m_xg_s"], r + 1)
                        else:
                            pe.wait_ge(S["m_xg_v"], r + 1)
                        for c in range(4 * b, 4 * b + 4):
                            last = pe.transpose(bank[b][:, (c % 4) * P:(c % 4) * P + P], xg[:, c * P:c * P + P], ident)
                        last.then_inc(S["m_xt"], 1)

                def landed_unit(which, r, l):
                    for i in range(2):
                        pe.wait_ge(landed[2 * which + i], ((l + 1) * USES[2 * which + i] + r + 1) * 16)

                def hidden(r, l, pair, first=False):
                    pe.wait_ge(S["m_xgT_v"], r * 2 + 2)
                    if first:
                        pe.wait_ge(S["pos_v"], l + 1)
                    else:
                        pe.wait_ge(S["m_hid_v"], r)
                    for which in range(2):
                        landed_unit(which, r, l)
                        o = bank[4 + which]
                        if pair:
                            w = [ring_view(2 * which + i, KD, F_EXP) for i in range(2)]
                            for k in range(KD):
                                for i in range(2):
                                    last = pe.matmul(o[i * CAP:i * CAP + CAP, :], xgT[:, k, i * CAP:i * CAP + CAP],
                                                     w[i][:, k, :], start=(k == 0), stop=(k == KD - 1))
                        else:
                            w = [ring_view(2 * which + i, KD // 2, F_EXP) for i in range(2)]
                            for k in range(KD):
                                last = pe.matmul(o[:, :], xgT[:, k, :], w[k // 4][:, k % 4, :],
                                                 start=(k == 0), stop=(k == KD - 1))
                        last.then_inc(S["m_h"], 1)

                def turn_hidden(r, first=False):
                    pe.wait_ge(S["m_hid_v"], r + 1)
                    if not first:
                        pe.wait_ge(S["m_add_v"], r * 4)
                    for f in range(KF):
                        last = pe.transpose(bank[2][:, f * P:f * P + P], hid[:, f * P:f * P + P], ident)
                    last.then_inc(S["m_ht"], 1)
                    pe.wait_ge(S["m_selg_v"], r + 1)
                    for tt in range(TT):
                        last = pe.transpose(bank[3][:, tt * P:tt * P + P], selg[:, tt, :], ident)
                    last.then_inc(S["m_st"], 1)

                def expert_out(r, l, pair, first=False):
                    landed_unit(2, r, l)
                    pe.wait_ge(S["m_hT_s"], r + 1)
                    if not first:
                        pe.wait_ge(S["m_y_s"], r)
                        pe.wait_ge(S["m_y_v"], r)
                    for dh in range(2):
                        for f in range(KF):
                            if pair:
                                for i in range(2):
                                    last = pe.matmul(bank[6 + dh][i * CAP:i * CAP + CAP, :], hT[:, f, i * CAP:i * CAP + CAP],
                                                     ring_view(4 + i, KF, D)[:, f, dh * 512:dh * 512 + 512],
                                                     start=(f == 0), stop=(f == KF - 1))
                            else:
                                last = pe.matmul(bank[6 + dh][:, :], hT[:, f, :],
                                                 ring_view(4 + f // 2, KF // 2, D)[:, f % 2, dh * 512:dh * 512 + 512],
                                                 start=(f == 0), stop=(f == KF - 1))
                        last.then_inc(S["m_y"], 1)

                def scatter(r):
                    pe.wait_ge(S["m_selT_s"], r + 1)
                    for dh in range(2):
                        pe.wait_ge(S["m_y_v" if dh else "m_y_s"], r + 1)
                        for tt in range(TT):
                            if dh:
                                pe.wait_ge(S["m_add_v"], r * 4 + tt + 1)
                            pe.matmul(bank[2 + tt][:, :], selT[:, tt * P:tt * P + P], y_e[:, dh * 512:dh * 512 + 512],
                                      start=True, stop=True).then_inc(S["m_sc"], 1)

                def unit(r, l, more, first=False):
                    hidden(r, l, True, first)
                    if more:
                        gather(r + 1)
                    turn_hidden(r, first)
                    expert_out(r, l, True, first)
                    if more:
                        turn_rows(r + 1)
                    scatter(r)

                r = pe.snap(units)
                gather(r, first=True)
                turn_rows(r)
                unit(r, l, True, first=True)
                pe.reg_add(units, units, 1)
                with pe.Fori(1, PAIRS - 1):
                    r = pe.snap(units)
                    unit(r, l, True)
                    pe.reg_add(units, units, 1)
                r = pe.snap(units)
                unit(r, l, False)
                pe.reg_add(units, units, 1)
                pe.wait_ge(S["over_v"], l + 1)
                pe.sem_inc(S["list_seen"], 1)
                n_over = pe.value_load(nexp[0:1, 0:1], min_val=0, max_val=N_OVER)
                with pe.If(n_over > 0):
                    with pe.Fori(0, n_over):
                        r = pe.snap(units)
                        gather(r)
                        turn_rows(r)
                        hidden(r, l, False)
                        turn_hidden(r)
                        expert_out(r, l, False)
                        scatter(r)
                        pe.reg_add(units, units, 1)

        @block.scalar
        def _(act):
            units = act.alloc_register("act_units")
            act.reg_mov(units, 0)

            def squares(l, which, n_done):
                for tt in range(TT):
                    last = nc.scalar.activation(zone_p[:, tt * D:tt * D + D], h3[:, tt, :], ACT.Square,
                                                accum_out=ss[:, tt:tt + 1])
                last.then_inc(S["sq"], 1)
                act.wait_ge(S["sq"], n_done + 1)
                nc.scalar.activation(std, ss, ACT.Sqrt, bias=eps1, scale=1.0 / D).then_inc(S["std_s"], 1)

            def split_hi(n, l):
                i = SLOT_OF[AT["in", UNITS[n][3]]]
                if n == 0 or UNITS[n][3] != UNITS[n - 1][3]:
                    uses = l * USES[i] + act.snap(units) + NTH[AT["in", UNITS[n][3]]] + 1
                    act.wait_ge(landed[i], uses * 16)
                if n >= 2:
                    act.wait_ge(S["unit_pe"], l * N_UNITS + n - 1)
                nc.scalar.activation(part_of(w_hi, n), weights_of(n), ACT.Copy).then_inc(S["hi_s"], 1)

            act.wait_ge(S["x_in"], 16)
            act.wait_ge(S["setup_v"], 4)
            act.wait_ge(S["zero_q1"], 1)
            with act.Fori(0, DEPTH) as l:
                squares(l, 0, l * 2)
                split_hi(0, l)
                act.wait_ge(S["gain1_v"], l + 1)
                for c in range(KD):
                    if c % 2 == 0:
                        act.wait_ge(S["turned"], l * 8 + c // 2 + 1)
                    nc.scalar.activation(xn_hi3[:, c, :], bank[2 + c // 2][:, (c % 2) * T:(c % 2) * T + T], ACT.Copy,
                                         scale=gain1[:, c:c + 1]).then_inc(S["x_hi_s"], 1)
                split_hi(1, l)
                for kind, br, n in TIMELINE:
                    if kind == "unit":
                        _, role, i, b, t0 = UNITS[n]
                        o = bank[1] if role == "gate" else bank[n % 2]
                        if n + 2 < N_UNITS:
                            split_hi(n + 2, l)
                        if role == "v" and i == 0:
                            continue
                        if role != "v":
                            act.wait_ge(S["unit_pe"], l * N_UNITS + n + 1)
                        if role == "gate":
                            g = i
                            if g == 0:
                                act.wait_ge(S["rope_v"], l * len(ROPE) + 10)
                            if g >= 2:
                                act.wait_ge(S["mix_v"], l * 12 + g - 1)
                            if g - 2 >= 4:
                                act.wait_ge(S["mix_p"], l * 8 + g - 2 - 4 + 1)
                            nc.scalar.activation(pre[:, g % 2, :], o[:, :], ACT.Sigmoid).then_inc(S["unit_s"], 1)
                        elif br == "A" and role == "q":
                            o2 = o[:, :].rearrange("p (i t) -> p i t", i=2)
                            nc.scalar.activation(q_of["A"][0:64, 2 * i:2 * i + 2, 0, :], o2[0:64], ACT.Copy)
                            nc.scalar.activation(q_of["A"][64:128, 2 * i:2 * i + 2, 1, :], o2[64:128],
                                                 ACT.Copy).then_inc(S["unit_s"], 1)
                        elif br == "A" and role == "k":
                            nc.scalar.activation(zone_k1[:, 512 * i:512 * i + 512], o[:, :], ACT.Copy).then_inc(S["unit_s"], 1)
                        elif role in "qk":
                            j = ROPE.index(n)
                            if j >= 2:
                                act.wait_ge(S["rope_v"], l * len(ROPE) + j - 1)
                            nc.scalar.activation(pre[:, n % 2, :], o[:, :], ACT.Copy).then_inc(S["unit_s"], 1)
                        elif role == "v":
                            if br != "A":
                                act.wait_ge(S["scoreA_v"], l * A_HEADS + A_HEADS)
                            act.wait_ge(S["v_pe"], l * 3 + "ABC".index(br) + 1)
                            nc.scalar.activation(v_of[br][:, 0, 0:512], bank[(n - 1) % 2][:, :],
                                                 ACT.Copy).then_inc(S["unit_s"], 1)
                            act.wait_ge(S["unit_pe"], l * N_UNITS + n + 1)
                            nc.scalar.activation(v_of[br][:, 1, 0:512], o[:, :], ACT.Copy).then_inc(S["unit_s"], 1)
                        else:
                            nc.scalar.activation(v_of["C"][:, :, 512:768], o[:, :].rearrange("p (t n) -> p t n", t=TT),
                                                 ACT.Copy).then_inc(S["unit_s"], 1)
                    elif kind == "lambda":
                        act.wait_ge(S["lam_pe"], l + 1)
                        nc.scalar.activation(lam_e, bank[5][:, 0:2], ACT.Exp, scale=float(P)).then_inc(S["lam_s"], 1)
                    elif kind == "score":
                        for part in range({"A": 1, "B": 2, "C": 3}[br]):
                            no = score_no(br, n, part)
                            act.wait_ge(S["max_v"], l * N_MAX + max_no(br, n, part) + 1)
                            if br == "A":
                                for tt in range(TT):
                                    last = nc.scalar.activation(prob[:, n % 4, tt, :], prob[:, n % 4, tt, :], ACT.Exp,
                                                                bias=nmx[:, n % 4, tt:tt + 1],
                                                                accum_out=psum_[:, n % 4, tt:tt + 1])
                            else:
                                s = 2 * (n % 2) + part if br == "B" else part
                                if br == "B":
                                    m = turn_no("A", 4 + s) if n < 2 else turn_no("B", n - 2)
                                    act.wait_ge(S["turn_pe"], l * N_TURN + m + 1)
                                elif n == 0:
                                    act.wait_ge(S["turn_pe"], l * N_TURN + turn_no("B", 3) + 1)
                                else:
                                    act.wait_ge(S["turn_pe"], l * N_TURN + turn_no("C", n - 1, part) + 1)
                                o = bank[2 + part]
                                for tt in range(TT):
                                    bias = nmx[:, s, tt:tt + 1] if br == "B" else nmx[:, n % 4, tt:tt + 1]
                                    acc = psum_[:, s, tt:tt + 1] if br == "B" else psc[:, tt, part:part + 1]
                                    last = nc.scalar.activation(prob[:, s, tt, :], o[:, tt * T:tt * T + T], ACT.Exp,
                                                                bias=bias, scale=SCALE, accum_out=acc)
                            last.then_inc(S["exp_s"], 1)
                    elif kind == "pv":
                        act.wait_ge(S["pv_pe"], l * 12 + pv_no(br, n) + 1)
                        if br == "A":
                            nc.scalar.activation(y_of["A"][:, n, :], bank[7][:, 0:T], ACT.Copy).then_inc(S["y_s"], 1)
                        elif br == "C":
                            m = n % 2
                            nc.scalar.activation(y_of["C"][m * DH:m * DH + DH, n // 2, :], bank[7][m * DH:m * DH + DH, 0:T],
                                                 ACT.Copy).then_inc(S["y_s"], 1)
                        else:
                            if n >= 2:
                                act.wait_ge(S["yb_v"], l * B_HEADS + n - 1)
                            nc.scalar.activation(root[:, n % 2, :], bank[7 if n % 2 == 0 else 4][:, 0:T],
                                                 ACT.Square).then_inc(S["msq_s"], 1)
                    elif kind == "ms":
                        act.wait_ge(S["ms_pe"], l * B_HEADS + n + 1)
                        nc.scalar.activation(root[:, n % 2, :], bank[7 if n % 2 == 0 else 4][:, T:2 * T], ACT.Sqrt,
                                             bias=eps2).then_inc(S["std_b"], 1)

                act.wait_ge(S["h_v"], l * 4 + 4)
                squares(l, 1, l * 2 + 1)
                for b in (1, 3):
                    act.wait_ge(S["turned"], l * 8 + 4 + b + 1)
                    for c in (2 * b, 2 * b + 1):
                        nc.scalar.activation(xnT3[:, c, :], bank[b][:, (c % 2) * T:(c % 2) * T + T], ACT.Copy,
                                             scale=gain2[:, c:c + 1]).then_inc(S["xnT_s"], 1)
                act.wait_ge(S["rd_v"], l * 2 + 1)
                nc.scalar.activation(g4b, g4a, ACT.Exp).then_inc(S["rexp_s"], 1)
                act.wait_ge(S["rd_v"], l * 2 + 2)
                nc.scalar.activation(s2[3], s2[2], ACT.Exp).then_inc(S["rexp_s"], 1)

                def rows_out(r):
                    act.wait_ge(S["m_gather"], r * 2 + 1)
                    nc.scalar.activation(xg[:, 0:512], bank[0][:, :], ACT.Copy).then_inc(S["m_xg_s"], 1)

                def gate(r):
                    act.wait_ge(S["m_h"], r * 2 + 1)
                    nc.scalar.activation(sig, bank[4][:, :], ACT.Sigmoid).then_inc(S["m_sig_s"], 1)

                def turned_out(r):
                    act.wait_ge(S["m_ht"], r + 1)
                    nc.scalar.activation(zone_t[:, D:D + 512], bank[2][:, :], ACT.Copy).then_inc(S["m_hT_s"], 1)
                    act.wait_ge(S["m_st"], r + 1)
                    nc.scalar.activation(selT, bank[3][:, 0:T], ACT.Copy).then_inc(S["m_selT_s"], 1)

                def y_out(r):
                    act.wait_ge(S["m_y"], r * 2 + 1)
                    nc.scalar.activation(y_e[:, 0:512], bank[6][:, :], ACT.Copy).then_inc(S["m_y_s"], 1)

                def unit(r, more):
                    gate(r)
                    if more:
                        rows_out(r + 1)
                    turned_out(r)
                    y_out(r)

                rows_out(act.snap(units))
                with act.Fori(0, PAIRS - 1):
                    unit(act.snap(units), True)
                    act.reg_add(units, units, 1)
                unit(act.snap(units), False)
                act.reg_add(units, units, 1)
                act.wait_ge(S["over_v"], l + 1)
                act.sem_inc(S["list_seen"], 1)
                n_over = act.value_load(nexp[0:1, 0:1], min_val=0, max_val=N_OVER)
                with act.If(n_over > 0):
                    with act.Fori(0, n_over):
                        r = act.snap(units)
                        rows_out(r)
                        unit(r, False)
                        act.reg_add(units, units, 1)
                act.wait_ge(S["m_add_v"], act.snap(units) * 4)

            squares(0, 0, DEPTH * 2)
            act.wait_ge(S["final_v"], 1)
            act.dma_start(out[0].rearrange("(t p) d -> p t d", p=P), xh3).then_inc(S["out_done"], 16)
            act.wait_ge(S["out_done"], 16)

        @block.vector
        def _(dve):
            units = dve.alloc_register("dve_units")
            steps = dve.alloc_register("dve_steps")
            dve.reg_mov(units, 0)
            dve.reg_mov(steps, 0)
            link, base = [0], [0]

            def chain(ins):
                link[0] += 1
                ins.then_inc(S["vstep"], 1)
                dve.wait_ge(S["vstep"], base[0] + link[0])

            def begin():
                base[0] = dve.snap(steps)

            def chained():
                if link[0]:
                    dve.reg_add(steps, steps, link[0])
                link[0] = 0

            V = nc.vector
            V.memset(msq[:, :], 1.0 / P).then_inc(S["setup_v"], 1)
            V.memset(zero32, 0.0).then_inc(S["setup_v"], 1)
            V.memset(eps1, NORM_EPS).then_inc(S["setup_v"], 1)
            V.memset(eps2, SUBLN_EPS).then_inc(S["setup_v"], 1)
            begin()
            dve.wait_ge(S["cf_in"], 16)

            def bc(ap, shape):
                return ap.broadcast_to(shape)

            def normalise(which, n_std):
                dve.wait_ge(S["std_s"], n_std)
                chain(V.reciprocal(rstd, std))
                for tt in range(TT):
                    V.tensor_scalar(xh3[:, tt, :], h3[:, tt, :], rstd[:, tt:tt + 1], None, ALU.mult).then_inc(S["xh_v"], 1)

            def split_lo(n, l):
                dve.wait_ge(S["hi_s"], l * N_UNITS + n + 1)
                V.tensor_tensor(part_of(w_lo, n), weights_of(n), part_of(w_hi, n).bitcast(F32),
                                ALU.subtract).then_inc(S["lo_v"], 1)

            dve.wait_ge(S["gains_in"], 16)
            with dve.Fori(0, DEPTH) as l:
                begin()
                V.tensor_copy(gain1[:, :], gains1[:, bass.ds(l * KD, KD)]).then_inc(S["gain1_v"], 1)
                normalise(0, l * 2 + 1)
                split_lo(0, l)
                for c in range(KD):
                    if c % 2 == 0:
                        dve.wait_ge(S["x_hi_s"], l * KD + c + 2)
                    if c == 0:
                        dve.wait_ge(S["gain1_v"], l + 1)
                    V.scalar_tensor_tensor(xn_lo3[:, c, :], bank[2 + c // 2][:, (c % 2) * T:(c % 2) * T + T],
                                           gain1[:, c:c + 1], xn_hi3[:, c, :].bitcast(F32), ALU.mult,
                                           ALU.subtract).then_inc(S["x_lo_v"], 1)
                split_lo(1, l)

                for kind, br, n in TIMELINE:
                    if kind == "unit" and n + 2 < N_UNITS:
                        split_lo(n + 2, l)
                    elif kind == "lambda":
                        dve.wait_ge(S["small_in"], (l + 1) * N_LOADS * 16)
                        V.tensor_tensor(lam_pr[0:DH, :], vec[:, 0:2], vec[:, 2:4], ALU.mult).then_inc(S["lam_v"], 1)
                        chain(V.tensor_tensor(subg, subg, cf[:, bass.ds(l * 2 + (C_LINIT + 1), 1)], ALU.mult))
                    elif kind == "soft" and br == "B" and n == 0:
                        dve.wait_ge(S["lam_s"], l + 1)
                        chain(V.tensor_tensor(lam, lam_e[:, 0:1], lam_e[:, 1:2], ALU.subtract))
                        chain(V.tensor_tensor(lam, lam, cf[:, bass.ds(l * 2 + C_LINIT, 1)], ALU.add))
                    if kind == "swap":
                        i = ROPE.index(n)
                        if i == 0:
                            dve.wait_ge(S["zero_q2"], l + 1)
                        b_, role, pr, _, _ = UNITS[n]
                        dve.wait_ge(S["swap_pe"], l * len(ROPE) + i + 1)
                        dve.wait_ge(S["cos_p"], l * len(ROPE) + i + 1)
                        o2 = bank[6][:, :].rearrange("p (i t) -> p i t", i=2)
                        x2 = pre[:, n % 2, :].rearrange("p (i t) -> p i t", i=2)
                        c2 = zone_c[:, :].rearrange("p (i t) -> p i t", i=2)
                        chain(V.tensor_tensor(x2, o2, sin2, ALU.mult))
                        if role == "q":
                            V.tensor_tensor(q_of[b_][0:64, 2 * pr:2 * pr + 2, 0, :], x2[0:64], c2[0:64], ALU.add)
                            V.tensor_tensor(q_of[b_][64:128, 2 * pr:2 * pr + 2, 1, :], x2[64:128], c2[64:128],
                                            ALU.add).then_inc(S["rope_v"], 1)
                        else:
                            V.tensor_tensor(k_of[b_][:, 2 * pr:2 * pr + 2, :], x2, c2, ALU.add).then_inc(S["rope_v"], 1)
                    elif kind == "score" and br == "A":
                        s = n % 4
                        if n % 2 == 0:
                            dve.wait_ge(S["bias_p"], l * 4 + n // 2 + 1)
                        dve.wait_ge(S["score_pe"], l * N_SCORE + n + 1)
                        if n >= 4:
                            dve.wait_ge(S["turn_pe"], l * N_TURN + n - 3)
                        V.scalar_tensor_tensor(prob[:, s, :, :].rearrange("p t k -> p (t k)"), bank[2 + n % 2][:, :], SCALE,
                                               biasA[n // 2][:, n % 2, :, :].rearrange("p t k -> p (t k)"),
                                               ALU.mult, ALU.add).then_inc(S["scoreA_v"], 1)
                        dve.wait_ge(S["scoreA_v"], l * A_HEADS + n + 1)
                        V.tensor_reduce(nmx[:, s, :], prob[:, s, :, :], AX_X, ALU.max, negate=True).then_inc(S["max_v"], 1)
                    elif kind == "score":
                        for part in range({"B": 2, "C": 3}[br]):
                            dve.wait_ge(S["score_pe"], l * N_SCORE + score_no(br, n, part) + 1)
                            s = 2 * (n % 2) + part if br == "B" else n % 4
                            o = bank[2 + part][:, :].rearrange("p (t k) -> p t k", t=TT)
                            if br == "B":
                                chain(V.tensor_reduce(raw[:, s, :], o, AX_X, ALU.max, negate=True))
                                V.tensor_scalar(nmx[:, s, :], raw[:, s, :], SCALE, None, ALU.mult).then_inc(S["max_v"], 1)
                            else:
                                chain(V.tensor_reduce(mxc[:, :, part:part + 1], o, AX_X, ALU.max))
                        if br == "C":
                            chain(V.tensor_reduce(raw[:, s, :], mxc, AX_X, ALU.max, negate=True))
                            V.tensor_scalar(nmx[:, s, :], raw[:, s, :], SCALE, None, ALU.mult).then_inc(S["max_v"], 1)
                    elif kind == "soft":
                        for b_, m in [(br, n)]:
                            if b_ == "A":
                                s = m % 4
                                dve.wait_ge(S["exp_s"], l * N_SCORE + m + 1)
                                chain(V.reciprocal(rin[:, s, :], psum_[:, s, :]))
                                for tt in range(TT):
                                    last = V.tensor_scalar(prob[:, s, tt, :], prob[:, s, tt, :], rin[:, s, tt:tt + 1],
                                                           None, ALU.mult)
                                last.then_inc(S["prob_v"], 1)
                            elif b_ == "B":
                                s = 2 * (m % 2)
                                dve.wait_ge(S["exp_s"], l * N_SCORE + score_no("B", m, 1) + 1)
                                chain(V.reciprocal(rin[:, s:s + 2, :], psum_[:, s:s + 2, :]))
                                chain(V.tensor_scalar(rin[:, s + 1, :], rin[:, s + 1, :], lam, None, ALU.mult))
                                for tt in range(TT):
                                    chain(V.tensor_scalar(prob[:, s + 1, tt, :], prob[:, s + 1, tt, :],
                                                          rin[:, s + 1, tt:tt + 1], None, ALU.mult))
                                for tt in range(TT):
                                    last = V.scalar_tensor_tensor(prob[:, s, tt, :], prob[:, s, tt, :],
                                                                  rin[:, s, tt:tt + 1], prob[:, s + 1, tt, :],
                                                                  ALU.mult, ALU.subtract)
                                last.then_inc(S["prob_v"], 1)
                            else:
                                dve.wait_ge(S["exp_s"], l * N_SCORE + score_no("C", m, 2) + 1)
                                chain(V.tensor_reduce(s2[1], psc, AX_X, ALU.add))
                                chain(V.reciprocal(rin[:, m % 4, :], s2[1]))
                                for g in range(C_GROUPS):
                                    for tt in range(TT):
                                        last = V.tensor_scalar(prob[:, g, tt, :], prob[:, g, tt, :],
                                                               rin[:, m % 4, tt:tt + 1], None, ALU.mult)
                                    last.then_inc(S["prob_v"], 1)
                    elif kind == "turn":
                        for part in range(C_GROUPS if br == "C" else 1):
                            no = turn_no(br, n, part)
                            o = {"A": bank[4 + n % 2], "B": bank[5], "C": bank[5 + part % 2]}[br]
                            s = part if br == "C" else n % 4
                            dve.wait_ge(S["turn_pe"], l * N_TURN + no + 1)
                            if br == "A" and n >= 4:
                                dve.wait_ge(S["pv_pe"], l * 12 + (n - 4) // 2 + 1)
                            elif br == "B":
                                dve.wait_ge(S["pv_pe"], l * 12 + 4)
                            elif br == "C":
                                dve.wait_ge(S["pv_pe"], l * 12 + 8 + n)
                            V.tensor_copy(probT[:, s, :, :].rearrange("p k t -> p (k t)"), o[:, :]).then_inc(S["turn_v"], 1)
                    elif kind == "ms":
                        o = bank[7 if n % 2 == 0 else 4]
                        dve.wait_ge(S["std_b"], l * B_HEADS + n + 1)
                        chain(V.reciprocal(root[:, n % 2, :], root[:, n % 2, :]))
                        V.scalar_tensor_tensor(y_of["B"][:, n, :], o[:, 0:T], subg, root[:, n % 2, :], ALU.mult,
                                               ALU.mult).then_inc(S["yb_v"], 1)
                    elif kind == "branch":
                        dve.wait_ge(S["branch_pe"], l * 12 + n + 1)
                        dve.wait_ge(S["unit_s"], l * N_UNITS + GATE0 + n + 1)
                        dst = xh[:, 512 * n:512 * n + 512] if br == "A" else pre[:, n % 2, :]
                        V.tensor_tensor(dst, bank[0][:, :], pre[:, n % 2, :], ALU.mult).then_inc(S["mix_v"], 1)
                    elif kind == "out":
                        dve.wait_ge(S["out_pe"], l * 4 + n + 1)
                        hs = h3[:, :, 256 * n:256 * n + 256]
                        V.tensor_tensor(hs, bank[n % 2][:, :].rearrange("p (t d) -> p t d", t=TT), hs,
                                        ALU.add).then_inc(S["h_v"], 1)

                normalise(1, l * 2 + 2)
                for b in (0, 2):
                    dve.wait_ge(S["turned"], l * 8 + 4 + b + 1)
                    V.tensor_tensor(xnT3[:, 2 * b:2 * b + 2, :], bank[b][:, :].rearrange("p (c t) -> p c t", c=2),
                                    bc(gain2[:, 2 * b:2 * b + 2].unsqueeze(2), [P, 2, T]),
                                    ALU.mult).then_inc(S["xnT_v"], 1)
                dve.wait_ge(S["logit_pe"], l + 1)
                chain(V.tensor_tensor(lg, bank[4][:, 0:40].rearrange("p (t e) -> p t e", t=TT),
                                      bc(rb.unsqueeze(1), [P, TT, 20]), ALU.add))
                w16 = bc(cf[:, C_W16:C_W16 + 16].unsqueeze(1), [P, TT, 16])
                w4 = bc(cf[:, C_W16:C_W16 + 4].unsqueeze(1), [P, TT, 4])
                col = lambda a, n: bc(a.unsqueeze(2), [P, TT, n])
                lg4, lg16 = lg[:, :, 0:4], lg[:, :, 4:20]
                chain(V.tensor_reduce(s2[4], lg4, AX_X, ALU.max))
                V.tensor_tensor(g4a, lg4, col(s2[4], 4), ALU.subtract).then_inc(S["rd_v"], 1)
                chain(V.tensor_tensor(goh, lg4, col(s2[4], 4), ALU.is_equal))
                chain(V.tensor_tensor(goh, goh, w4, ALU.mult))
                chain(V.tensor_reduce(s2[5], goh, AX_X, ALU.max))
                chain(V.tensor_tensor(goh, goh, col(s2[5], 4), ALU.is_equal))
                chain(V.tensor_scalar(goh, goh, -NEG, NEG, ALU.mult, ALU.add))
                chain(V.tensor_tensor(e16[0].rearrange("p t (g e) -> p t g e", g=N_GRP),
                                      lg16.rearrange("p t (g e) -> p t g e", g=N_GRP),
                                      goh.unsqueeze(3).broadcast_to([P, TT, N_GRP, PER_GRP]), ALU.add))

                def first_max(dst, value, src):
                    chain(V.tensor_reduce(value, src, AX_X, ALU.max))
                    chain(V.tensor_tensor(dst, src, col(value, 16), ALU.is_equal))
                    chain(V.tensor_tensor(dst, dst, w16, ALU.mult))
                    chain(V.tensor_reduce(s2[5], dst, AX_X, ALU.max))
                    chain(V.tensor_tensor(dst, dst, col(s2[5], 16), ALU.is_equal))

                first_max(e16[1], s2[6], e16[0])
                chain(V.scalar_tensor_tensor(e16[0], e16[1], NEG, e16[0], ALU.mult, ALU.add))
                first_max(e16[2], s2[7], e16[0])
                V.tensor_tensor(asg, e16[1], e16[2], ALU.add).then_inc(S["asg_v"], 1)
                V.tensor_tensor(s2[2], s2[7], s2[6], ALU.subtract).then_inc(S["rd_v"], 1)
                dve.wait_ge(S["rexp_s"], l * 2 + 1)
                chain(V.tensor_reduce(s2[8], g4b, AX_X, ALU.add))
                chain(V.reciprocal(s2[8], s2[8]))
                dve.wait_ge(S["rexp_s"], l * 2 + 2)
                chain(V.tensor_scalar(s2[9], s2[3], 1.0, None, ALU.add))
                chain(V.reciprocal(s2[9], s2[9]))
                chain(V.tensor_tensor(s2[9], s2[9], s2[8], ALU.mult))
                chain(V.tensor_tensor(s2[3], s2[3], s2[9], ALU.mult))
                chain(V.tensor_tensor(gat, e16[1], col(s2[9], 16), ALU.mult))
                chain(V.tensor_tensor(e16[3], e16[2], col(s2[3], 16), ALU.mult))
                chain(V.tensor_tensor(gat, gat, e16[3], ALU.add))
                chain(V.tensor_tensor(e16[4], e16[1], e16[2], ALU.add))
                chain(V.tensor_scalar(e16[4], e16[4], -FAR, FAR, ALU.mult, ALU.add))
                dve.wait_ge(S["rank_pe"], l + 1)
                chain(V.tensor_tensor(pos, bank[5][:, 0:32].rearrange("p (t e) -> p t e", t=TT), e16[4], ALU.add))
                V.tensor_copy(cnt, bank[5][:, 32:48]).then_inc(S["pos_v"], 1)
                dve.wait_ge(S["pos_v"], l + 1)
                chained()
                begin()

                iota = cf[:, C_IOTA:C_IOTA + P]
                iota64 = cf[:, C_IOTA:C_IOTA + CAP]

                def one(a, tt, e):
                    return a[:, tt, e:e + 1] if isinstance(e, int) else a[:, tt, bass.ds(e, 1)]

                def select(r, e0):
                    for i in range(2):
                        for tt in range(TT):
                            last = V.tensor_scalar(sel[:, tt, i * CAP:i * CAP + CAP], iota64,
                                                   one(pos, tt, e0 + i), None, ALU.is_equal)
                    last.then_inc(S["m_sel_v"], 1)

                def select_gated(r, e0):
                    for i in range(2):
                        for tt in range(TT):
                            last = V.tensor_scalar(selg[:, tt, i * CAP:i * CAP + CAP], iota64,
                                                   one(pos, tt, e0 + i), one(gat, tt, e0 + i),
                                                   ALU.is_equal, ALU.mult)
                    last.then_inc(S["m_selg_v"], 1)

                def rows_out(r):
                    dve.wait_ge(S["m_gather"], r * 2 + 2)
                    V.tensor_copy(xg[:, 512:1024], bank[1][:, :]).then_inc(S["m_xg_v"], 1)

                def rows_turned(r):
                    for b in range(2):
                        dve.wait_ge(S["m_xt"], r * 2 + b + 1)
                        V.tensor_tensor(xgT[:, 4 * b:4 * b + 4, :], bank[b][:, :].rearrange("p (c s) -> p c s", c=4),
                                        bc(gain2[:, 4 * b:4 * b + 4].unsqueeze(2), [P, 4, P]),
                                        ALU.mult).then_inc(S["m_xgT_v"], 1)

                def hidden(r):
                    dve.wait_ge(S["m_sig_s"], r + 1)
                    chain(V.tensor_tensor(sig, bank[4][:, :], sig, ALU.mult))
                    dve.wait_ge(S["m_h"], r * 2 + 2)
                    V.tensor_tensor(hid, bank[5][:, :], sig, ALU.mult).then_inc(S["m_hid_v"], 1)

                def y_out(r):
                    dve.wait_ge(S["m_y"], r * 2 + 2)
                    V.tensor_copy(y_e[:, 512:1024], bank[7][:, :]).then_inc(S["m_y_v"], 1)

                def add(r):
                    for dh in range(2):
                        for tt in range(TT):
                            dve.wait_ge(S["m_sc"], r * 4 + dh * 2 + tt + 1)
                            hs = h3[:, tt, dh * 512:dh * 512 + 512]
                            V.tensor_tensor(hs, bank[2 + tt][:, :], hs, ALU.add).then_inc(S["m_add_v"], 1)

                def unit(r, p, more):
                    if more:
                        dve.wait_ge(S["m_gather"], r * 2 + 2)
                        select(r + 1, p * 2 + 2)
                    hidden(r)
                    if more:
                        rows_out(r + 1)
                    y_out(r)
                    if more:
                        rows_turned(r + 1)
                        dve.wait_ge(S["m_st"], r + 1)
                        select_gated(r + 1, p * 2 + 2)
                    add(r)
                    chained()

                r = dve.snap(units)
                select(r, 0)
                select_gated(r, 0)
                rows_out(r)
                rows_turned(r)
                thr = cf[:, C_THR:C_THR + 32]
                by2 = lambda a: a.rearrange("p (e c) -> p e c", c=2)
                chain(V.tensor_tensor(by2(exist), bc(cnt.unsqueeze(2), [P, 16, 2]), by2(thr), ALU.is_gt))
                chain(V.tensor_tensor_scan(cum, exist, zero32, 0.0, ALU.add, ALU.add))
                row = lambda a: bc(a.unsqueeze(1), [P, N_OVER, 32])
                jrow = cf[:, C_JROW:C_JROW + N_OVER]
                chain(V.tensor_tensor(over_a, row(cum), bc(jrow.unsqueeze(2), [P, N_OVER, 32]), ALU.is_equal))
                chain(V.tensor_tensor(over_a, over_a, row(exist), ALU.mult))
                for src, dst in ((pos, pos_o), (gat, gat_o)):
                    for tt in range(TT):
                        wide = src[:, tt, :].unsqueeze(1).unsqueeze(3).broadcast_to([P, N_OVER, 16, 2])
                        by4 = lambda a: a.rearrange("p j (e c) -> p j e c", c=2)
                        chain(V.tensor_tensor(by4(over_b), by4(over_a), wide, ALU.mult))
                        chain(V.tensor_reduce(dst[:, tt, :], over_b, AX_X, ALU.add))
                chain(V.tensor_tensor(over_b, over_a, row(thr), ALU.mult))
                chain(V.tensor_reduce(eid_o, over_b, AX_X, ALU.add))
                for tt in range(TT):
                    chain(V.tensor_tensor(pos_o[:, tt, :], pos_o[:, tt, :], eid_o, ALU.subtract))
                chain(V.tensor_tensor(over_b, over_a, row(cf[:, C_EIDX:C_EIDX + 32]), ALU.mult))
                chain(V.tensor_reduce(eid_o, over_b, AX_X, ALU.add))
                chain(V.tensor_copy(nexp[:, 1:1 + N_OVER], eid_o))
                V.tensor_copy(nexp[:, 0:1], cum[:, 31:32]).then_inc(S["over_v"], 1)
                chained()

                with dve.Fori(0, PAIRS - 1) as p:
                    begin()
                    unit(dve.snap(units), p, True)
                    dve.reg_add(units, units, 1)
                begin()
                unit(dve.snap(units), 0, False)
                dve.reg_add(units, units, 1)
                dve.wait_ge(S["over_v"], l + 1)
                dve.sem_inc(S["list_seen"], 1)
                n_over = dve.value_load(nexp[0:1, 0:1], min_val=0, max_val=N_OVER)
                with dve.If(n_over > 0):
                    with dve.Fori(0, n_over) as j:
                        begin()
                        r = dve.snap(units)
                        dve.wait_ge(S["m_st"], r)
                        for tt in range(TT):
                            last = V.tensor_scalar(sel[:, tt, :], iota, pos_o[:, tt, bass.ds(j, 1)], None, ALU.is_equal)
                        last.then_inc(S["m_sel_v"], 1)
                        for tt in range(TT):
                            last = V.tensor_scalar(selg[:, tt, :], iota, pos_o[:, tt, bass.ds(j, 1)],
                                                   gat_o[:, tt, bass.ds(j, 1)], ALU.is_equal, ALU.mult)
                        last.then_inc(S["m_selg_v"], 1)
                        rows_out(r)
                        rows_turned(r)
                        unit(r, 0, False)
                        dve.reg_add(units, units, 1)

            begin()
            dve.wait_ge(S["fin_in"], 16)
            dve.wait_ge(S["std_s"], DEPTH * 2 + 1)
            chain(V.reciprocal(rstd, std))
            for tt in range(TT):
                last = V.scalar_tensor_tensor(xh3[:, tt, :], h3[:, tt, :], rstd[:, tt:tt + 1], fin[:, :], ALU.mult, ALU.mult)
            last.then_inc(S["final_v"], 1)


_INS = ["x", "w_in", "na_rpb", "lam_q1", "lam_k1", "lam_q2", "lam_k2", "diff_subln", "w_pa", "w_pb", "w_pc", "w_o",
        "norm_mix", "norm_ffn", "router_group_w", "router_group_b", "router_expert_w", "router_expert_b",
        "w1", "w3", "w2", "norm_final"]


def kernel(**inputs):
    import concourse.bacc as bacc
    from concourse.bass_utils import run_bass_kernel_spmd

    nc = bacc.Bacc("TRN2", target_bir_lowering=False, num_devices=1)
    arrays = {f"in_{n}": np.ascontiguousarray(inputs[n]) for n in _INS}
    arrays["in_consts"] = constants()
    args = [nc.dram_tensor(n, a.shape, mybir.dt.from_np(a.dtype), kind="ExternalInput").ap() for n, a in arrays.items()]
    out = nc.dram_tensor("out", (1, T, D), F32, kind="ExternalOutput").ap()
    build(nc, *args, out)
    return run_bass_kernel_spmd(nc, [arrays], core_ids=[0]).results[0]["out"]
```

```python
import math
from contextlib import ExitStack

import numpy as np

import concourse.bass as bass
from concourse import mybir

F32 = mybir.dt.float32
F32R = mybir.dt.float32r
BF16 = mybir.dt.bfloat16
I32 = mybir.dt.int32
ALU = mybir.AluOpType
ACT = mybir.ActivationFunctionType
AX_X = mybir.AxisListType.X

P = 128
T = 256
TT = T // P
D = 1024
KD = D // P
DEPTH = 2
DH = 64
GRID_W = 64
A_HEADS = 8
B_HEADS = 4
C_GROUPS = 3
C_HEADS = 4
SCALE = DH ** -0.5
NEG = -1e30
NORM_EPS = 1e-6
SUBLN_EPS = 1e-5
N_EXP = 16
N_GRP = 4
PER_GRP = N_EXP // N_GRP
F_EXP = D // 2
KF = F_EXP // P
CAP = 64
FAR = 1000.0
PAIRS = N_EXP // 2
N_OVER = 8
SLOT = 4096
RING = 6
RPB = 15 * 31
RPB_C = 31
N_GAIN, N_SUBG, N_LAM, N_RB, N_WR, N_VEC, N_CUR = 0, 8, 9, 10, 30, 190, 194
N_LOADS = 10

C_IDENT, C_SWAP, C_COS, C_SIN = 0, 128, 256, 512
C_IOTA, C_W16, C_THR, C_EIDX, C_JROW, C_LINIT = 768, 896, 912, 944, 976, 984
C_KEEP = 988
C_TRI, C_IDB, C_ONE, C_MASKA = C_KEEP, C_KEEP + 128, C_KEEP + 256, C_KEEP + 384
C_MASKC = C_MASKA + 512
C_ALL = C_MASKC + C_GROUPS * TT * T
NB16 = C_ALL - C_KEEP


def constants():
    c = np.zeros((P, C_ALL), np.float32)
    p = np.arange(P)
    c[:, C_IDENT:C_IDENT + P] = np.eye(P)
    half = 8
    inv = (1.0 / (np.float32(500000.0) ** (np.arange(0, 16, 2, dtype=np.float32) / np.float32(16)))).astype(np.float32)
    ang = np.arange(T, dtype=np.float32)[:, None] * inv[None, :]
    cos, sin = np.cos(ang).T, np.sin(ang).T
    c[:, C_COS:C_COS + T] = 1.0
    for q in p:
        d = q % DH
        if d < 2 * half:
            partner = q + half if d < half else q - half
            c[partner, C_SWAP + q] = 1.0
            c[q, C_COS:C_COS + T] = cos[d % half]
            c[q, C_SIN:C_SIN + T] = -sin[d] if d < half else sin[d - half]
    tok = np.arange(T)
    col = tok % GRID_W
    first = np.clip(col - 8, 0, GRID_W - 16)
    ok = (col[None, :] >= first[:, None]) & (col[None, :] < first[:, None] + 16)
    mask = lambda ok: np.where(ok, 0.0, NEG).reshape(TT, P, T).transpose(1, 0, 2).reshape(P, TT * T)
    c[:, C_MASKA:C_MASKA + TT * T] = mask(ok)
    c[:, C_IOTA:C_IOTA + P] = np.arange(P)
    c[:, C_W16:C_W16 + 16] = 16 - np.arange(16)
    c[:, C_THR:C_THR + 32] = np.tile([CAP, CAP + P], 16)
    c[:, C_EIDX:C_EIDX + 32] = np.repeat(np.arange(16), 2)
    c[:, C_JROW:C_JROW + N_OVER] = 1 + np.arange(N_OVER)
    for layer in range(DEPTH):
        lam = 0.8 - 0.6 * math.exp(-0.3 * layer)
        c[:, C_LINIT + 2 * layer] = lam
        c[:, C_LINIT + 2 * layer + 1] = 1.0 - lam
    c[:, C_TRI:C_TRI + P] = p[:, None] < p[None, :]
    c[:, C_IDB:C_IDB + P] = np.eye(P)
    c[:, C_ONE:C_ONE + P] = 1.0
    for g, dil in enumerate((1, 4, 16)):
        diff = tok[None, :] - tok[:, None]
        ok = (diff % dil == 0) & (np.abs(diff) <= 64 * dil)
        c[:, C_MASKC + g * TT * T:C_MASKC + (g + 1) * TT * T] = mask(ok)
    return c


ORDER = [("in", b) for b in range(10)] + [("pa", 0), ("in", 10), ("in", 11), ("in", 12), ("pb", 0), ("in", 13),
         ("in", 14), ("pc", 0), ("in", 15), ("in", 16)] + [("wo", s) for s in range(4)]
AT = {w: n for n, w in enumerate(ORDER)}
SLOT_OF = [0, 1, 2, 3, 0, 1, 2, 3, 0, 1, 2, 3, 0, 1, 3, 0, 1, 2, 0, 1, 3, 0, 1, 2]
USES = [SLOT_OF.count(i) for i in range(RING)]
MISSED = [1, 1, 1, 0, 0, 0]
NTH = [SLOT_OF[:n].count(i) for n, i in enumerate(SLOT_OF)]
BEFORE = [max((m for m in range(n) if SLOT_OF[m] == i), default=None) for n, i in enumerate(SLOT_OF)]
LAST_USE = [max((n for n, j in enumerate(SLOT_OF) if j == i), default=None) for i in range(RING)]
assert DEPTH <= 4 and len(ORDER) == len(SLOT_OF) and USES[4] == USES[5] == 0

UNITS = []
for _br, _b0 in (("A", 0), ("B", 3)):
    for _role, _b in (("q", 0), ("k", 1)):
        UNITS += [(_br, _role, i, _b0 + _b, 2 * i) for i in range(2)]
    UNITS += [(_br, "v", half, _b0 + 2, 0) for half in range(2)]
UNITS += [("C", "q", 0, 6, 0), ("C", "q", 1, 6, 2), ("C", "q", 2, 7, 0),
          ("C", "k", 0, 7, 2), ("C", "k", 1, 8, 0), ("C", "k", 2, 8, 2),
          ("C", "v", 0, 9, 0), ("C", "v", 1, 9, 0), ("C", "v2", 0, 10, 0)]
UNITS += [("ABC"[(g := (4 * b + t - 42) // 2) // 4], "gate", g, b, t)
          for b in range(10, 17) for t in (0, 2) if 4 * b + t >= 42 and 4 * b + t < 66]
FIRSTS = [sum(x[1] != "v2" for x in UNITS[:n + 1]) for n in range(len(UNITS))]
GATE0 = UNITS.index(("A", "gate", 0, 10, 2))
N_UNITS = len(UNITS)
N_SPLIT = N_UNITS + 4
ROPE = [u for u, x in enumerate(UNITS) if x[0] in "BC" and x[1] in "qk"]
LAST_UNIT = {b: max(u for u, x in enumerate(UNITS) if x[3] == b) for b in range(17)}


def timeline():
    after = {
        6: [("score", "A", 0), ("score", "A", 1), ("soft", "A", 0), ("soft", "A", 1)],
        7: [("turn", "A", 0), ("score", "A", 2), ("turn", "A", 1), ("score", "A", 3), ("soft", "A", 2), ("soft", "A", 3)],
        8: [("pv", "A", 0), ("turn", "A", 2), ("score", "A", 4), ("turn", "A", 3), ("score", "A", 5), ("soft", "A", 4),
            ("soft", "A", 5)],
        9: [("pv", "A", 1), ("turn", "A", 4), ("score", "A", 6), ("turn", "A", 5), ("score", "A", 7), ("soft", "A", 6),
            ("soft", "A", 7)],
        10: [("pv", "A", 2), ("turn", "A", 6), ("turn", "A", 7)],
        11: [("pv", "A", 3), ("vectors", "B", 0)],
        12: [("score", "B", 0), ("lambda", "B", 0), ("soft", "B", 0)],
        13: [("turn", "B", 0), ("score", "B", 1), ("soft", "B", 1)],
        14: [("pv", "B", 0), ("turn", "B", 1), ("score", "B", 2), ("soft", "B", 2)],
        15: [("ms", "B", 0), ("pv", "B", 1), ("turn", "B", 2), ("score", "B", 3), ("soft", "B", 3)],
        16: [("ms", "B", 1), ("pv", "B", 2), ("turn", "B", 3)],
        17: [("ms", "B", 2), ("pv", "B", 3)],
        18: [("ms", "B", 3), ("norm", "B", 0)],
        19: [("inv", "B", 0)],
        20: [("score", "C", 0), ("inv", "B", 1), ("soft", "C", 0)],
        GATE0: [("turn", "C", 0)], GATE0 + 1: [("pv", "C", 0), ("score", "C", 1), ("soft", "C", 1)],
        GATE0 + 2: [("turn", "C", 1)], GATE0 + 3: [("pv", "C", 1), ("score", "C", 2), ("soft", "C", 2)],
        GATE0 + 4: [("turn", "C", 2)], GATE0 + 5: [("pv", "C", 2), ("score", "C", 3), ("soft", "C", 3)],
        GATE0 + 6: [("turn", "C", 3)], GATE0 + 7: [("pv", "C", 3)],
    }
    steps = []
    for u, x in enumerate(UNITS):
        steps.append(("unit", x[0], u))
        if u - 1 in ROPE:
            steps.append(("swap", UNITS[u - 1][0], u - 1))
        if x[1] == "gate":
            steps.append(("branch", x[0], x[2]))
            if x[2] >= 9:
                steps.append(("m_parts", "", x[2] - 9))
        steps += after.get(u, [])
    steps.append(("m_parts", "", 3))
    for part in range(4):
        steps.append(("out", "", part))
        if part >= 1:
            steps.append(("turn_h", "", part - 1))
        if part >= 2:
            steps.append(("logit", "", part - 2))
    return steps + [("turn_h", "", 3), ("logit", "", 2), ("logit", "", 3)]


TIMELINE = timeline()

N_SCORE = A_HEADS + 2 * B_HEADS + C_GROUPS * C_HEADS
N_TURN = A_HEADS + B_HEADS + C_GROUPS * C_HEADS


def score_no(br, n, part=0):
    return {"A": n, "B": A_HEADS + 2 * n + part, "C": A_HEADS + 2 * B_HEADS + C_GROUPS * n + part}[br]


def turn_no(br, n, part=0):
    return {"A": n, "B": A_HEADS + n, "C": A_HEADS + B_HEADS + C_GROUPS * n + part}[br]


def max_no(br, n, part=0):
    return {"A": n, "B": A_HEADS + 2 * n + part, "C": A_HEADS + 2 * B_HEADS + n}[br]


BIAS_IN = 4 * 8 * 16
N_MAX = A_HEADS + 2 * B_HEADS + C_HEADS


def pv_no(br, n):
    return {"A": n, "B": 4 + n, "C": 8 + n}[br]


def build(nc, x, w_in, na_rpb, lam_q1, lam_k1, lam_q2, lam_k2, diff_subln, w_pa, w_pb, w_pc, w_o,
          norm_mix, norm_ffn, router_group_w, router_group_b, router_expert_w, router_expert_b,
          w1, w3, w2, norm_final, consts, out):
    with ExitStack() as ctx:
        def sb(name, cols, dt=F32):
            return ctx.enter_context(nc.sbuf_tensor(name, [P, cols], dt))

        def sem(name):
            return ctx.enter_context(nc.semaphore(name))

        ring = sb("ring", RING * SLOT)
        ring_at = nc.sbuf_base - 4 * RING * SLOT
        w_hi, w_lo = (nc.alloc_sbuf_tensor_at(name, [P, SLOT], F32R, offset=ring_at + 4 * i * SLOT)
                      for i, name in ((4, "w_hi"), (5, "w_lo")))
        h = sb("h", TT * D)
        xh = sb("xh", TT * D)
        xn_hi = sb("xn_hi", KD * T, F32R)
        xn_lo = sb("xn_lo", KD * T, F32R)
        early0 = nc.alloc_sbuf_tensor_at("early0", [P, SLOT], F32, offset=nc.sbuf_base - 4 * SLOT)
        zone_q1 = sb("zone_q1", 6 * 2 * T)
        zone_at = nc.sbuf_base - 4 * 12 * T
        zone_k1 = sb("zone_k1", 6 * T)
        zone_c = sb("zone_c", 512)
        zone_v1 = sb("zone_v1", TT * 512)
        zone_b = sb("zone_b", 2048)
        early1, early2 = (nc.alloc_sbuf_tensor_at(f"early{i + 1}", [P, SLOT], F32, offset=zone_at + 4 * i * SLOT)
                          for i in range(2))
        assert nc.sbuf_base == zone_at + 4 * 2 * SLOT
        zone_q2 = sb("zone_q2", 4 * 2 * T)
        early = [early0, early1, early2]
        zone_k2 = xh[:, 0:4 * T]
        zone_v2 = xh[:, 4 * T:4 * T + TT * 512]
        zone_y = sb("zone_y", 6 * T)
        zone_p = sb("zone_p", 4 * TT * T)
        m_hi = nc.alloc_sbuf_tensor_at("m_hi", [P, KD * T], F32R, offset=nc.sbuf_base - 4 * KD * T)
        zone_t = sb("zone_t", 4 * TT * T)
        m_lo = nc.alloc_sbuf_tensor_at("m_lo", [P, KD * T], F32R, offset=nc.sbuf_base - 4 * KD * T)
        zone_s = sb("zone_s", 2 * 512)
        cf = sb("cf", C_KEEP)
        cb = sb("cb", NB16, BF16)
        msq = sb("msq", P)
        gains1 = sb("gains1", DEPTH * KD)
        gain1 = sb("gain1", KD)
        cur = sb("cur", N_CUR)
        sm = sb("sm", 640)
        nexp = sb("nexp", 16, I32)

        h3 = h[:, :].rearrange("p (t d) -> p t d", t=TT)
        xh3 = xh[:, :].rearrange("p (t d) -> p t d", t=TT)
        m_hi3 = m_hi[:, :].rearrange("p (c t) -> p c t", c=KD)
        m_lo3 = m_lo[:, :].rearrange("p (c t) -> p c t", c=KD)
        xn_hi3 = xn_hi[:, :].rearrange("p (c t) -> p c t", c=KD)
        xn_lo3 = xn_lo[:, :].rearrange("p (c t) -> p c t", c=KD)
        hT3 = zone_q2[:, :].rearrange("p (c t) -> p c t", c=KD)
        q_of = {"A": zone_q1, "B": zone_q2, "C": zone_q1}
        k_of = {"A": zone_k1[:, :], "B": zone_k2, "C": zone_k1[:, :]}
        q_of = {b: z[:, :].rearrange("p (i m t) -> p i m t", m=2, t=T) for b, z in q_of.items()}
        k_of = {b: z.rearrange("p (i t) -> p i t", t=T) for b, z in k_of.items()}
        v_of = {"A": zone_v1[:, :].rearrange("p (t n) -> p t n", t=TT),
                "B": zone_v2.rearrange("p (t n) -> p t n", t=TT),
                "C": zone_b[:, 0:TT * 768].rearrange("p (t n) -> p t n", t=TT)}
        biasA = [z.rearrange("p (h t k) -> p h t k", h=2, t=TT)
                 for z in (zone_b[:, 0:1024], zone_b[:, 1024:2048], zone_v2, zone_b[:, 0:1024])]
        y_of = {"A": zone_y[:, 0:4 * T], "B": zone_v1[:, :], "C": zone_y[:, 4 * T:6 * T]}
        y_of = {b: z.rearrange("p (i t) -> p i t", t=T) for b, z in y_of.items()}
        prob = zone_p[:, :].rearrange("p (s t k) -> p s t k", s=4, t=TT)
        probT = zone_t[:, :].rearrange("p (s k t) -> p s k t", s=4, k=TT)
        gain2 = cur[:, N_GAIN:N_GAIN + KD]
        vec = cur[0:DH, N_VEC:N_VEC + 4]
        subg, lam = cur[:, N_SUBG:N_SUBG + 1], cur[:, N_LAM:N_LAM + 1]
        rb, wr = cur[:, N_RB:N_RB + 20], cur[:, N_WR:N_WR + KD * 20]
        square = zone_y[:, 4 * T:6 * T].rearrange("p (s t) -> p s t", s=2)
        root = xh[:, 0:4 * T].rearrange("p (i t) -> p i t", t=T)
        fin = zone_p[:, 0:D]
        pre = zone_s[:, :].rearrange("p (s n) -> p s n", s=2)
        ident = cf[:, C_IDENT:C_IDENT + P]
        swap = cf[:, C_SWAP:C_SWAP + P]
        cos2 = cf[:, C_COS:C_COS + T].unsqueeze(1).broadcast_to([P, 2, T])
        sin2 = cf[:, C_SIN:C_SIN + T].unsqueeze(1).broadcast_to([P, 2, T])
        bcol = lambda at, n: cb[:, at - C_KEEP:at - C_KEEP + n]
        tri, identb, oneb = bcol(C_TRI, P), bcol(C_IDB, P), bcol(C_ONE, P)
        maskA = bcol(C_MASKA, TT * T)
        maskC = bcol(C_MASKC, C_GROUPS * TT * T).rearrange("p (g t k) -> p g t k", g=C_GROUPS, t=TT)
        xgT = zone_p[:, D:2 * D].rearrange("p (c s) -> p c s", c=KD)
        y_e = zone_t[:, 0:D]
        hT = zone_t[:, D:D + 512].rearrange("p (f s) -> p f s", f=KF)
        sig = zone_t[:, D + 512:D + 1024]
        hid = zone_y[:, 0:512]
        selT = zone_y[:, 512:768]
        sel = zone_y[:, 768:1024].rearrange("p (t s) -> p t s", t=TT)
        selg = zone_y[:, 1024:1280].rearrange("p (t s) -> p t s", t=TT)
        over_a = zone_q2[:, 0:256].rearrange("p (j e) -> p j e", j=N_OVER)
        over_b = zone_q2[:, 256:512].rearrange("p (j e) -> p j e", j=N_OVER)

        at = [0]

        def small(n):
            at[0] += n
            return sm[:, at[0] - n:at[0]]

        ss, std, rstd = small(2), small(2), small(2)
        ss4 = small(8).rearrange("p (t n) -> p t n", t=TT)
        eps1, eps2, unused = small(1), small(1), small(1)
        lam_pr, lam_e = small(2), small(2)
        nmx = small(4 * 2).rearrange("p (s t) -> p s t", s=4)
        raw = small(4 * 2).rearrange("p (s t) -> p s t", s=4)
        mxc = small(2 * 3).rearrange("p (t g) -> p t g", g=3)
        psum_ = small(4 * 2).rearrange("p (s t) -> p s t", s=4)
        psc = small(2 * 3).rearrange("p (t g) -> p t g", g=3)
        rin = small(4 * 2).rearrange("p (s t) -> p s t", s=4)
        lg = small(2 * 20).rearrange("p (t e) -> p t e", t=TT)
        g4a, g4b, goh = (small(8).rearrange("p (t e) -> p t e", t=TT) for _ in range(3))
        s2 = [small(2) for _ in range(12)]
        e16 = [small(32).rearrange("p (t e) -> p t e", t=TT) for _ in range(5)]
        pos, gat = (small(32).rearrange("p (t e) -> p t e", t=TT) for _ in range(2))
        cnt = small(16)
        exist, cum, zero32 = small(32), small(32), small(32)
        pos_o, gat_o = (small(2 * N_OVER).rearrange("p (t j) -> p t j", t=TT) for _ in range(2))
        eid_o = small(N_OVER)
        asg = sb("asg", 32, BF16)[:, :].rearrange("p (t e) -> p t e", t=TT)
        assert at[0] <= 640, at[0]

        copies = nc.dram_tensor("copies", (GRID_W, DEPTH * A_HEADS * RPB), F32).ap()

        bank = [ctx.enter_context(nc.psum_tensor(f"bank{i}", [P, 512], F32)) for i in range(8)]

        names = """cf_in cb_in copies_in setup_v zero_q1 zero_q2 x_in gains_in small_in bias_in fin_in out_done
            lam_v lam_pe lam_s gain1_v final_v
            sq std_s xh_v turned x_hi_s x_lo_v sq2 ss_v rstd_v xh_s turned_h hT_in_s
            hi_s lo_v v_pe half_pe unit_pe unit_s swap_pe cos_p rope_v vstep bias_p
            score_pe scoreA_v max_v exp_s prob_v turn_pe turn_v pv_pe y_s yb_p inv_v msq_s ms_pe std_b
            branch_pe mix_v mix_p sum_v m_hi_s m_lo_v out_pe h_v
            logit_pe rexp_s rd_v asg_v rank_pe pos_v over_v list_seen
            m_sel_v m_selg_v m_xt m_xgT_v m_h m_sig_s m_hid_v m_ht m_hT_s m_st m_selT_s
            m_y m_y_s m_y_v m_sc m_add_v""".split()
        S = {n: sem(n) for n in names}
        landed_early = [sem(f"landed_early{i}") for i in range(3)]
        landed = [sem(f"landed{i}") for i in range(RING)]

        def slot(n, cols=SLOT):
            return ring[:, n * SLOT:n * SLOT + cols]

        def ring_view(n, k, cols):
            return slot(n, k * cols).rearrange("p (k n) -> p k n", k=k)

        def halves(n):
            role = UNITS[n][1] if n < N_UNITS else "wo"
            return {"v": (2, 512), "v2": (4, 256), "wo": (4, 256)}.get(role, (KD, P))

        def weights_of(n, half):
            if n >= N_UNITS:
                return ring_view(SLOT_OF[AT["wo", n - N_UNITS]], KD, 256)[:, 4 * half:4 * half + 4, :]
            _, role, i, b, t0 = UNITS[n]
            w = ring_view(SLOT_OF[AT["in", b]], KD, min(512, 8448 - 512 * b))
            if role == "v":
                return w[:, 4 * i + 2 * half:4 * i + 2 * half + 2, :]
            if role == "v2":
                return w[:, 4 * half:4 * half + 4, 0:256]
            return w[:, :, (t0 + half) * P:(t0 + half + 1) * P]

        def part_of(parts, n, half):
            at = (n % 2) * 2048 + half * 1024
            return parts[:, at:at + 1024].rearrange("p (k n) -> p k n", k=halves(n)[0])

        block = ctx.enter_context(nc.Block())

        @block.sync
        def _(sp):
            units = sp.alloc_register("sp_units")
            sp.reg_mov(units, 0)
            layers = sp.alloc_register("sp_layers")
            sp.reg_mov(layers, 0)

            def load(n, l):
                kind, b = ORDER[n]
                if kind == "in":
                    cols = min(512, 8448 - 512 * b)
                    src = w_in[l, :, 512 * b:512 * b + cols].rearrange("(k p) n -> p k n", p=P)
                    dst = ring_view(SLOT_OF[n], KD, cols)
                elif kind == "wo":
                    src = w_o[l, :, 256 * b:256 * b + 256].rearrange("(k p) n -> p k n", p=P)
                    dst = ring_view(SLOT_OF[n], KD, 256)
                else:
                    w = {"pa": w_pa, "pb": w_pb, "pc": w_pc}[kind]
                    src = w[l].rearrange("(k p) n -> p k n", p=P)
                    dst = ring_view(SLOT_OF[n], w.shape[1] // P, D)
                sp.dma_start(dst, src).then_inc(landed[SLOT_OF[n]], 16)

            def wait_free(n, l):
                kind, b = ORDER[n]
                if kind == "in":
                    sp.wait_ge(S["lo_v"], l * (2 * N_SPLIT) + 2 * LAST_UNIT[b] + 2)
                elif kind == "wo":
                    sp.wait_ge(S["lo_v"], l * (2 * N_SPLIT) + 2 * (N_UNITS + b) + 2)
                else:
                    sp.wait_ge(S["branch_pe"], l * 12 + {"pa": 4, "pb": 8, "pc": 12}[kind])

            def bias_loads(l, pair):
                for hh in range(2):
                    for r in range(4):
                        tt, p0 = r // 2, 64 * (r % 2)
                        at = (2 * pair + hh) * RPB + (7 - r) * RPB_C + 15
                        src = copies[:, bass.ds(l * A_HEADS * RPB + at, 3 * RPB_C + GRID_W)]
                        src = bass.AP(tensor=src.tensor, offset=src.offset,
                                      ap=[[DEPTH * A_HEADS * RPB - 1, GRID_W], [RPB_C, 4], [1, GRID_W]])
                        dst = biasA[pair][p0:p0 + 64, hh, tt, :].rearrange("p (a b) -> p a b", b=GRID_W)
                        sp.dma_start(dst, src).then_inc(S["bias_in"], 16)

            w1_r = w1.rearrange("l e (k p) f -> (l e) p k f", p=P)
            w3_r = w3.rearrange("l e (k p) f -> (l e) p k f", p=P)
            w2_r = w2.rearrange("l e (k p) f -> (l e) p k f", p=P)

            def load_expert(which, item, e):
                src = (w1_r, w3_r, w2_r)[which][bass.ds(e, 1)].rearrange("o p k f -> p (o k) f")
                k, cols = (KF, D) if which == 2 else (KD, F_EXP)
                sp.dma_start(ring_view(2 * which + item, k, cols), src).then_inc(landed[2 * which + item], 16)

            def load_early(n, l):
                src = (w1_r, w3_r)[n // 2][bass.ds(l * N_EXP + 2 + n % 2, 1)].rearrange("o p k f -> p (o k) f")
                sp.dma_start(early[n][:, :].rearrange("p (k n) -> p k n", k=KD), src).then_inc(landed_early[n], 16)

            def wait_unit(which, last):
                if which < 2:
                    sp.wait_ge(S["m_h"], last * 2 + 1 + which)
                else:
                    sp.wait_ge(S["m_y"], last * 2 + 2)

            sp.dma_start(h3, x[0].rearrange("(t p) d -> p t d", p=P)).then_inc(S["x_in"], 16)
            sp.dma_start(gains1[:, :].rearrange("p (l c) -> p l c", l=DEPTH), norm_mix.rearrange("l (c p) -> p l c", p=P),
                         allow_slow_non_contiguous=True).then_inc(S["gains_in"], 16)
            sp.dma_start(cf[:, :], consts[:, 0:C_KEEP]).then_inc(S["cf_in"], 16)
            for n in range(4):
                load(n, 0)
                if n < DEPTH:
                    sp.dma_start(copies[:, n * A_HEADS * RPB:(n + 1) * A_HEADS * RPB],
                                 na_rpb[n].rearrange("h a b -> (h a b)").partition_broadcast(GRID_W)
                                 ).then_inc(S["copies_in"], 16)
            with sp.Fori(0, DEPTH) as l:
                sp.wait_ge(S["turned"], l * 4 + 4)
                sp.wait_ge(S["copies_in"], DEPTH * 16)
                for pair in range(3):
                    bias_loads(l, pair)
                for n in range(4, len(ORDER)):
                    if n == 8:
                        sp.wait_ge(S["scoreA_v"], l * A_HEADS + 2)
                        bias_loads(l, 3)
                    if n == AT["wo", 0]:
                        sp.wait_ge(S["pv_pe"], l * 12 + 12)
                        for early_n in (1, 2):
                            load_early(early_n, l)
                    wait_free(BEFORE[n], l)
                    load(n, l)
                sp.wait_ge(S["unit_pe"], l * N_UNITS + N_UNITS)
                load_early(0, l)
                for i in sorted(range(4), key=lambda i: LAST_USE[i]):
                    wait_free(LAST_USE[i], l)
                    load_expert(i // 2, i % 2, l * N_EXP + i % 2)
                sp.wait_ge(S["out_pe"], l * 4 + 4)
                for item in range(2):
                    load_expert(2, item, l * N_EXP + item)
                for pair in (1, 2):
                    last = sp.snap(units)
                    for which in range(3):
                        items = [i for i in (1, 0) if pair == 1 or not MISSED[2 * which + i]]
                        if items:
                            wait_unit(which, last)
                        for item in items:
                            loaded = pair + MISSED[2 * which + item]
                            load_expert(which, item, l * N_EXP + loaded * 2 + item)
                    sp.reg_add(units, units, 1)
                with sp.Fori(3, PAIRS) as p:
                    last = sp.snap(units)
                    for which in range(3):
                        wait_unit(which, last)
                        for item in range(2):
                            load_expert(which, item, l * N_EXP + p * 2 + item)
                    sp.reg_add(units, units, 1)
                sp.wait_ge(S["over_v"], l + 1)
                sp.sem_inc(S["list_seen"], 1)
                n_over = sp.value_load(nexp[0:1, 0:1], min_val=0, max_val=N_OVER - 1)
                with sp.If(n_over > 0):
                    with sp.Fori(0, n_over) as j:
                        last = sp.snap(units)
                        e = sp.value_load(nexp[0:1, bass.ds(j + 1, 1)], min_val=0, max_val=N_EXP - 1)
                        for which in range(3):
                            wait_unit(which, last)
                            src = (w1_r, w3_r, w2_r)[which][bass.ds(l * N_EXP + e, 1)].rearrange("o p k f -> p (o k) f")
                            k, cols = (KF, D) if which == 2 else (KD, F_EXP)
                            for part in range(2):
                                sp.dma_start(ring_view(2 * which + part, k // 2, cols),
                                             src[:, part * k // 2:(part + 1) * k // 2, :]).then_inc(
                                                 landed[2 * which + part], 16)
                        sp.reg_add(units, units, 1)
                sp.reg_add(layers, layers, 1)
                with sp.If(l < DEPTH - 1):
                    last = sp.snap(units)
                    following = sp.snap(layers, min_val=1, max_val=DEPTH - 1)
                    for n in range(4):
                        wait_unit(SLOT_OF[n] // 2, last)
                        load(n, following)
                sp.reg_add(units, units, 1)

        @block.gpsimd
        def _(pool):
            nc.gpsimd.memset(zone_q1[:, :], 0.0).then_inc(S["zero_q1"], 1)
            nc.gpsimd.memset(zone_q2[:, :], 0.0).then_inc(S["zero_q2"], 1)
            pool.dma_start(cb[:, :], consts[:, C_KEEP:C_ALL]).then_inc(S["cb_in"], 16)

            def small_loads(l):
                def get(dst, src):
                    pool.dma_start(dst, src, allow_slow_non_contiguous=True).then_inc(S["small_in"], 16)

                def row(a):
                    return a[bass.ds(l, 1), :].rearrange("l n -> (l n)")

                for i, a in enumerate((lam_q1, lam_q2, lam_k1, lam_k2)):
                    get(cur[0:DH, N_VEC + i:N_VEC + i + 1], row(a).unsqueeze(1))
                get(cur[:, N_SUBG:N_SUBG + 1], row(diff_subln).unsqueeze(1))
                get(gain2, row(norm_ffn).rearrange("(c p) -> p c", p=P))
                get(cur[:, N_RB:N_RB + 4], row(router_group_b).partition_broadcast(P))
                get(cur[:, N_RB + 4:N_RB + 20], row(router_expert_b).partition_broadcast(P))
                w = wr.rearrange("p (k e) -> p k e", e=20)
                get(w[:, :, 0:4], router_group_w[bass.ds(l, 1)].rearrange("l (k p) e -> p (l k) e", p=P))
                get(w[:, :, 4:20], router_expert_w[bass.ds(l, 1)].rearrange("l (k p) e -> p (l k) e", p=P))

            def add_mask(pair):
                b = biasA[pair].rearrange("p h t k -> p h (t k)")
                nc.gpsimd.tensor_tensor(b, b, maskA.unsqueeze(1).broadcast_to([P, 2, TT * T]),
                                        ALU.add).then_inc(S["bias_p"], 1)

            pool.wait_ge(S["cb_in"], 16)
            pool.wait_ge(S["cf_in"], 16)
            with pool.Fori(0, DEPTH) as l:
                for kind, br, n in TIMELINE:
                    if kind == "unit" and n == 0:
                        pool.wait_ge(S["turned"], l * 4 + 4)
                        small_loads(l)
                        pool.wait_ge(S["bias_in"], l * BIAS_IN + 3 * 8 * 16)
                        for pair in range(3):
                            add_mask(pair)
                    if kind == "unit" and n == 9:
                        pool.wait_ge(S["bias_in"], l * BIAS_IN + BIAS_IN)
                        add_mask(3)
                    if kind == "swap":
                        i = ROPE.index(n)
                        pool.wait_ge(S["unit_s"], l * N_UNITS + n + 1)
                        if i > 0:
                            pool.wait_ge(S["rope_v"], l * len(ROPE) + i)
                        nc.gpsimd.tensor_tensor(zone_c[:, :].rearrange("p (i t) -> p i t", i=2),
                                                pre[:, n % 2, :].rearrange("p (i t) -> p i t", i=2),
                                                cos2, ALU.mult).then_inc(S["cos_p"], 1)
                    if kind == "inv":
                        for m in (2 * n, 2 * n + 1):
                            pool.wait_ge(S["inv_v"], l * B_HEADS + m + 1)
                            y = y_of["B"][:, (2, 0, 3, 1)[m], :]
                            nc.gpsimd.tensor_tensor(y, y, root[:, m, :], ALU.mult).then_inc(S["yb_p"], 1)
                    if kind == "branch" and br == "B":
                        pool.wait_ge(S["mix_v"], l * 12 + n + 1)
                        i = n % 4
                        m = xh[:, 512 * i:512 * i + 512]
                        nc.gpsimd.tensor_tensor(m, m, pre[:, n % 2, :], ALU.add).then_inc(S["mix_p"], 1)

            pool.wait_ge(S["over_v"], DEPTH)
            pool.dma_start(fin, norm_final[:].partition_broadcast(P)).then_inc(S["fin_in"], 16)

        @block.tensor
        def _(pe):
            units = pe.alloc_register("pe_units")
            pe.reg_mov(units, 0)

            def arrived(n, l):
                i = SLOT_OF[n]
                pe.wait_ge(landed[i], (l * (USES[i] - MISSED[i]) + pe.snap(units) + NTH[n] + 1) * 16)

            def turn_x(l):
                pe.wait_ge(S["xh_v"], l * 2 + 2)
                for b in range(4):
                    for c in (2 * b, 2 * b + 1):
                        for tt in range(TT):
                            at = (c % 2) * T + tt * P
                            last = pe.transpose(bank[b + 2][:, at:at + P], xh3[:, tt, c * P:c * P + P], ident)
                    last.then_inc(S["turned"], 1)

            pe.wait_ge(S["cf_in"], 16)
            with pe.Fori(0, DEPTH) as l:
                turn_x(l)
                for kind, br, n in TIMELINE:
                    if kind == "unit":
                        _, role, i, b, t0 = UNITS[n]
                        if role == "v":
                            passes = [(c, h_, (2 * h_, 2 * h_ + 1)) for h_ in range(2) for c in range(2)]
                        elif role == "v2":
                            passes = [(c, h_, range(4 * h_, 4 * h_ + 4)) for c in range(2) for h_ in range(2)]
                        else:
                            passes = [(c, c, range(KD)) for c in range(2)]
                        arrived_halves = set()
                        for at, (c, half, ks) in enumerate(passes):
                            if role == "v":
                                o = bank[(n - i + c) % 2][:, :]
                                if i == 0 and half == 0:
                                    pe.wait_ge(S["unit_s"], l * N_UNITS + n - 1 + c)
                            else:
                                o = bank[1 if role == "gate" else n % 2][:, c * T:c * T + T]
                                if at == 0 and role == "gate" and n > GATE0:
                                    pe.wait_ge(S["unit_s"], l * N_UNITS + n)
                                elif at == 0 and n >= 2:
                                    pe.wait_ge(S["unit_s"], l * N_UNITS + n - 1)
                            new = half not in arrived_halves
                            arrived_halves.add(half)
                            if new:
                                pe.wait_ge(S["hi_s"], l * (2 * N_SPLIT) + 2 * n + half + 1)
                            first = not (role == "v" and i == 1) and ks[0] == 0
                            done = not (role == "v" and i == 0) and ks[-1] == (3 if role == "v" else KD - 1)
                            w_h, w_l = part_of(w_hi, n, half), part_of(w_lo, n, half)
                            for low in range(2):
                                if low and new:
                                    pe.wait_ge(S["lo_v"], l * (2 * N_SPLIT) + 2 * n + half + 1)
                                for k in ks:
                                    if n == 0 and at == 0 and not low:
                                        pe.wait_ge(S["x_lo_v"], l * KD + k + 1)
                                    for w, x_ in ((w_l, xn_hi3),) if low else ((w_h, xn_hi3), (w_h, xn_lo3)):
                                        kw = k - ks[0]
                                        if role == "v":
                                            lhs, rhs = x_[:, 4 * i + k, c * P:c * P + P], w[:, kw, :]
                                        elif role == "v2":
                                            lhs, rhs = x_[:, k, c * P:c * P + P], w[:, kw, :]
                                        else:
                                            lhs, rhs = w[:, kw, :], x_[:, k, :]
                                        last = pe.matmul(o, lhs, rhs,
                                                         start=(first and k == ks[0] and w is w_h and x_ is xn_hi3),
                                                         stop=(done and low == 1 and k == ks[-1]))
                            if role == "v" and i == 1 and c == 0 and half == 1:
                                last.then_inc(S["v_pe"], 1)
                            elif at == (1 if role == "v" else 0) and role != "v2":
                                last.then_inc(S["half_pe"], 1)
                        last.then_inc(S["unit_pe"], 1)
                    elif kind == "swap":
                        i = ROPE.index(n)
                        pe.wait_ge(S["unit_s"], l * N_UNITS + n + 1)
                        if i > 0:
                            pe.wait_ge(S["rope_v"], l * len(ROPE) + i)
                        pe.matmul(bank[6][:, :], swap, pre[:, n % 2, :], start=True, stop=True).then_inc(S["swap_pe"], 1)
                    elif kind == "lambda":
                        pe.wait_ge(S["lam_v"], l + 1)
                        pe.wait_ge(S["turn_v"], l * N_TURN + A_HEADS)
                        pe.matmul(bank[5][:, 0:2], msq[0:DH, :], lam_pr[0:DH, :], start=True,
                                  stop=True).then_inc(S["lam_pe"], 1)
                    elif kind == "score":
                        if br == "C" and n == 0:
                            pe.wait_ge(S["cb_in"], 16)
                        for part in range({"A": 1, "B": 2, "C": 3}[br]):
                            no = score_no(br, n, part)
                            if br == "A":
                                tile, m, o = n // 2, n % 2, bank[2 + n % 2]
                                if n == 0:
                                    pe.wait_ge(S["unit_s"], l * N_UNITS + 6)
                                if n >= 2:
                                    pe.wait_ge(S["scoreA_v"], l * A_HEADS + n - 1)
                            elif br == "B":
                                tile, m, o = n, part, bank[2 + part]
                                if n == 0 and part == 0:
                                    pe.wait_ge(S["rope_v"], l * len(ROPE) + 4)
                                    pe.wait_ge(S["scoreA_v"], l * A_HEADS + A_HEADS)
                                if n > 0:
                                    pe.wait_ge(S["exp_s"], l * N_SCORE + score_no(br, n - 1, part) + 1)
                            else:
                                tile, m, o = (part * C_HEADS + n) // 2, n % 2, bank[2 + part]
                                if n == 0 and part == 0:
                                    pe.wait_ge(S["rope_v"], l * len(ROPE) + 10)
                                    pe.wait_ge(S["exp_s"], l * N_SCORE + score_no("B", 3, 1) + 1)
                                    pe.wait_ge(S["std_b"], l * 2 + 2)
                                if n > 0:
                                    pe.wait_ge(S["exp_s"], l * N_SCORE + score_no(br, n - 1, part) + 1)
                                for tt in range(TT):
                                    pe.matmul(o[:, tt * T:tt * T + T], identb, maskC[:, part, tt, :],
                                              start=True, stop=False, skip_group_check=True)
                                    last = pe.matmul(o[:, tt * T:tt * T + T], q_of[br][:, tile, m, tt * P:tt * P + P],
                                                     k_of[br][:, tile, :], start=False, stop=True, skip_group_check=True)
                            if br != "C":
                                for tt in range(TT):
                                    last = pe.matmul(o[:, tt * T:tt * T + T], q_of[br][:, tile, m, tt * P:tt * P + P],
                                                     k_of[br][:, tile, :], start=True, stop=True)
                            last.then_inc(S["score_pe"], 1)
                    elif kind == "turn":
                        for part in range(C_GROUPS if br == "C" else 1):
                            no = turn_no(br, n, part)
                            slot_p = {"A": n % 4, "B": 2 * (n % 2), "C": part}[br]
                            o = {"A": bank[4 + n % 2], "B": bank[5], "C": bank[5 + part % 2]}[br]
                            pe.wait_ge(S["prob_v"], l * N_TURN + no + 1)
                            if br == "A" and n >= 2:
                                pe.wait_ge(S["turn_v"], l * N_TURN + no - 1)
                            elif br == "B":
                                pe.wait_ge(S["turn_v"], l * N_TURN + no)
                                if n == 0:
                                    pe.wait_ge(S["lam_s"], l + 1)
                            elif br == "C":
                                pe.wait_ge(S["turn_v"], l * N_TURN + no - (1 if part == 2 or part == 1 else 0))
                            for kt in range(TT):
                                for tt in range(TT):
                                    at = kt * T + tt * P
                                    last = pe.transpose(o[:, at:at + P], prob[:, slot_p, tt, kt * P:kt * P + P], ident)
                            last.then_inc(S["turn_pe"], 1)
                    elif kind == "pv":
                        if br == "A":
                            o = bank[7]
                            pe.wait_ge(S["turn_v"], l * N_TURN + turn_no("A", 2 * n + 1) + 1)
                            if n > 0:
                                pe.wait_ge(S["y_s"], l * 8 + n)
                            for kt in range(TT):
                                for m in range(2):
                                    hd = 2 * n + m
                                    last = pe.matmul(o[m * DH:m * DH + DH, 0:T], v_of["A"][:, kt, hd * DH:hd * DH + DH],
                                                     probT[:, hd % 4, kt, :], start=(kt == 0), stop=(kt == TT - 1))
                        elif br == "B":
                            o = bank[7 if n % 2 == 0 else 4]
                            pe.wait_ge(S["turn_v"], l * N_TURN + turn_no("B", n) + 1)
                            if n == 0:
                                pe.wait_ge(S["y_s"], l * 8 + 4)
                                pe.wait_ge(S["unit_s"], l * N_UNITS + 12)
                            if n >= 2:
                                pe.wait_ge(S["msq_s"], l * B_HEADS + n - 1)
                            for kt in range(TT):
                                last = pe.matmul(o[:, 0:T], v_of["B"][:, kt, n * P:n * P + P], probT[:, n % 4, kt, :],
                                                 start=(kt == 0), stop=(kt == TT - 1))
                        else:
                            o = bank[7]
                            pe.wait_ge(S["turn_v"], l * N_TURN + turn_no("C", n, 2) + 1)
                            if n == 0:
                                pe.wait_ge(S["unit_s"], l * N_UNITS + GATE0)
                            else:
                                pe.wait_ge(S["y_s"], l * 8 + 4 + n)
                            m = n % 2
                            for g in range(C_GROUPS):
                                hd = g * C_HEADS + n
                                for kt in range(TT):
                                    last = pe.matmul(o[m * DH:m * DH + DH, 0:T], v_of["C"][:, kt, hd * DH:hd * DH + DH],
                                                     probT[:, g, kt, :], start=(g == 0 and kt == 0),
                                                     stop=(g == C_GROUPS - 1 and kt == TT - 1))
                        last.then_inc(S["pv_pe"], 1)
                    elif kind == "ms":
                        o = bank[7 if n % 2 == 0 else 4]
                        pe.wait_ge(S["msq_s"], l * B_HEADS + n + 1)
                        at = T - n // 2 * T
                        pe.matmul(o[:, at:at + T], msq[:, :], square[:, n % 2, :], start=True, stop=True,
                                  skip_group_check=True).then_inc(S["ms_pe"], 1)
                    elif kind == "branch":
                        w_at = AT[{"A": "pa", "B": "pb", "C": "pc"}[br], 0]
                        kk = 2 if br == "C" else 4
                        w = ring_view(SLOT_OF[w_at], kk, D)
                        if n % 4 == 0:
                            arrived(w_at, l)
                        if n == 0:
                            pe.wait_ge(S["unit_s"], l * N_UNITS + GATE0)
                            pe.wait_ge(S["y_s"], l * 8 + 4)
                        if n == 4:
                            pe.wait_ge(S["yb_p"], l * B_HEADS + 4)
                        if n == 8:
                            pe.wait_ge(S["y_s"], l * 8 + 8)
                        if n > 0:
                            pe.wait_ge(S["mix_v"], l * 12 + n)
                        for c2 in range(2):
                            c = 2 * (n % 4) + c2
                            for k in range(kk):
                                last = pe.matmul(bank[0][:, c2 * T:c2 * T + T], w[:, k, c * P:c * P + P],
                                                 y_of[br][:, k, :], start=(k == 0), stop=(k == kk - 1))
                        last.then_inc(S["branch_pe"], 1)
                    elif kind == "out":
                        u = N_UNITS + n
                        if n == 1:
                            pe.wait_ge(S["unit_s"], l * N_UNITS + N_UNITS)
                        if n >= 2:
                            pe.wait_ge(S["h_v"], l * 4 + n - 1)
                        for tt in range(TT):
                            o = bank[n % 2][:, tt * 256:tt * 256 + 256]
                            for half in range(2):
                                w_h, w_l = part_of(w_hi, u, half), part_of(w_lo, u, half)
                                if tt == 0:
                                    pe.wait_ge(S["hi_s"], l * (2 * N_SPLIT) + 2 * u + half + 1)
                                for k in range(4 * half, 4 * half + 4):
                                    if n == 0 and tt == 0 and k % 2 == 0:
                                        pe.wait_ge(S["m_lo_v"], l * 4 + k // 2 + 1)
                                        pe.wait_ge(S["mix_v"], l * 12 + 12)
                                    for m in (m_hi3, m_lo3):
                                        pe.matmul(o, m[:, k, tt * P:tt * P + P], w_h[:, k - 4 * half, :],
                                                  start=(k == 0 and m is m_hi3), stop=False)
                                if tt == 0:
                                    pe.wait_ge(S["lo_v"], l * (2 * N_SPLIT) + 2 * u + half + 1)
                                for k in range(4 * half, 4 * half + 4):
                                    last = pe.matmul(o, m_hi3[:, k, tt * P:tt * P + P], w_l[:, k - 4 * half, :],
                                                     start=False, stop=(k == KD - 1))
                        last.then_inc(S["out_pe"], 1)
                    elif kind == "turn_h":
                        pe.wait_ge(S["h_v"], l * 4 + n + 1)
                        for c in (2 * n, 2 * n + 1):
                            for tt in range(TT):
                                at = (c % 2) * T + tt * P
                                last = pe.transpose(bank[2 + n][:, at:at + P], h3[:, tt, c * P:c * P + P], ident)
                        last.then_inc(S["turned_h"], 1)
                    elif kind == "logit":
                        pe.wait_ge(S["hT_in_s"], l * 4 + n + 1)
                        for tt in range(TT):
                            for k in (2 * n, 2 * n + 1):
                                last = pe.matmul(bank[6 + tt][:, 0:20], hT3[:, k, tt * P:tt * P + P],
                                                 wr[:, k * 20:k * 20 + 20], start=(k == 0), stop=(k == KD - 1))
                        if n == 3:
                            last.then_inc(S["logit_pe"], 1)

                pe.wait_ge(S["asg_v"], l + 1)
                pe.matmul(bank[5][:, 0:16], tri, asg[:, 0, :], start=True, stop=True)
                pe.matmul(bank[5][:, 16:32], oneb, asg[:, 0, :], start=True, stop=False, skip_group_check=True)
                pe.matmul(bank[5][:, 16:32], tri, asg[:, 1, :], start=False, stop=True, skip_group_check=True)
                pe.matmul(bank[5][:, 32:48], oneb, asg[:, 0, :], start=True, stop=False, skip_group_check=True)
                pe.matmul(bank[5][:, 32:48], oneb, asg[:, 1, :], start=False, stop=True,
                          skip_group_check=True).then_inc(S["rank_pe"], 1)

                def gather(g, b, first=False):
                    if b == 0:
                        pe.wait_ge(S["m_sel_v"], g + 1)
                        if first:
                            pe.wait_ge(S["xh_s"], l * 2 + 2)
                        else:
                            pe.wait_ge(S["m_xgT_v"], g * 2)
                    for c in range(4 * b, 4 * b + 4):
                        for tt in range(TT):
                            last = pe.matmul(bank[b][:, (c % 4) * P:(c % 4) * P + P], xh3[:, tt, c * P:c * P + P],
                                             sel[:, tt, :], start=(tt == 0), stop=(tt == TT - 1))
                    last.then_inc(S["m_xt"], 1)

                def landed_unit(which, r, l, no):
                    for i in range(2):
                        n = 2 * which + i
                        if no == 1 and MISSED[n]:
                            pe.wait_ge(landed_early[n], (l + 1) * 16)
                        else:
                            passed = MISSED[n] if no else 0
                            pe.wait_ge(landed[n], (l * (USES[n] - MISSED[n]) + r + USES[n] - passed + 1) * 16)

                def hidden(r, l, pair, no):
                    pe.wait_ge(S["m_xgT_v"], r * 2 + l * 2 + 2)
                    if no == 0:
                        pe.wait_ge(S["pos_v"], l + 1)
                    else:
                        pe.wait_ge(S["m_hid_v"], r)
                    for which in range(2):
                        landed_unit(which, r, l, no)
                        o = bank[4 + which]
                        if pair:
                            w = [ring_view(2 * which + i, KD, F_EXP) for i in range(2)]
                            for i in range(2):
                                if no == 1 and MISSED[2 * which + i]:
                                    w[i] = early[2 * which + i][:, :].rearrange("p (k n) -> p k n", k=KD)
                            for k in range(KD):
                                for i in range(2):
                                    last = pe.matmul(o[i * CAP:i * CAP + CAP, :], xgT[:, k, i * CAP:i * CAP + CAP],
                                                     w[i][:, k, :], start=(k == 0), stop=(k == KD - 1))
                        else:
                            w = [ring_view(2 * which + i, KD // 2, F_EXP) for i in range(2)]
                            for k in range(KD):
                                last = pe.matmul(o[:, :], xgT[:, k, :], w[k // 4][:, k % 4, :],
                                                 start=(k == 0), stop=(k == KD - 1))
                        last.then_inc(S["m_h"], 1)

                def turn_hidden(r, l, first=False):
                    pe.wait_ge(S["m_hid_v"], r + 1)
                    if not first:
                        pe.wait_ge(S["m_add_v"], r * 4)
                    for f in range(KF):
                        last = pe.transpose(bank[2][:, f * P:f * P + P], hid[:, f * P:f * P + P], ident)
                    last.then_inc(S["m_ht"], 1)
                    pe.wait_ge(S["m_selg_v"], r + l + 1)
                    for tt in range(TT):
                        last = pe.transpose(bank[3][:, tt * P:tt * P + P], selg[:, tt, :], ident)
                    last.then_inc(S["m_st"], 1)

                def expert_out(r, l, pair, first=False):
                    landed_unit(2, r, l, 2)
                    pe.wait_ge(S["m_hT_s"], r + 1)
                    if not first:
                        pe.wait_ge(S["m_y_s"], r)
                        pe.wait_ge(S["m_y_v"], r)
                    for dh in range(2):
                        for f in range(KF):
                            if pair:
                                for i in range(2):
                                    last = pe.matmul(bank[6 + dh][i * CAP:i * CAP + CAP, :], hT[:, f, i * CAP:i * CAP + CAP],
                                                     ring_view(4 + i, KF, D)[:, f, dh * 512:dh * 512 + 512],
                                                     start=(f == 0), stop=(f == KF - 1))
                            else:
                                last = pe.matmul(bank[6 + dh][:, :], hT[:, f, :],
                                                 ring_view(4 + f // 2, KF // 2, D)[:, f % 2, dh * 512:dh * 512 + 512],
                                                 start=(f == 0), stop=(f == KF - 1))
                        last.then_inc(S["m_y"], 1)

                def scatter(r):
                    pe.wait_ge(S["m_selT_s"], r + 1)
                    for dh in range(2):
                        pe.wait_ge(S["m_y_v" if dh else "m_y_s"], r + 1)
                        for tt in range(TT):
                            if dh:
                                pe.wait_ge(S["m_add_v"], r * 4 + tt + 1)
                            pe.matmul(bank[2 + tt][:, :], selT[:, tt * P:tt * P + P], y_e[:, dh * 512:dh * 512 + 512],
                                      start=True, stop=True).then_inc(S["m_sc"], 1)

                def unit(r, l, pair, no):
                    hidden(r, l, pair, no)
                    gather(r + l + 1, 0)
                    turn_hidden(r, l, no == 0)
                    gather(r + l + 1, 1)
                    expert_out(r, l, pair, no == 0)
                    scatter(r)

                g = pe.snap(units) + l
                for b in range(2):
                    gather(g, b, first=True)
                for no in range(2):
                    unit(pe.snap(units), l, True, no)
                    pe.reg_add(units, units, 1)
                with pe.Fori(2, PAIRS):
                    unit(pe.snap(units), l, True, 2)
                    pe.reg_add(units, units, 1)
                pe.wait_ge(S["over_v"], l + 1)
                pe.sem_inc(S["list_seen"], 1)
                n_over = pe.value_load(nexp[0:1, 0:1], min_val=0, max_val=N_OVER - 1)
                with pe.If(n_over > 0):
                    with pe.Fori(0, n_over):
                        unit(pe.snap(units), l, False, 2)
                        pe.reg_add(units, units, 1)

        @block.scalar
        def _(act):
            units = act.alloc_register("act_units")
            act.reg_mov(units, 0)

            def squares(n_done):
                for tt in range(TT):
                    last = nc.scalar.activation(xh3[:, tt, :], h3[:, tt, :], ACT.Square,
                                                accum_out=ss[:, tt:tt + 1])
                last.then_inc(S["sq"], 1)
                act.wait_ge(S["sq"], n_done + 1)
                nc.scalar.activation(std, ss, ACT.Sqrt, bias=eps1, scale=1.0 / D).then_inc(S["std_s"], 1)

            def split_hi(n, half, l):
                at = AT["in", UNITS[n][3]] if n < N_UNITS else AT["wo", n - N_UNITS]
                i = SLOT_OF[at]
                if half == 0 and (n == 0 or n >= N_UNITS or UNITS[n][3] != UNITS[n - 1][3]):
                    act.wait_ge(landed[i], (l * (USES[i] - MISSED[i]) + act.snap(units) + NTH[at] + 1) * 16)
                if n - 2 >= N_UNITS:
                    act.wait_ge(S["out_pe"], l * 4 + n - 2 - N_UNITS + 1)
                elif n >= 2 and half == 0 and UNITS[n - 2][1] != "v2":
                    act.wait_ge(S["half_pe"], l * (N_UNITS - 1) + FIRSTS[n - 2])
                elif n >= 2:
                    act.wait_ge(S["unit_pe"], l * N_UNITS + n - 1)
                nc.scalar.activation(part_of(w_hi, n, half), weights_of(n, half), ACT.Copy).then_inc(S["hi_s"], 1)

            def load_table(f):
                nc.scalar.activation(unused, eps1, f)

            act.wait_ge(S["setup_v"], 4)
            load_table(ACT.Sqrt)
            act.wait_ge(S["x_in"], 16)
            squares(0)
            with act.Fori(0, DEPTH) as l:
                split_hi(0, 0, l)
                split_hi(0, 1, l)
                act.wait_ge(S["gain1_v"], l + 1)
                for c in range(KD):
                    if c % 2 == 0:
                        act.wait_ge(S["turned"], l * 4 + c // 2 + 1)
                    nc.scalar.activation(xn_hi3[:, c, :], bank[2 + c // 2][:, (c % 2) * T:(c % 2) * T + T], ACT.Copy,
                                         scale=gain1[:, c:c + 1]).then_inc(S["x_hi_s"], 1)
                split_hi(1, 0, l)
                split_hi(1, 1, l)
                for kind, br, n in TIMELINE:
                    if kind == "unit":
                        _, role, i, b, t0 = UNITS[n]
                        o = bank[1] if role == "gate" else bank[n % 2]
                        split_hi(n + 2, 0, l)
                        if role not in ("v", "gate") or i == 0 and role == "v":
                            split_hi(n + 2, 1, l)
                        if role == "v" and i == 0:
                            continue
                        if role != "v":
                            act.wait_ge(S["unit_pe"], l * N_UNITS + n + 1)
                        if role == "gate":
                            g = i
                            if g == 0:
                                act.wait_ge(S["rope_v"], l * len(ROPE) + 10)
                            if g >= 2:
                                act.wait_ge(S["mix_v"], l * 12 + g - 1)
                            if 4 <= g - 2 < 8:
                                act.wait_ge(S["mix_p"], l * 4 + g - 2 - 4 + 1)
                            elif g - 2 >= 8:
                                act.wait_ge(S["sum_v"], l * 4 + g - 2 - 8 + 1)
                            nc.scalar.activation(pre[:, g % 2, :], o[:, :], ACT.Tanh,
                                                 scale=0.5).then_inc(S["unit_s"], 1)
                            split_hi(n + 2, 1, l)
                        elif br == "A" and role == "q":
                            o2 = o[:, :].rearrange("p (i t) -> p i t", i=2)
                            if i == 0:
                                act.wait_ge(S["zero_q1"], l + 1)
                            nc.scalar.activation(q_of["A"][0:64, 2 * i:2 * i + 2, 0, :], o2[0:64], ACT.Copy)
                            nc.scalar.activation(q_of["A"][64:128, 2 * i:2 * i + 2, 1, :], o2[64:128],
                                                 ACT.Copy).then_inc(S["unit_s"], 1)
                        elif br == "A" and role == "k":
                            nc.scalar.activation(zone_k1[:, 512 * i:512 * i + 512], o[:, :], ACT.Copy).then_inc(S["unit_s"], 1)
                        elif role in "qk":
                            j = ROPE.index(n)
                            if j >= 2:
                                act.wait_ge(S["rope_v"], l * len(ROPE) + j - 1)
                            nc.scalar.activation(pre[:, n % 2, :], o[:, :], ACT.Copy).then_inc(S["unit_s"], 1)
                        elif role == "v":
                            if br != "A":
                                act.wait_ge(S["scoreA_v"], l * A_HEADS + A_HEADS)
                            act.wait_ge(S["v_pe"], l * 3 + "ABC".index(br) + 1)
                            nc.scalar.activation(v_of[br][:, 0, 0:512], bank[(n - 1) % 2][:, :],
                                                 ACT.Copy).then_inc(S["unit_s"], 1)
                            act.wait_ge(S["unit_pe"], l * N_UNITS + n + 1)
                            nc.scalar.activation(v_of[br][:, 1, 0:512], o[:, :], ACT.Copy).then_inc(S["unit_s"], 1)
                            split_hi(n + 2, 1, l)
                        else:
                            nc.scalar.activation(v_of["C"][:, :, 512:768], o[:, :].rearrange("p (t n) -> p t n", t=TT),
                                                 ACT.Copy).then_inc(S["unit_s"], 1)
                    elif kind == "lambda":
                        act.wait_ge(S["lam_pe"], l + 1)
                        nc.scalar.activation(lam_e, bank[5][:, 0:2], ACT.Exp, scale=float(P)).then_inc(S["lam_s"], 1)
                    elif kind == "score":
                        for part in range({"A": 1, "B": 2, "C": 3}[br]):
                            no = score_no(br, n, part)
                            act.wait_ge(S["max_v"], l * N_MAX + max_no(br, n, part) + 1)
                            if br == "A":
                                for tt in range(TT):
                                    last = nc.scalar.activation(prob[:, n % 4, tt, :], prob[:, n % 4, tt, :], ACT.Exp,
                                                                bias=nmx[:, n % 4, tt:tt + 1],
                                                                accum_out=psum_[:, n % 4, tt:tt + 1])
                            else:
                                s = 2 * (n % 2) + part if br == "B" else part
                                if br == "B":
                                    m = turn_no("A", 4 + s) if n < 2 else turn_no("B", n - 2)
                                    act.wait_ge(S["turn_pe"], l * N_TURN + m + 1)
                                elif n == 0:
                                    act.wait_ge(S["turn_pe"], l * N_TURN + turn_no("B", 3) + 1)
                                else:
                                    act.wait_ge(S["turn_pe"], l * N_TURN + turn_no("C", n - 1, part) + 1)
                                o = bank[2 + part]
                                for tt in range(TT):
                                    bias = nmx[:, s, tt:tt + 1] if br == "B" else nmx[:, n % 4, tt:tt + 1]
                                    acc = psum_[:, s, tt:tt + 1] if br == "B" else psc[:, tt, part:part + 1]
                                    last = nc.scalar.activation(prob[:, s, tt, :], o[:, tt * T:tt * T + T], ACT.Exp,
                                                                bias=bias, scale=SCALE, accum_out=acc)
                            last.then_inc(S["exp_s"], 1)
                    elif kind == "pv":
                        act.wait_ge(S["pv_pe"], l * 12 + pv_no(br, n) + 1)
                        if br == "A":
                            nc.scalar.activation(y_of["A"][:, n, :], bank[7][:, 0:T], ACT.Copy).then_inc(S["y_s"], 1)
                        elif br == "C":
                            m = n % 2
                            nc.scalar.activation(y_of["C"][m * DH:m * DH + DH, n // 2, :], bank[7][m * DH:m * DH + DH, 0:T],
                                                 ACT.Copy).then_inc(S["y_s"], 1)
                        else:
                            o = bank[7 if n % 2 == 0 else 4]
                            if n >= 2:
                                act.wait_ge(S["ms_pe"], l * B_HEADS + n - 1)
                            nc.scalar.activation(y_of["B"][:, n, :], o[:, 0:T], ACT.Copy, scale=subg)
                            nc.scalar.activation(square[:, n % 2, :], o[:, 0:T], ACT.Square).then_inc(S["msq_s"], 1)
                    elif kind == "norm":
                        act.wait_ge(S["ms_pe"], l * B_HEADS + 4)
                        for m in range(2):
                            nc.scalar.activation(root[:, 2 * m:2 * m + 2, :].rearrange("p i t -> p (i t)"),
                                                 bank[4 if m else 7][:, :], ACT.Sqrt, bias=eps2).then_inc(S["std_b"], 1)
                        load_table(ACT.Exp)
                    elif kind == "m_parts":
                        act.wait_ge(S["sum_v"], l * 4 + n + 1)
                        nc.scalar.activation(m_hi[:, 512 * n:512 * n + 512], xh[:, 512 * n:512 * n + 512],
                                             ACT.Copy).then_inc(S["m_hi_s"], 1)
                        if n == 3:
                            load_table(ACT.Sqrt)
                    elif kind == "out":
                        if n < 2:
                            split_hi(N_UNITS + n + 2, 0, l)
                            split_hi(N_UNITS + n + 2, 1, l)
                        act.wait_ge(S["h_v"], l * 4 + n + 1)
                        for tt in range(TT):
                            at = tt * D + 256 * n
                            last = nc.scalar.activation(xh[:, at:at + 256], h[:, at:at + 256], ACT.Square,
                                                        accum_out=ss4[:, tt, n:n + 1])
                        last.then_inc(S["sq2"], 1)
                    elif kind == "turn_h":
                        act.wait_ge(S["turned_h"], l * 4 + n + 1)
                        nc.scalar.activation(zone_q2[:, 512 * n:512 * n + 512], bank[2 + n][:, :],
                                             ACT.Copy).then_inc(S["hT_in_s"], 1)

                act.wait_ge(S["ss_v"], l + 1)
                nc.scalar.activation(std, ss, ACT.Sqrt, bias=eps1, scale=1.0 / D).then_inc(S["std_s"], 1)
                act.wait_ge(S["rstd_v"], l + 1)
                for tt in range(TT):
                    nc.scalar.activation(xh3[:, tt, :], h3[:, tt, :], ACT.Copy,
                                         scale=rstd[:, tt:tt + 1]).then_inc(S["xh_s"], 1)
                act.wait_ge(S["rd_v"], l * 2 + 1)
                nc.scalar.activation(g4b, g4a, ACT.Exp).then_inc(S["rexp_s"], 1)
                act.wait_ge(S["rd_v"], l * 2 + 2)
                nc.scalar.activation(s2[3], s2[2], ACT.Exp).then_inc(S["rexp_s"], 1)

                def gate(r):
                    act.wait_ge(S["m_h"], r * 2 + 1)
                    nc.scalar.activation(sig, bank[4][:, :], ACT.Sigmoid).then_inc(S["m_sig_s"], 1)

                def turned_out(r):
                    act.wait_ge(S["m_ht"], r + 1)
                    nc.scalar.activation(zone_t[:, D:D + 512], bank[2][:, :], ACT.Copy).then_inc(S["m_hT_s"], 1)
                    act.wait_ge(S["m_st"], r + 1)
                    nc.scalar.activation(selT, bank[3][:, 0:T], ACT.Copy).then_inc(S["m_selT_s"], 1)

                def y_out(r):
                    act.wait_ge(S["m_y"], r * 2 + 1)
                    nc.scalar.activation(y_e[:, 0:512], bank[6][:, :], ACT.Copy).then_inc(S["m_y_s"], 1)

                def unit(r):
                    gate(r)
                    turned_out(r)
                    y_out(r)

                with act.Fori(0, PAIRS):
                    unit(act.snap(units))
                    act.reg_add(units, units, 1)
                act.wait_ge(S["over_v"], l + 1)
                act.sem_inc(S["list_seen"], 1)
                n_over = act.value_load(nexp[0:1, 0:1], min_val=0, max_val=N_OVER - 1)
                with act.If(n_over > 0):
                    with act.Fori(0, n_over):
                        unit(act.snap(units))
                        act.reg_add(units, units, 1)
                load_table(ACT.Sqrt)
                act.wait_ge(S["m_add_v"], act.snap(units) * 4)
                squares(l + 1)

            for tt in range(TT):
                act.wait_ge(S["final_v"], tt + 1)
                act.dma_start(out[0, tt * P:tt * P + P, :], xh3[:, tt, :]).then_inc(S["out_done"], 16)
            act.wait_ge(S["out_done"], TT * 16)

        @block.vector
        def _(dve):
            units = dve.alloc_register("dve_units")
            steps = dve.alloc_register("dve_steps")
            dve.reg_mov(units, 0)
            dve.reg_mov(steps, 0)
            link, base = [0], [0]

            def chain(ins):
                link[0] += 1
                ins.then_inc(S["vstep"], 1)
                dve.wait_ge(S["vstep"], base[0] + link[0])

            def begin():
                base[0] = dve.snap(steps)

            def chained():
                if link[0]:
                    dve.reg_add(steps, steps, link[0])
                link[0] = 0

            V = nc.vector
            V.memset(msq[:, :], 1.0 / P).then_inc(S["setup_v"], 1)
            V.memset(zero32, 0.0).then_inc(S["setup_v"], 1)
            V.memset(eps1, NORM_EPS).then_inc(S["setup_v"], 1)
            V.memset(eps2, SUBLN_EPS).then_inc(S["setup_v"], 1)
            begin()
            def bc(ap, shape):
                return ap.broadcast_to(shape)

            def split_lo(n, l):
                for half in range(2):
                    dve.wait_ge(S["hi_s"], l * (2 * N_SPLIT) + 2 * n + half + 1)
                    V.tensor_tensor(part_of(w_lo, n, half), weights_of(n, half), part_of(w_hi, n, half).bitcast(F32),
                                    ALU.subtract).then_inc(S["lo_v"], 1)

            with dve.Fori(0, DEPTH) as l:
                begin()
                dve.wait_ge(S["std_s"], l * 2 + 1)
                chain(V.reciprocal(rstd, std))
                for tt in range(TT):
                    V.tensor_scalar(xh3[:, tt, :], h3[:, tt, :], rstd[:, tt:tt + 1], None, ALU.mult).then_inc(S["xh_v"], 1)
                dve.wait_ge(S["cf_in"], 16)
                dve.wait_ge(S["gains_in"], 16)
                V.tensor_copy(gain1[:, :], gains1[:, bass.ds(l * KD, KD)]).then_inc(S["gain1_v"], 1)
                split_lo(0, l)
                for c in range(KD):
                    if c % 2 == 0:
                        dve.wait_ge(S["x_hi_s"], l * KD + c + 2)
                    if c == 0:
                        dve.wait_ge(S["gain1_v"], l + 1)
                    V.scalar_tensor_tensor(xn_lo3[:, c, :], bank[2 + c // 2][:, (c % 2) * T:(c % 2) * T + T],
                                           gain1[:, c:c + 1], xn_hi3[:, c, :].bitcast(F32), ALU.mult,
                                           ALU.subtract).then_inc(S["x_lo_v"], 1)
                split_lo(1, l)

                for kind, br, n in TIMELINE:
                    if kind == "unit":
                        split_lo(n + 2, l)
                    elif kind == "m_parts":
                        dve.wait_ge(S["m_hi_s"], l * 4 + n + 1)
                        V.tensor_tensor(m_lo[:, 512 * n:512 * n + 512], xh[:, 512 * n:512 * n + 512],
                                        m_hi[:, 512 * n:512 * n + 512].bitcast(F32), ALU.subtract).then_inc(S["m_lo_v"], 1)
                    elif kind == "vectors":
                        dve.wait_ge(S["small_in"], (l + 1) * N_LOADS * 16)
                        chain(V.tensor_tensor(subg, subg, cf[:, bass.ds(l * 2 + (C_LINIT + 1), 1)], ALU.mult))
                        V.tensor_tensor(lam_pr[0:DH, :], vec[:, 0:2], vec[:, 2:4], ALU.mult).then_inc(S["lam_v"], 1)
                        w = wr.rearrange("p (k e) -> p k e", e=20)
                        chain(V.tensor_tensor(w, w, bc(gain2.unsqueeze(2), [P, KD, 20]), ALU.mult))
                    elif kind == "soft" and br == "B" and n == 0:
                        dve.wait_ge(S["lam_s"], l + 1)
                        chain(V.tensor_tensor(lam, lam_e[:, 0:1], lam_e[:, 1:2], ALU.subtract))
                        chain(V.tensor_tensor(lam, lam, cf[:, bass.ds(l * 2 + C_LINIT, 1)], ALU.add))
                    if kind == "swap":
                        i = ROPE.index(n)
                        if i == 0:
                            dve.wait_ge(S["zero_q2"], l + 1)
                        b_, role, pr, _, _ = UNITS[n]
                        dve.wait_ge(S["swap_pe"], l * len(ROPE) + i + 1)
                        dve.wait_ge(S["cos_p"], l * len(ROPE) + i + 1)
                        o2 = bank[6][:, :].rearrange("p (i t) -> p i t", i=2)
                        x2 = pre[:, n % 2, :].rearrange("p (i t) -> p i t", i=2)
                        c2 = zone_c[:, :].rearrange("p (i t) -> p i t", i=2)
                        chain(V.tensor_tensor(x2, o2, sin2, ALU.mult))
                        if role == "q":
                            V.tensor_tensor(q_of[b_][0:64, 2 * pr:2 * pr + 2, 0, :], x2[0:64], c2[0:64], ALU.add)
                            V.tensor_tensor(q_of[b_][64:128, 2 * pr:2 * pr + 2, 1, :], x2[64:128], c2[64:128],
                                            ALU.add).then_inc(S["rope_v"], 1)
                        else:
                            V.tensor_tensor(k_of[b_][:, 2 * pr:2 * pr + 2, :], x2, c2, ALU.add).then_inc(S["rope_v"], 1)
                    elif kind == "score" and br == "A":
                        s = n % 4
                        if n % 2 == 0:
                            dve.wait_ge(S["bias_p"], l * 4 + n // 2 + 1)
                        dve.wait_ge(S["score_pe"], l * N_SCORE + n + 1)
                        if n >= 4:
                            dve.wait_ge(S["turn_pe"], l * N_TURN + n - 3)
                        V.scalar_tensor_tensor(prob[:, s, :, :].rearrange("p t k -> p (t k)"), bank[2 + n % 2][:, :], SCALE,
                                               biasA[n // 2][:, n % 2, :, :].rearrange("p t k -> p (t k)"),
                                               ALU.mult, ALU.add).then_inc(S["scoreA_v"], 1)
                        dve.wait_ge(S["scoreA_v"], l * A_HEADS + n + 1)
                        V.tensor_reduce(nmx[:, s, :], prob[:, s, :, :], AX_X, ALU.max, negate=True).then_inc(S["max_v"], 1)
                    elif kind == "score":
                        for part in range({"B": 2, "C": 3}[br]):
                            dve.wait_ge(S["score_pe"], l * N_SCORE + score_no(br, n, part) + 1)
                            s = 2 * (n % 2) + part if br == "B" else n % 4
                            o = bank[2 + part][:, :].rearrange("p (t k) -> p t k", t=TT)
                            if br == "B":
                                chain(V.tensor_reduce(raw[:, s, :], o, AX_X, ALU.max, negate=True))
                                V.tensor_scalar(nmx[:, s, :], raw[:, s, :], SCALE, None, ALU.mult).then_inc(S["max_v"], 1)
                            else:
                                chain(V.tensor_reduce(mxc[:, :, part:part + 1], o, AX_X, ALU.max))
                        if br == "C":
                            chain(V.tensor_reduce(raw[:, s, :], mxc, AX_X, ALU.max, negate=True))
                            V.tensor_scalar(nmx[:, s, :], raw[:, s, :], SCALE, None, ALU.mult).then_inc(S["max_v"], 1)
                    elif kind == "soft":
                        for b_, m in [(br, n)]:
                            if b_ == "A":
                                s = m % 4
                                dve.wait_ge(S["exp_s"], l * N_SCORE + m + 1)
                                chain(V.reciprocal(rin[:, s, :], psum_[:, s, :]))
                                for tt in range(TT):
                                    last = V.tensor_scalar(prob[:, s, tt, :], prob[:, s, tt, :], rin[:, s, tt:tt + 1],
                                                           None, ALU.mult)
                                last.then_inc(S["prob_v"], 1)
                            elif b_ == "B":
                                s = 2 * (m % 2)
                                dve.wait_ge(S["exp_s"], l * N_SCORE + score_no("B", m, 1) + 1)
                                chain(V.reciprocal(rin[:, s:s + 2, :], psum_[:, s:s + 2, :]))
                                chain(V.tensor_scalar(rin[:, s + 1, :], rin[:, s + 1, :], lam, None, ALU.mult))
                                for tt in range(TT):
                                    chain(V.tensor_scalar(prob[:, s + 1, tt, :], prob[:, s + 1, tt, :],
                                                          rin[:, s + 1, tt:tt + 1], None, ALU.mult))
                                for tt in range(TT):
                                    last = V.scalar_tensor_tensor(prob[:, s, tt, :], prob[:, s, tt, :],
                                                                  rin[:, s, tt:tt + 1], prob[:, s + 1, tt, :],
                                                                  ALU.mult, ALU.subtract)
                                last.then_inc(S["prob_v"], 1)
                            else:
                                dve.wait_ge(S["exp_s"], l * N_SCORE + score_no("C", m, 2) + 1)
                                chain(V.tensor_reduce(s2[1], psc, AX_X, ALU.add))
                                chain(V.reciprocal(rin[:, m % 4, :], s2[1]))
                                for g in range(C_GROUPS):
                                    for tt in range(TT):
                                        last = V.tensor_scalar(prob[:, g, tt, :], prob[:, g, tt, :],
                                                               rin[:, m % 4, tt:tt + 1], None, ALU.mult)
                                    last.then_inc(S["prob_v"], 1)
                    elif kind == "turn":
                        for part in range(C_GROUPS if br == "C" else 1):
                            no = turn_no(br, n, part)
                            o = {"A": bank[4 + n % 2], "B": bank[5], "C": bank[5 + part % 2]}[br]
                            s = part if br == "C" else n % 4
                            dve.wait_ge(S["turn_pe"], l * N_TURN + no + 1)
                            if br == "A" and n >= 4:
                                dve.wait_ge(S["pv_pe"], l * 12 + (n - 4) // 2 + 1)
                            elif br == "B":
                                dve.wait_ge(S["pv_pe"], l * 12 + 4)
                            elif br == "C":
                                dve.wait_ge(S["pv_pe"], l * 12 + 8 + n)
                            V.tensor_copy(probT[:, s, :, :].rearrange("p k t -> p (k t)"), o[:, :]).then_inc(S["turn_v"], 1)
                    elif kind == "inv":
                        for m in (2 * n, 2 * n + 1):
                            dve.wait_ge(S["std_b"], l * 2 + n + 1)
                            V.reciprocal(root[:, m, :], root[:, m, :]).then_inc(S["inv_v"], 1)
                    elif kind == "branch":
                        dve.wait_ge(S["branch_pe"], l * 12 + n + 1)
                        if n == 0:
                            dve.wait_ge(S["yb_p"], l * B_HEADS + 4)
                        dve.wait_ge(S["unit_s"], l * N_UNITS + GATE0 + n + 1)
                        dst = xh[:, 512 * n:512 * n + 512] if br == "A" else pre[:, n % 2, :]
                        V.scalar_tensor_tensor(dst, pre[:, n % 2, :], 1.0, bank[0][:, :], ALU.add,
                                               ALU.mult).then_inc(S["mix_v"], 1)
                        if br == "C":
                            dve.wait_ge(S["mix_p"], l * 4 + n - 7)
                            dve.wait_ge(S["mix_v"], l * 12 + n + 1)
                            m = xh[:, 512 * (n - 8):512 * (n - 8) + 512]
                            V.tensor_tensor(m, m, dst, ALU.add).then_inc(S["sum_v"], 1)
                            if n == 11:
                                dve.wait_ge(S["sum_v"], l * 4 + 4)
                    elif kind == "out":
                        if n < 2:
                            split_lo(N_UNITS + n + 2, l)
                        dve.wait_ge(S["out_pe"], l * 4 + n + 1)
                        hs = h3[:, :, 256 * n:256 * n + 256]
                        V.scalar_tensor_tensor(hs, bank[n % 2][:, :].rearrange("p (t d) -> p t d", t=TT), 0.5, hs,
                                               ALU.mult, ALU.add).then_inc(S["h_v"], 1)

                dve.wait_ge(S["sq2"], l * 4 + 4)
                V.tensor_reduce(ss, ss4, AX_X, ALU.add).then_inc(S["ss_v"], 1)
                dve.wait_ge(S["std_s"], l * 2 + 2)
                V.reciprocal(rstd, std).then_inc(S["rstd_v"], 1)
                dve.wait_ge(S["rstd_v"], l + 1)
                dve.wait_ge(S["logit_pe"], l + 1)
                for tt in range(TT):
                    last = V.scalar_tensor_tensor(lg[:, tt, :], bank[6 + tt][:, 0:20], rstd[:, tt:tt + 1], rb,
                                                  ALU.mult, ALU.add)
                chain(last)
                col = lambda a, n: bc(a.unsqueeze(2), [P, TT, n])
                lg4, lg16 = lg[:, :, 0:4], lg[:, :, 4:20]
                chain(V.tensor_reduce(s2[4], lg4, AX_X, ALU.max))
                V.tensor_tensor(g4a, lg4, col(s2[4], 4), ALU.subtract).then_inc(S["rd_v"], 1)
                for tt in range(TT):
                    last = V.scalar_tensor_tensor(goh[:, tt, :], lg4[:, tt, :], s2[4][:, tt:tt + 1],
                                                  cf[:, C_W16:C_W16 + 4], ALU.is_equal, ALU.mult)
                chain(last)
                chain(V.tensor_reduce(s2[5], goh, AX_X, ALU.max))
                chain(V.tensor_tensor(goh, goh, col(s2[5], 4), ALU.is_equal))
                chain(V.tensor_scalar(goh, goh, -NEG, NEG, ALU.mult, ALU.add))
                chain(V.tensor_tensor(e16[0].rearrange("p t (g e) -> p t g e", g=N_GRP),
                                      lg16.rearrange("p t (g e) -> p t g e", g=N_GRP),
                                      goh.unsqueeze(3).broadcast_to([P, TT, N_GRP, PER_GRP]), ALU.add))

                def first_max(dst, value, src):
                    chain(V.tensor_reduce(value, src, AX_X, ALU.max))
                    for tt in range(TT):
                        last = V.scalar_tensor_tensor(dst[:, tt, :], src[:, tt, :], value[:, tt:tt + 1],
                                                      cf[:, C_W16:C_W16 + 16], ALU.is_equal, ALU.mult)
                    chain(last)
                    chain(V.tensor_reduce(s2[5], dst, AX_X, ALU.max))
                    chain(V.tensor_tensor(dst, dst, col(s2[5], 16), ALU.is_equal))

                first_max(e16[1], s2[6], e16[0])
                chain(V.scalar_tensor_tensor(e16[0], e16[1], NEG, e16[0], ALU.mult, ALU.add))
                first_max(e16[2], s2[7], e16[0])
                V.tensor_tensor(asg, e16[1], e16[2], ALU.add).then_inc(S["asg_v"], 1)
                g = dve.snap(units) + l
                dve.wait_ge(S["asg_v"], l + 1)
                V.tensor_tensor(s2[2], s2[7], s2[6], ALU.subtract).then_inc(S["rd_v"], 1)
                chain(V.tensor_scalar(e16[4], asg, -FAR, FAR, ALU.mult, ALU.add))
                dve.wait_ge(S["rank_pe"], l + 1)
                chain(V.tensor_tensor(pos, bank[5][:, 0:32].rearrange("p (t e) -> p t e", t=TT), e16[4], ALU.add))
                V.tensor_copy(cnt, bank[5][:, 32:48]).then_inc(S["pos_v"], 1)
                dve.wait_ge(S["pos_v"], l + 1)

                iota = cf[:, C_IOTA:C_IOTA + P]
                iota64 = cf[:, C_IOTA:C_IOTA + CAP]

                def one(a, tt, e):
                    return a[:, tt, e:e + 1] if isinstance(e, int) else a[:, tt, bass.ds(e, 1)]

                def select(e0):
                    for i in range(2):
                        for tt in range(TT):
                            last = V.tensor_scalar(sel[:, tt, i * CAP:i * CAP + CAP], iota64,
                                                   one(pos, tt, e0 + i), None, ALU.is_equal)
                    last.then_inc(S["m_sel_v"], 1)

                def select_gated(e0):
                    for i in range(2):
                        for tt in range(TT):
                            last = V.tensor_scalar(selg[:, tt, i * CAP:i * CAP + CAP], iota64,
                                                   one(pos, tt, e0 + i), one(gat, tt, e0 + i),
                                                   ALU.is_equal, ALU.mult)
                    last.then_inc(S["m_selg_v"], 1)

                def select_extra(j):
                    for tt in range(TT):
                        last = V.tensor_scalar(sel[:, tt, :], iota, one(pos_o, tt, j), None, ALU.is_equal)
                    last.then_inc(S["m_sel_v"], 1)

                def select_extra_gated(j):
                    for tt in range(TT):
                        last = V.tensor_scalar(selg[:, tt, :], iota, one(pos_o, tt, j), one(gat_o, tt, j),
                                               ALU.is_equal, ALU.mult)
                    last.then_inc(S["m_selg_v"], 1)

                def rows_out(g):
                    for b in range(2):
                        dve.wait_ge(S["m_xt"], g * 2 + b + 1)
                        V.tensor_tensor(xgT[:, 4 * b:4 * b + 4, :], bank[b][:, :].rearrange("p (c s) -> p c s", c=4),
                                        bc(gain2[:, 4 * b:4 * b + 4].unsqueeze(2), [P, 4, P]),
                                        ALU.mult).then_inc(S["m_xgT_v"], 1)

                def hidden(r):
                    dve.wait_ge(S["m_sig_s"], r + 1)
                    chain(V.tensor_tensor(sig, bank[4][:, :], sig, ALU.mult))
                    dve.wait_ge(S["m_h"], r * 2 + 2)
                    V.tensor_tensor(hid, bank[5][:, :], sig, ALU.mult).then_inc(S["m_hid_v"], 1)

                def y_out(r):
                    dve.wait_ge(S["m_y"], r * 2 + 2)
                    V.tensor_copy(y_e[:, 512:1024], bank[7][:, :]).then_inc(S["m_y_v"], 1)

                def add(r):
                    for dh in range(2):
                        for tt in range(TT):
                            dve.wait_ge(S["m_sc"], r * 4 + dh * 2 + tt + 1)
                            hs = h3[:, tt, dh * 512:dh * 512 + 512]
                            V.tensor_tensor(hs, bank[2 + tt][:, :], hs, ALU.add).then_inc(S["m_add_v"], 1)

                def unit(r, extra, n):
                    dve.wait_ge(S["m_xt"], r * 2 + l * 2 + 2)
                    (select_extra if extra else select)(n)
                    hidden(r)
                    rows_out(r + l + 1)
                    y_out(r)
                    dve.wait_ge(S["m_st"], r + 1)
                    (select_extra_gated if extra else select_gated)(n)
                    add(r)
                    chained()

                select(0)
                dve.wait_ge(S["rexp_s"], l * 2 + 1)
                chain(V.tensor_reduce(s2[8], g4b, AX_X, ALU.add))
                chain(V.reciprocal(s2[8], s2[8]))
                dve.wait_ge(S["rexp_s"], l * 2 + 2)
                chain(V.tensor_scalar(s2[9], s2[3], 1.0, None, ALU.add))
                chain(V.reciprocal(s2[9], s2[9]))
                chain(V.tensor_tensor(s2[9], s2[9], s2[8], ALU.mult))
                chain(V.tensor_tensor(s2[3], s2[3], s2[9], ALU.mult))
                chain(V.tensor_tensor(gat, e16[1], col(s2[9], 16), ALU.mult))
                chain(V.tensor_tensor(e16[3], e16[2], col(s2[3], 16), ALU.mult))
                chain(V.tensor_tensor(gat, gat, e16[3], ALU.add))
                select_gated(0)
                rows_out(g)
                thr = cf[:, C_THR:C_THR + 32]
                by2 = lambda a: a.rearrange("p (e c) -> p e c", c=2)
                chain(V.tensor_tensor(by2(exist), bc(cnt.unsqueeze(2), [P, 16, 2]), by2(thr), ALU.is_gt))
                chain(V.tensor_tensor_scan(cum, exist, zero32, 0.0, ALU.add, ALU.add))
                row = lambda a: bc(a.unsqueeze(1), [P, N_OVER, 32])
                jrow = cf[:, C_JROW:C_JROW + N_OVER]
                chain(V.tensor_tensor(over_a, row(cum), bc(jrow.unsqueeze(2), [P, N_OVER, 32]), ALU.is_equal))
                chain(V.tensor_tensor(over_a, over_a, row(exist), ALU.mult))
                for src, dst in ((pos, pos_o), (gat, gat_o)):
                    for tt in range(TT):
                        wide = src[:, tt, :].unsqueeze(1).unsqueeze(3).broadcast_to([P, N_OVER, 16, 2])
                        by4 = lambda a: a.rearrange("p j (e c) -> p j e c", c=2)
                        chain(V.tensor_tensor(by4(over_b), by4(over_a), wide, ALU.mult))
                        chain(V.tensor_reduce(dst[:, tt, :], over_b, AX_X, ALU.add))
                chain(V.tensor_tensor(over_b, over_a, row(thr), ALU.mult))
                chain(V.tensor_reduce(eid_o, over_b, AX_X, ALU.add))
                for tt in range(TT):
                    chain(V.tensor_tensor(pos_o[:, tt, :], pos_o[:, tt, :], eid_o, ALU.subtract))
                chain(V.tensor_tensor(over_b, over_a, row(cf[:, C_EIDX:C_EIDX + 32]), ALU.mult))
                chain(V.tensor_reduce(eid_o, over_b, AX_X, ALU.add))
                chain(V.tensor_copy(nexp[:, 1:1 + N_OVER], eid_o))
                V.tensor_copy(nexp[:, 0:1], cum[:, 31:32]).then_inc(S["over_v"], 1)
                chained()

                for p in range(2):
                    begin()
                    unit(dve.snap(units), False, p * 2 + 2)
                    dve.reg_add(units, units, 1)
                V.memset(zone_q1[:, :], 0.0).then_inc(S["zero_q1"], 1)
                V.memset(zone_q2[:, :], 0.0).then_inc(S["zero_q2"], 1)
                with dve.Fori(2, PAIRS - 1) as p:
                    begin()
                    unit(dve.snap(units), False, p * 2 + 2)
                    dve.reg_add(units, units, 1)
                begin()
                dve.wait_ge(S["over_v"], l + 1)
                dve.sem_inc(S["list_seen"], 1)
                unit(dve.snap(units), True, 0)
                dve.reg_add(units, units, 1)
                n_over = dve.value_load(nexp[0:1, 0:1], min_val=0, max_val=N_OVER - 1)
                with dve.If(n_over > 0):
                    with dve.Fori(0, n_over) as j:
                        begin()
                        unit(dve.snap(units), True, j + 1)
                        dve.reg_add(units, units, 1)

            begin()
            dve.wait_ge(S["fin_in"], 16)
            dve.wait_ge(S["std_s"], DEPTH * 2 + 1)
            chain(V.reciprocal(rstd, std))
            for tt in range(TT):
                V.scalar_tensor_tensor(xh3[:, tt, :], h3[:, tt, :], rstd[:, tt:tt + 1], fin[:, :], ALU.mult,
                                       ALU.mult).then_inc(S["final_v"], 1)


_INS = ["x", "w_in", "na_rpb", "lam_q1", "lam_k1", "lam_q2", "lam_k2", "diff_subln", "w_pa", "w_pb", "w_pc", "w_o",
        "norm_mix", "norm_ffn", "router_group_w", "router_group_b", "router_expert_w", "router_expert_b",
        "w1", "w3", "w2", "norm_final"]


def kernel(**inputs):
    import concourse.bacc as bacc
    from concourse.bass_utils import run_bass_kernel_spmd

    nc = bacc.Bacc("TRN2", target_bir_lowering=False, num_devices=1)
    arrays = {f"in_{n}": np.ascontiguousarray(inputs[n]) for n in _INS}
    arrays["in_consts"] = constants()
    args = [nc.dram_tensor(n, a.shape, mybir.dt.from_np(a.dtype), kind="ExternalInput").ap() for n, a in arrays.items()]
    out = nc.dram_tensor("out", (1, T, D), F32, kind="ExternalOutput").ap()
    build(nc, *args, out)
    return run_bass_kernel_spmd(nc, [arrays], core_ids=[0]).results[0]["out"]
```
